# Optimizing a Trainium2 kernel written in Bass

```python
import jax
import jax.numpy as jnp
from jax import lax
import numpy as np
import math
import jax, jax.numpy as jnp

D_MODEL = 1024
BATCH = 1
SEQ = 1024
DEPTH = 1

HEAD_DIM = 64
N_HEADS = 4
BRANCH_W = N_HEADS * HEAD_DIM
N_BRANCH = 4
Q_BLOCK = 128
CMP_BLOCK = 32
SEL_BLOCK = 64
SEL_TOPK = 16
NSA_WINDOW = 512
SWA_WINDOW = 128
SWA_KV_HEADS = 2
RET_CHUNK = 128
RMS_EPS = 1e-6
LN_EPS = 1e-5
NEG_INF = -1e30
TINY = 1e-30
FORCED_SCORE = 1e4

IN_WIDTHS = (
    BRANCH_W, 6 * HEAD_DIM, 3 * N_HEADS, BRANCH_W,
    BRANCH_W, SWA_KV_HEADS * HEAD_DIM, SWA_KV_HEADS * HEAD_DIM, BRANCH_W,
    BRANCH_W, BRANCH_W, BRANCH_W, BRANCH_W,
    BRANCH_W, BRANCH_W, BRANCH_W, BRANCH_W,
)
IN_W = sum(IN_WIDTHS)
IN_OFFSETS = tuple(int(v) for v in np.cumsum(IN_WIDTHS)[:-1])


def alibi_slopes(n):
    return jnp.asarray(2.0 ** (-8.0 * (np.arange(n) + 1) / n), dtype=jnp.float32)

def rms_norm(x, g):
    xf = x.astype(jnp.float32)
    y = xf * lax.rsqrt(jnp.mean(xf * xf, axis=-1, keepdims=True) + RMS_EPS)
    return (y * g.astype(jnp.float32)).astype(x.dtype)

def masked_softmax(s, mask, sink=None):
    s = jnp.where(mask, s, NEG_INF)
    m = jnp.max(s, axis=-1, keepdims=True)
    if sink is not None:
        m = jnp.maximum(m, sink)
    e = jnp.where(mask, jnp.exp(s - m), 0.0)
    den = jnp.sum(e, axis=-1, keepdims=True)
    if sink is not None:
        den = den + jnp.exp(sink - m)
    return e / jnp.maximum(den, TINY)

def band_windows(k, n_prev):
    B, S = k.shape[:2]
    nblk = S // Q_BLOCK
    pad = [(0, 0), (n_prev * Q_BLOCK, 0)] + [(0, 0)] * (k.ndim - 2)
    kp = jnp.pad(k, pad).reshape(B, nblk + n_prev, Q_BLOCK, *k.shape[2:])
    return jnp.concatenate([kp[:, j:j + nblk] for j in range(n_prev + 1)], axis=2)

def banded_attention(q, k, v, window, slopes, sink=None):
    B, S, H, Dh = q.shape
    Hkv = k.shape[2]
    G = H // Hkv
    nblk = S // Q_BLOCK
    n_prev = -(-(window - 1) // Q_BLOCK)
    K = (n_prev + 1) * Q_BLOCK
    kw = band_windows(k, n_prev)
    vw = band_windows(v, n_prev)
    qb = q.reshape(B, nblk, Q_BLOCK, Hkv, G, Dh)
    s = jnp.einsum("bnqhgd,bnkhd->bnhgqk", qb, kw).astype(jnp.float32) * Dh ** -0.5
    rel = jnp.arange(Q_BLOCK)[:, None] + n_prev * Q_BLOCK - jnp.arange(K)[None, :]
    kpos = jnp.arange(nblk)[:, None] * Q_BLOCK - n_prev * Q_BLOCK + jnp.arange(K)[None, :]
    mask = ((rel >= 0) & (rel < window))[None] & (kpos >= 0)[:, None, :]
    s = s - slopes.reshape(Hkv, G, 1, 1) * rel.astype(jnp.float32)
    sk = None if sink is None else sink.astype(jnp.float32).reshape(1, 1, Hkv, G, 1, 1)
    p = masked_softmax(s, mask[None, :, None, None], sk)
    o = jnp.einsum("bnhgqk,bnkhd->bnqhgd", p.astype(v.dtype), vw)
    return o.reshape(B, S, H, Dh)

def nsa_attention(q, kv, gate_logits, pos_emb, w1, w2):
    B, S, H, Dh = q.shape
    k_cmp, v_cmp, k_sel, v_sel, k_win, v_win = jnp.split(kv, 6, axis=-1)
    slopes = alibi_slopes(H)
    scale = Dh ** -0.5
    t = jnp.arange(S)

    nc = S // CMP_BLOCK
    def compress(z, j):
        zb = z.reshape(B, nc, CMP_BLOCK, Dh) + pos_emb[j]
        return jax.nn.silu(zb.reshape(B, nc, CMP_BLOCK * Dh) @ w1[j]) @ w2[j]
    kc = compress(k_cmp, 0)
    vc = compress(v_cmp, 1)
    blk_end = jnp.arange(nc) * CMP_BLOCK + CMP_BLOCK - 1
    dist = t[:, None] - blk_end[None, :]
    s = jnp.einsum("bshd,bcd->bhsc", q, kc).astype(jnp.float32) * scale
    s = s - slopes[:, None, None] * dist.astype(jnp.float32)
    p_cmp = masked_softmax(s, dist >= 0)
    o_cmp = jnp.einsum("bhsc,bcd->bshd", p_cmp.astype(vc.dtype), vc)

    ns = S // SEL_BLOCK
    ratio = SEL_BLOCK // CMP_BLOCK
    imp = p_cmp.sum(axis=1).reshape(B, S, ns, ratio).sum(axis=-1)
    blk = jnp.arange(ns)[None, :]
    cur = (t // SEL_BLOCK)[:, None]
    future = blk * SEL_BLOCK > t[:, None]
    forced = (blk == 0) | (blk == cur) | (blk == cur - 1)
    imp = jnp.where(forced, FORCED_SCORE, jnp.where(future, -1.0, imp))
    topk = min(SEL_TOPK, ns)
    _, idx = lax.top_k(imp, topk)

    kb = k_sel.reshape(B, ns, SEL_BLOCK, Dh)
    vb = v_sel.reshape(B, ns, SEL_BLOCK, Dh)
    nq = S // Q_BLOCK
    qs = q.reshape(B, nq, Q_BLOCK, H, Dh).swapaxes(0, 1)
    ids = idx.reshape(B, nq, Q_BLOCK, topk).swapaxes(0, 1)
    qpos = t.reshape(nq, Q_BLOCK)
    bidx = jnp.arange(B)[:, None, None]
    n_keys = topk * SEL_BLOCK

    def sel_block(args):
        qi, ii, pi = args
        kg = kb[bidx, ii].reshape(B, Q_BLOCK, n_keys, Dh)
        vg = vb[bidx, ii].reshape(B, Q_BLOCK, n_keys, Dh)
        kpos = (ii[..., None] * SEL_BLOCK + jnp.arange(SEL_BLOCK)).reshape(B, Q_BLOCK, n_keys)
        d = pi[None, :, None] - kpos
        sc = jnp.einsum("bqhd,bqkd->bhqk", qi, kg).astype(jnp.float32) * scale
        sc = sc - slopes[:, None, None] * d[:, None].astype(jnp.float32)
        pr = masked_softmax(sc, (d >= 0)[:, None])
        return jnp.einsum("bhqk,bqkd->bqhd", pr.astype(vg.dtype), vg)

    o_sel = lax.map(sel_block, (qs, ids, qpos)).swapaxes(0, 1).reshape(B, S, H, Dh)

    o_win = banded_attention(q, k_win[:, :, None], v_win[:, :, None], NSA_WINDOW, slopes)

    g = jax.nn.sigmoid(gate_logits.astype(jnp.float32)).reshape(B, S, H, 3).astype(q.dtype)
    return g[..., 0:1] * o_cmp + g[..., 1:2] * o_sel + g[..., 2:3] * o_win

def stick_breaking_attention(q, k, v):
    B, S, H, Dh = q.shape
    nq = S // Q_BLOCK
    qs = q.reshape(B, nq, Q_BLOCK, H, Dh).swapaxes(0, 1)
    qpos = jnp.arange(S).reshape(nq, Q_BLOCK)
    kpos = jnp.arange(S)
    scale = Dh ** -0.5

    def one_block(args):
        qi, pi = args
        z = jnp.einsum("bqhd,bkhd->bhqk", qi, k).astype(jnp.float32) * scale
        mask = kpos[None, :] < pi[:, None]
        log_beta = jax.nn.log_sigmoid(z)
        log_1m = jnp.where(mask, jax.nn.log_sigmoid(-z), 0.0)
        suffix = lax.cumsum(log_1m, axis=3, reverse=True) - log_1m
        a = jnp.where(mask, jnp.exp(log_beta + suffix), 0.0)
        return jnp.einsum("bhqk,bkhd->bqhd", a.astype(v.dtype), v)

    return lax.map(one_block, (qs, qpos)).swapaxes(0, 1).reshape(B, S, H, Dh)

def retention(q, k, v):
    B, S, H, Dh = q.shape
    C = RET_CHUNK
    n = S // C
    log_g = jnp.log(1.0 - jnp.asarray(2.0 ** (-5.0 - np.arange(H)), dtype=jnp.float32))
    qc = (q.astype(jnp.float32) * Dh ** -0.5).reshape(B, n, C, H, Dh)
    kc = k.astype(jnp.float32).reshape(B, n, C, H, Dh)
    vc = v.astype(jnp.float32).reshape(B, n, C, H, Dh)
    i = jnp.arange(C)
    diff = (i[:, None] - i[None, :]).astype(jnp.float32)
    dmat = jnp.where(diff >= 0, jnp.exp(log_g[:, None, None] * jnp.maximum(diff, 0.0)), 0.0)
    s = jnp.einsum("bnihd,bnjhd->bnhij", qc, kc) * dmat
    intra = jnp.einsum("bnhij,bnjhd->bnihd", s, vc)
    zeta = jnp.exp(log_g[:, None] * (C - 1 - i)[None, :].astype(jnp.float32))
    u = jnp.einsum("bnjhd,bnjhe,hj->nbhde", kc, vc, zeta)
    g_chunk = jnp.exp(log_g * C)[None, :, None, None]

    def step(r, u_n):
        return r * g_chunk + u_n, r

    _, r_prev = lax.scan(step, jnp.zeros((B, H, Dh, Dh), jnp.float32), u)
    xi = jnp.exp(log_g[:, None] * (i + 1)[None, :].astype(jnp.float32))
    cross = jnp.einsum("bnihd,nbhde,hi->bnihe", qc, r_prev, xi)
    o = (intra + cross).reshape(B, S, H, Dh)
    mu = jnp.mean(o, axis=-1, keepdims=True)
    var = jnp.mean((o - mu) ** 2, axis=-1, keepdims=True)
    return ((o - mu) * lax.rsqrt(var + LN_EPS)).astype(q.dtype)

def hybrid_layer(x, c, w_ada, b_ada, norm_g, w_in, cmp_pos, cmp_w1, cmp_w2, sink, w_merge, w_br, w_out):
    B, S, _ = x.shape
    mod = (jax.nn.silu(c) @ w_ada + b_ada)[:, None, :]
    shift, scale, gate = jnp.split(mod, 3, axis=-1)
    h = rms_norm(x, norm_g) * (1.0 + scale) + shift
    (a_q, a_kv, a_g, a_z, b_q, b_k, b_v, b_z,
     c_q, c_k, c_v, c_z, d_q, d_k, d_v, d_z) = jnp.split(h @ w_in, IN_OFFSETS, axis=-1)

    def heads(z):
        return z.reshape(B, S, -1, HEAD_DIM)

    y_a = nsa_attention(heads(a_q), a_kv, a_g, cmp_pos, cmp_w1, cmp_w2)
    y_b = banded_attention(heads(b_q), heads(b_k), heads(b_v), SWA_WINDOW, alibi_slopes(N_HEADS), sink)
    y_c = stick_breaking_attention(heads(c_q), heads(c_k), heads(c_v))
    y_d = retention(heads(d_q), heads(d_k), heads(d_v))

    branches = ((y_a, a_z), (y_b, b_z), (y_c, c_z), (y_d, d_z))
    merged = None
    for i, (y, z) in enumerate(branches):
        yi = y.reshape(B, S, BRANCH_W) * jax.nn.silu(z)
        term = jax.nn.sigmoid(h @ w_merge[i]) * (yi @ w_br[i])
        merged = term if merged is None else merged + term
    return x + gate * (merged @ w_out)

def first_inputs(seed: int = 0) -> dict:
    key = jax.random.key(seed)
    ks = jax.random.split(key, 14)
    D = D_MODEL
    f32 = jnp.float32

    def nrm(k, shape, fan):
        return jax.random.normal(k, shape, f32) * fan ** -0.5

    return {
        "x": jax.random.normal(ks[0], (BATCH, SEQ, D), f32),
        "c": jax.random.normal(ks[1], (BATCH, D), f32),
        "w_ada": nrm(ks[2], (DEPTH, D, 3 * D), D) * 0.5,
        "b_ada": 0.02 * jax.random.normal(ks[3], (DEPTH, 3 * D), f32),
        "norm_g": 1.0 + 0.05 * jax.random.normal(ks[4], (DEPTH, D), f32),
        "w_in": nrm(ks[5], (DEPTH, D, IN_W), D),
        "cmp_pos": 0.1 * jax.random.normal(ks[6], (DEPTH, 2, CMP_BLOCK, HEAD_DIM), f32),
        "cmp_w1": nrm(ks[7], (DEPTH, 2, CMP_BLOCK * HEAD_DIM, HEAD_DIM), CMP_BLOCK * HEAD_DIM),
        "cmp_w2": nrm(ks[8], (DEPTH, 2, HEAD_DIM, HEAD_DIM), HEAD_DIM),
        "sink": 0.5 * jax.random.normal(ks[9], (DEPTH, N_HEADS), f32),
        "w_merge": nrm(ks[10], (DEPTH, N_BRANCH, D, D), D),
        "w_br": nrm(ks[11], (DEPTH, N_BRANCH, BRANCH_W, D), BRANCH_W),
        "w_out": nrm(ks[12], (DEPTH, D, D), D),
        "final_g": 1.0 + 0.05 * jax.random.normal(ks[13], (D,), f32),
    }

def first_block(x, c, w_ada, b_ada, norm_g, w_in, cmp_pos, cmp_w1, cmp_w2, sink, w_merge, w_br, w_out, final_g):
    for l in range(DEPTH):
        x = hybrid_layer(x, c, w_ada[l], b_ada[l], norm_g[l], w_in[l], cmp_pos[l], cmp_w1[l], cmp_w2[l],
                         sink[l], w_merge[l], w_br[l], w_out[l])
    return rms_norm(x, final_g)


DEPTH_2 = 2

N_EVEN = (DEPTH_2 + 1) // 2
N_ODD = DEPTH_2 // 2

W_A = D_MODEL
CONV_K = 31
A_GROUPS = 8
H_B = 4
DQK_B = D_MODEL // (2 * H_B)
DV_B = D_MODEL // H_B
W_B = H_B * DV_B
CHUNK = 64
H_C = 8
QK_NOPE = 128
QK_ROPE = 64
V_HEAD = 128
Q_LORA = 3 * D_MODEL // 8
KV_LORA = D_MODEL // 4
W_C = H_C * V_HEAD
ROPE_THETA = 10000.0
D_GROUPS = 4
D_GROUP_CH = D_MODEL // 8
W_D = D_GROUPS * D_GROUP_CH

EVEN_SIZES = (W_A, W_A, W_A, H_B * DQK_B, H_B * DQK_B, W_B, W_B, W_B, 4 * H_B)
ODD_SIZES = (Q_LORA, KV_LORA, QK_ROPE, W_D, W_C, W_D)
P_EVEN = sum(EVEN_SIZES)
P_ODD = sum(ODD_SIZES)


def split_cols(p, sizes):
    idx = [int(i) for i in np.cumsum(sizes)[:-1]]
    return jnp.split(p, idx, axis=-1)

def rms_norm_2(x, g):
    xf = x.astype(jnp.float32)
    y = xf * lax.rsqrt(jnp.mean(xf * xf, axis=-1, keepdims=True) + RMS_EPS)
    return (y * g.astype(jnp.float32)).astype(x.dtype)

def group_layer_norm(x, g, b, groups):
    B, S, C = x.shape
    xf = x.astype(jnp.float32).reshape(B, S, groups, C // groups)
    mu = jnp.mean(xf, axis=-1, keepdims=True)
    xc = xf - mu
    var = jnp.mean(xc * xc, axis=-1, keepdims=True)
    y = (xc * lax.rsqrt(var + LN_EPS)).reshape(B, S, C)
    return (y * g.astype(jnp.float32) + b.astype(jnp.float32)).astype(x.dtype)

def depthwise_conv_centred(x, w, b):
    K = w.shape[0]
    y = lax.conv_general_dilated(
        x, w[:, None, :].astype(x.dtype), window_strides=(1,),
        padding=[(K // 2, K // 2)], dimension_numbers=("NWC", "WIO", "NWC"),
        feature_group_count=x.shape[-1])
    return y + b.astype(x.dtype)

def rope_tables(positions):
    inv = ROPE_THETA ** (-jnp.arange(0, QK_ROPE, 2, dtype=jnp.float32) / QK_ROPE)
    ang = positions.astype(jnp.float32)[..., None] * inv
    return jnp.cos(ang), jnp.sin(ang)

def apply_rope(x, cos, sin):
    half = x.shape[-1] // 2
    xf = x.astype(jnp.float32)
    x1, x2 = xf[..., :half], xf[..., half:]
    return jnp.concatenate([x1 * cos - x2 * sin, x1 * sin + x2 * cos], axis=-1).astype(x.dtype)

def mlstm_chunkwise(q, k, v, i_pre, f_pre):
    B, H, S, dk = q.shape
    dv = v.shape[-1]
    nc = S // CHUNK
    f32 = jnp.float32

    def chunks(a):
        return jnp.moveaxis(a.reshape(B, H, nc, CHUNK, *a.shape[3:]), 2, 0)

    qc = chunks(q.astype(f32))
    kc = chunks(k.astype(f32) * (dk ** -0.5))
    vc = chunks(v.astype(f32))
    ic = chunks(i_pre.astype(f32))
    bc = jnp.cumsum(chunks(jax.nn.log_sigmoid(f_pre.astype(f32))), axis=-1)
    tril = jnp.tril(jnp.ones((CHUNK, CHUNK), dtype=bool))

    def step(carry, inp):
        C, n, m = carry
        qb, kb, vb, ib, bb = inp
        D = jnp.where(tril, bb[..., :, None] - bb[..., None, :] + ib[..., None, :], -jnp.inf)
        a = bb + m[..., None]
        m_t = jnp.maximum(a, jnp.max(D, axis=-1))
        Dw = jnp.exp(D - m_t[..., None])
        aw = jnp.exp(a - m_t)
        s = jnp.einsum('bhtd,bhsd->bhts', qb, kb) * Dw
        num = jnp.einsum('bhts,bhsv->bhtv', s, vb) + aw[..., None] * jnp.einsum('bhtd,bhdv->bhtv', qb, C)
        den = jnp.sum(s, axis=-1) + aw * jnp.einsum('bhtd,bhd->bht', qb, n)
        h = num / jnp.maximum(jnp.abs(den), jnp.exp(-m_t))[..., None]
        bL = bb[..., -1]
        g = bL[..., None] - bb + ib
        m_new = jnp.maximum(bL + m, jnp.max(g, axis=-1))
        wk = jnp.exp(g - m_new[..., None])
        decay = jnp.exp(bL + m - m_new)
        C_new = decay[..., None, None] * C + jnp.einsum('bhs,bhsd,bhsv->bhdv', wk, kb, vb)
        n_new = decay[..., None] * n + jnp.einsum('bhs,bhsd->bhd', wk, kb)
        return (C_new, n_new, m_new), h

    init = (jnp.zeros((B, H, dk, dv), f32), jnp.zeros((B, H, dk), f32), jnp.zeros((B, H), f32))
    _, hs = lax.scan(step, init, (qc, kc, vc, ic, bc))
    return jnp.moveaxis(hs, 0, 2).reshape(B, H, S, dv)

def even_layer(x, g_pre, g_post, w_in, b_gate, conv_w, conv_b, gn_g, gn_b, hn_g, w_out):
    B, S, _ = x.shape
    h = rms_norm_2(x, g_pre)
    p = h @ w_in
    a_val, a_gate, z_a, q, k, v, o, z_b, gates = split_cols(p, EVEN_SIZES)
    u = a_val * jax.nn.sigmoid(a_gate)
    u = depthwise_conv_centred(u, conv_w, conv_b)
    u = jax.nn.silu(group_layer_norm(u, gn_g, gn_b, A_GROUPS))
    y_a = u * jax.nn.silu(z_a)
    to_heads = lambda t, d: t.reshape(B, S, H_B, d).transpose(0, 2, 1, 3)
    qh, kh, vh = to_heads(q, DQK_B), to_heads(k, DQK_B), to_heads(v, DV_B)
    gt = (gates.astype(jnp.float32) + b_gate.astype(jnp.float32)).reshape(B, S, 4, H_B).transpose(2, 0, 3, 1)
    i_f, f_f, i_b, f_b = gt[0], gt[1], gt[2], gt[3]
    h_fwd = mlstm_chunkwise(qh, kh, vh, i_f, f_f)
    fl = lambda t: jnp.flip(t, axis=2)
    h_bwd = fl(mlstm_chunkwise(fl(qh), fl(kh), fl(vh), fl(i_b), fl(f_b)))
    hm = (h_fwd + h_bwd).transpose(0, 2, 1, 3)
    hm = rms_norm_2(hm, hn_g.reshape(H_B, DV_B)).astype(x.dtype)
    hm = jax.nn.sigmoid(o.reshape(B, S, H_B, DV_B)) * hm
    y_b = hm.reshape(B, S, W_B) * jax.nn.silu(z_b)
    y = jnp.concatenate([y_a, y_b], axis=-1) @ w_out
    return x + rms_norm_2(y, g_post)

def odd_layer(x, cos, sin, g_pre, g_post, w_in, g_q, w_uq, g_kv, w_ukv, w_fd, w_out):
    B, S, _ = x.shape
    h = rms_norm_2(x, g_pre)
    p = h @ w_in
    c_q, c_kv, k_r, f_in, z_c, z_d = split_cols(p, ODD_SIZES)
    qh = (rms_norm_2(c_q, g_q) @ w_uq).reshape(B, S, H_C, QK_NOPE + QK_ROPE)
    q_nope = qh[..., :QK_NOPE]
    q_rope = apply_rope(qh[..., QK_NOPE:], cos[:, :, None, :], sin[:, :, None, :])
    kv = (rms_norm_2(c_kv, g_kv) @ w_ukv).reshape(B, S, H_C, QK_NOPE + V_HEAD)
    k_nope, v = kv[..., :QK_NOPE], kv[..., QK_NOPE:]
    k_rope = apply_rope(k_r, cos, sin)
    scale = (QK_NOPE + QK_ROPE) ** -0.5
    nb = S // Q_BLOCK
    blk = lambda t: jnp.moveaxis(t.reshape(B, nb, Q_BLOCK, *t.shape[2:]), 1, 0)

    def attend(qs):
        qn, qr = qs
        s = jnp.einsum('bqhd,bkhd->bhqk', qn, k_nope) + jnp.einsum('bqhr,bkr->bhqk', qr, k_rope)
        pr = jax.nn.softmax(s.astype(jnp.float32) * scale, axis=-1).astype(v.dtype)
        return jnp.einsum('bhqk,bkhd->bqhd', pr, v)

    att = lax.map(attend, (blk(q_nope), blk(q_rope)))
    att = jnp.moveaxis(att, 0, 1).reshape(B, S, W_C)
    y_c = att * jax.nn.silu(z_c)
    fg = f_in.astype(jnp.float32).reshape(B, S, D_GROUPS, D_GROUP_CH)
    fr = jnp.real(jnp.fft.fft2(fg, axes=(1, 3), norm="ortho")).astype(x.dtype).reshape(B, S, W_D)
    y_d = (fr @ w_fd) * jax.nn.silu(z_d)
    y = jnp.concatenate([y_c, y_d], axis=-1) @ w_out
    return x + rms_norm_2(y, g_post)

def second_inputs(seed: int = 0) -> dict:
    key = jax.random.key(seed)
    ks = jax.random.split(key, 24)
    f32 = jnp.float32
    nrm = lambda k, shape, fan_in: jax.random.normal(k, shape, f32) * (fan_in ** -0.5)
    gain = lambda k, shape: 1.0 + 0.05 * jax.random.normal(k, shape, f32)
    small = lambda k, shape: 0.02 * jax.random.normal(k, shape, f32)
    x = jax.random.normal(ks[0], (BATCH, SEQ, D_MODEL), f32)
    positions = (jnp.arange(SEQ, dtype=jnp.int32)[None, :]
                 + jax.random.randint(ks[1], (BATCH, 1), 0, 1024, dtype=jnp.int32))
    fbias = jnp.linspace(3.0, 6.0, H_B, dtype=f32)
    gate_base = jnp.concatenate([jnp.zeros((H_B,), f32), fbias, jnp.zeros((H_B,), f32), fbias])
    even_b_gate = gate_base[None, :] + 0.1 * jax.random.normal(ks[2], (N_EVEN, 4 * H_B), f32)
    return {
        "x": x,
        "positions": positions,
        "even_g_pre": gain(ks[3], (N_EVEN, D_MODEL)),
        "even_g_post": gain(ks[4], (N_EVEN, D_MODEL)),
        "even_w_in": nrm(ks[5], (N_EVEN, D_MODEL, P_EVEN), D_MODEL),
        "even_b_gate": even_b_gate,
        "even_conv_w": nrm(ks[6], (N_EVEN, CONV_K, W_A), CONV_K),
        "even_conv_b": small(ks[7], (N_EVEN, W_A)),
        "even_gn_g": gain(ks[8], (N_EVEN, W_A)),
        "even_gn_b": small(ks[9], (N_EVEN, W_A)),
        "even_hn_g": gain(ks[10], (N_EVEN, W_B)),
        "even_w_out": nrm(ks[11], (N_EVEN, W_A + W_B, D_MODEL), W_A + W_B),
        "odd_g_pre": gain(ks[12], (N_ODD, D_MODEL)),
        "odd_g_post": gain(ks[13], (N_ODD, D_MODEL)),
        "odd_w_in": nrm(ks[14], (N_ODD, D_MODEL, P_ODD), D_MODEL),
        "odd_g_q": gain(ks[15], (N_ODD, Q_LORA)),
        "odd_w_uq": nrm(ks[16], (N_ODD, Q_LORA, H_C * (QK_NOPE + QK_ROPE)), Q_LORA),
        "odd_g_kv": gain(ks[17], (N_ODD, KV_LORA)),
        "odd_w_ukv": nrm(ks[18], (N_ODD, KV_LORA, H_C * (QK_NOPE + V_HEAD)), KV_LORA),
        "odd_w_fd": nrm(ks[19], (N_ODD, W_D, W_D), W_D),
        "odd_w_out": nrm(ks[20], (N_ODD, W_C + W_D, D_MODEL), W_C + W_D),
    }

def second_block(x, positions, even_g_pre, even_g_post, even_w_in, even_b_gate, even_conv_w,
              even_conv_b, even_gn_g, even_gn_b, even_hn_g, even_w_out, odd_g_pre, odd_g_post,
              odd_w_in, odd_g_q, odd_w_uq, odd_g_kv, odd_w_ukv, odd_w_fd, odd_w_out):
    cos, sin = rope_tables(positions)
    h = x
    for layer in range(DEPTH_2):
        j = layer // 2
        if layer % 2 == 0:
            h = even_layer(h, even_g_pre[j], even_g_post[j], even_w_in[j], even_b_gate[j],
                           even_conv_w[j], even_conv_b[j], even_gn_g[j], even_gn_b[j],
                           even_hn_g[j], even_w_out[j])
        else:
            h = odd_layer(h, cos, sin, odd_g_pre[j], odd_g_post[j], odd_w_in[j], odd_g_q[j],
                          odd_w_uq[j], odd_g_kv[j], odd_w_ukv[j], odd_w_fd[j], odd_w_out[j])
    return h


def setup_inputs(seed=0):
    out = dict(first_inputs(seed))
    for name, value in second_inputs(seed + 1).items():
        if name != "x":
            out[name + "_2"] = value
    return out


def reference(
    x, c, w_ada, b_ada, norm_g, w_in, cmp_pos, cmp_w1, cmp_w2, sink, w_merge, w_br, w_out,
    final_g, positions_2, even_g_pre_2, even_g_post_2, even_w_in_2, even_b_gate_2,
    even_conv_w_2, even_conv_b_2, even_gn_g_2, even_gn_b_2, even_hn_g_2, even_w_out_2,
    odd_g_pre_2, odd_g_post_2, odd_w_in_2, odd_g_q_2, odd_w_uq_2, odd_g_kv_2, odd_w_ukv_2,
    odd_w_fd_2, odd_w_out_2,
):
    x = first_block(
        x, c, w_ada, b_ada, norm_g, w_in, cmp_pos, cmp_w1, cmp_w2, sink, w_merge, w_br, w_out,
        final_g,
    )
    return second_block(
        x, positions_2, even_g_pre_2, even_g_post_2, even_w_in_2, even_b_gate_2, even_conv_w_2,
        even_conv_b_2, even_gn_g_2, even_gn_b_2, even_hn_g_2, even_w_out_2, odd_g_pre_2,
        odd_g_post_2, odd_w_in_2, odd_g_q_2, odd_w_uq_2, odd_g_kv_2, odd_w_ukv_2, odd_w_fd_2,
        odd_w_out_2,
    )


_drawn_inputs = setup_inputs


def setup_inputs(seed=0):
    import zlib

    import numpy as np

    out = dict(_drawn_inputs(seed))
    spreads = {}
    factors = {'cmp_pos': 6.573, 'sink': 8.0, 'even_gn_b_2': 4.138, 'odd_g_q_2': 8.0, 'odd_g_kv_2': 6.972}
    for name, (base, spread) in spreads.items():
        noise = np.random.default_rng([zlib.crc32(name.encode()), seed]).standard_normal(out[name].shape)
        drawn = base * np.exp(spread * noise) if base else spread * noise
        out[name] = jnp.asarray(drawn.astype(out[name].dtype))
    for name, factor in factors.items():
        out[name] = (out[name] * factor).astype(out[name].dtype)
    return out
```

```python
from contextlib import ExitStack

import numpy as np
import concourse.bass as bass
from concourse import mybir

P = 128
D = 1024
S = 1024
NT = S // P
HALF = 512
BLK = 8
HD = 64
NEG = -1e30
TINY = 1e-30
RMS_EPS = 1e-6
LN_EPS = 1e-5
SLOPES = [2.0 ** (-8.0 * (h + 1) / 4) for h in range(4)]
CONV_K = 31
H_B = 4
H_C = 8
ROPE = 64

F32 = mybir.dt.float32
F32R = mybir.dt.float32r
I32 = mybir.dt.int32
ALU = mybir.AluOpType
ACT = mybir.ActivationFunctionType
AX = mybir.AxisListType

PROJ = {"A": 8, "B": 6, "C": 8, "D": 8}
STREAM = [("mod", 24)]
for _b in "ABCD":
    STREAM += [("proj" + _b, PROJ[_b]), ("br" + _b, 2), ("merge" + _b, 8)]
STREAM += [("out1", 8), ("gates", 1)]
STREAM += [(f"lstm{h}", 8) for h in range(H_B)]
STREAM += [("out_b", 8), ("conv", 24), ("out_a", 8)]
STREAM += [("zc", 8), ("lat", 6), ("fin", 8), ("mla", 16), ("out_c", 8), ("dft", 16), ("fd", 2), ("out_d", 4)]
CHUNK0, _n = {}, 0
for _name, _c in STREAM:
    CHUNK0[_name] = _n
    _n += _c
N_CHUNKS = _n
N_CHUNKS_PADDED = N_CHUNKS + N_CHUNKS % 2

CONST = ["ident", "ones_d", "ones_c", "ones_h", "ones", "sum_neg", "neg", "mask_lt", "neg_ge",
         "cum_f", "cum_b", "neg_f", "neg_b", "rot", "ones_q", "ones_kv"]
CI = {n: i for i, n in enumerate(CONST)}


def build(nc, io, out):
    ctx = ExitStack()
    with ctx:
        base = (nc.sbuf_base + 63) // 64 * 64
        n_pairs = N_CHUNKS_PADDED // 2

        def sb(name, kb, shape, dt=F32):
            return nc.alloc_sbuf_tensor_at(name, shape, dt, offset=base + int(kb * 1024))

        def sem(name):
            return ctx.enter_context(nc.semaphore(name))

        H_hi = sb("H_hi", 0, [P, NT, S], F32R)
        H_lo = sb("H_lo", 32, [P, NT, S], F32R)
        w_raw = [sb(f"w_raw{s}", 64 + 4 * s, [P, BLK * P]) for s in range(2)]
        w_hi = [sb(f"w_hi{s}", 72 + 4 * s, [P, BLK * P], F32R) for s in range(2)]
        w_lo = [sb(f"w_lo{s}", 80 + 4 * s, [P, BLK * P], F32R) for s in range(2)]
        ACC = sb("ACC", 88, [P, NT, S])
        cols = sb("cols", 120, [P, 120])
        zero = sb("zero", 120.46875, [P, 1])
        ident = sb("ident", 120.5, [P, P])
        ones_d = sb("ones_d", 121, [P, P])
        cols2 = sb("cols2", 121.5, [P, 96])
        V = 122
        Y_hi = sb("Y_hi", V, [P, NT, S], F32R)
        Y_lo = sb("Y_lo", V + 32, [P, NT, S], F32R)
        proj = sb("proj", V, [P, NT, S])
        Ya_hi = sb("Ya_hi", V + 32, [P, 2, S], F32R)
        Ya_lo = sb("Ya_lo", V + 40, [P, 2, S], F32R)
        X = V + 48
        n_sq = sb("n_sq", V, [P, 2, S])
        n_t = sb("n_t", V + 8, [P, 2, S])
        n_rs = sb("n_rs", V + 16, [P, S])
        n_rt = sb("n_rt", V + 20, [P, S])

        ps = [nc.alloc_psum_tensor(f"ps{i}", [P, 2 * HALF], F32) for i in range(4)]

        w_loaded = [sem(f"w_loaded{s}") for s in range(2)]
        w_copied = sem("w_copied")
        w_split = sem("w_split")
        slot_free = sem("slot_free")
        out_ready = sem("out_ready")
        evac_act = sem("evac_act")
        evac_dve = sem("evac_dve")
        phase_end = sem("phase_end")
        zero_set = sem("zero_set")
        aux = sem("aux")
        act_own = sem("act_own")
        dve_own = sem("dve_own")

        block = ctx.enter_context(nc.Block())

        @block.sync
        def _(sp):
            for s in range(2):
                sp.dma_start(w_raw[s][:], io["wstream"][s]).then_inc(w_loaded[s], 16)
            with sp.Fori(1, n_pairs) as i:
                for s in range(2):
                    sp.wait_ge(w_split, 2 * i + s - 1)
                    sp.dma_start(w_raw[s][:], io["wstream"][2 * i + s]).then_inc(w_loaded[s], 16)

        @block.gpsimd
        def _(pool):
            pool.memset(zero[:], 0.0).then_inc(zero_set, 1)
            pool.wait_ge(zero_set, 1)
            with pool.Fori(0, n_pairs) as i:
                for s in range(2):
                    pool.wait_ge(w_loaded[s], 16 * i + 16)
                    pool.wait_ge(slot_free, 2 * i + s + 1)
                    pool.tensor_tensor(w_hi[s][:], w_raw[s][:], zero[:].to_broadcast([P, BLK * P]),
                                       ALU.add).then_inc(w_copied, 1)
                    pool.wait_ge(w_copied, 2 * i + s + 1)
                    pool.tensor_tensor(w_lo[s][:], w_raw[s][:], w_hi[s][:].bitcast(F32),
                                       ALU.subtract).then_inc(w_split, 1)

        class Count:

            def __init__(self, s):
                self.s, self.n, self.var, self.base, self.step = s, 0, None, 0, 0

            def inc(self, ins, by=1):
                ins.then_inc(self.s, by)
                self.n += by
                return self.now()

            def now(self):
                if self.var is None:
                    return self.n
                return self.base + self.step * self.var + (self.n - self.base)

            def enter(self, var, step):
                self.var, self.base, self.step = var, self.n, step

            def leave(self, times):
                assert self.n - self.base == self.step, (self.n - self.base, self.step)
                self.n = self.base + self.step * times
                self.var = None

        own = {}

        def link(eng, which, ins):
            c = own[which]
            eng.wait_ge(c.s, c.inc(ins))

        own["act"] = Count(act_own)
        own["dve"] = Count(dve_own)
        ended = {"pe": 0, "act": 0, "dve": 0}

        def end_phase(eng, which):
            ended[which] += 1
            eng.drain().then_inc(phase_end, 1)
            eng.wait_ge(phase_end, 3 * ended[which])

        def pairs(eng, n, body):
            if n < 4:
                for j in range(n):
                    body(j, j % 2)
                return
            with eng.Fori(0, n // 2) as i:
                for s in range(2):
                    body(2 * i + s, s)
            if n % 2:
                body(n - 1, 0)

        tiles = {"pe": 0, "act": 0, "dve": 0}

        def mm3(pe, out, wh, wl, ah, al, first, last, opens=False):

            mm = pe.matmul(out, wh, ah, start=first, stop=False)
            if opens:
                mm.then_inc(slot_free, 1)
            pe.matmul(out, wh, al, start=False, stop=False)
            return pe.matmul(out, wl, ah, start=False, stop=last)

        def pe_gemm(pe, name, n, kt, hi, lo, k0=0):
            n0, g0, per = CHUNK0[name] if isinstance(name, str) else name, tiles["pe"], BLK // kt

            def chunk(j, par):
                s = (n0 + par) % 2
                pe.wait_ge(w_split, n0 + 1 + j)
                for o in range(per):
                    t = ps[(g0 + per * par + o) % 2]
                    g = g0 + per * j + o
                    pe.wait_ge(evac_act, g + 1)
                    pe.wait_ge(evac_dve, g + 1)
                    for k in range(kt):
                        b = (o * kt + k) * P
                        for h in range(2):
                            mm = mm3(pe, t[:, h * HALF:(h + 1) * HALF], w_hi[s][:, b:b + P], w_lo[s][:, b:b + P],
                                     hi[:, k0 + k, h * HALF:(h + 1) * HALF], lo[:, k0 + k, h * HALF:(h + 1) * HALF],
                                     k == 0, k == kt - 1, opens=o == 0 and k == 0 and h == 0)
                    mm.then_inc(out_ready, 1)
            pairs(pe, n, chunk)
            tiles["pe"] += n * per

        def each_tile(eng, which, n, body):
            g0 = tiles[which]

            def one(j, par):
                eng.wait_ge(out_ready, g0 + 1 + j)
                body(j, ps[(g0 + par) % 2])
            pairs(eng, n, one)
            tiles[which] += n

        def copy_half(eng, which, n, dst):
            def one(j, t):
                if which == "act":
                    eng.activation(dst[:, j, 0:HALF], t[:, 0:HALF], ACT.Copy).then_inc(evac_act, 1)
                else:
                    eng.tensor_copy(dst[:, j, HALF:S], t[:, HALF:S]).then_inc(evac_dve, 1)
            each_tile(eng, which, n, one)

        shared_sems, counts = {}, {}

        def shared(name):
            if name not in shared_sems:
                shared_sems[name] = sem(name)
            return shared_sems[name]

        def since(kind, **adds):
            before = {x: counts.get((kind, x), 0) for x in adds}
            for x, n in adds.items():
                counts[kind, x] = before[x] + n
            return before

        class Norm:

            def __init__(self, name, src, n, ones, gcol, eps=RMS_EPS, shift=None, hi=None, lo=None, into=None,
                         sq=n_sq, t=n_t, rt=n_rt, rs=n_rs):
                self.name, self.src, self.n, self.ones, self.gcol, self.eps, self.shift = (
                    name, src, n, ones, gcol, eps, shift)
                self.hi, self.lo, self.into, self.sq, self.t, self.rt, self.rs = hi, lo, into, sq, t, rt, rs
                self.squared, self.summed, self.rooted, self.scaled, self.hi_done, self.lo_done = (
                    shared(f"norm_{x}") for x in ("squared", "summed", "rooted", "scaled", "hi", "lo"))
                split = n if hi is not None else 0
                self.at = since("norm", squared=n, summed=n, rooted=1, scaled=n, hi_done=split, lo_done=split)

            def pe(self, pe):
                for k in range(self.n):
                    pe.wait_ge(self.squared, self.at['squared'] + k + 1)
                    for h in range(2):
                        mm = pe.matmul(ps[0][:, h * HALF:(h + 1) * HALF], self.ones[:],
                                       self.sq[:, k % 2, h * HALF:(h + 1) * HALF], start=k == 0, stop=k == self.n - 1)
                    mm.then_inc(self.summed, 1)

            def act(self, act):
                for k in range(self.n):
                    if k >= 2:
                        act.wait_ge(self.summed, self.at['summed'] + k - 1)
                    act.activation(self.sq[:, k % 2], self.src[:, k], ACT.Square).then_inc(self.squared, 1)
                act.wait_ge(self.summed, self.at['summed'] + self.n)
                act.activation(self.rt[:], ps[0][:], ACT.Sqrt, bias=eps_col(self.eps)).then_inc(self.rooted, 1)
                if self.hi is None:
                    return
                for k in range(self.n):
                    act.wait_ge(self.scaled, self.at['scaled'] + k + 1)
                    t = self.t[:, k % 2]
                    if self.shift is not None:
                        link(act, "act", act.activation(t, t, ACT.Identity, bias=self.shift[:, k:k + 1]))
                    act.activation(self.hi[:, k], t, ACT.Copy).then_inc(self.hi_done, 1)

            def dve(self, v):
                v.wait_ge(self.rooted, self.at['rooted'] + 1)
                link(v, "dve", v.reciprocal(self.rs[:], self.rt[:]))

                def low(k):
                    v.wait_ge(self.hi_done, self.at['hi_done'] + k + 1)
                    v.tensor_tensor(self.lo[:, k], self.t[:, k % 2], self.hi[:, k].bitcast(F32),
                                    ALU.subtract).then_inc(self.lo_done, 1)
                for k in range(self.n):
                    dst = self.into[:, k] if self.hi is None else self.t[:, k % 2]
                    if self.hi is not None and k >= 2:
                        low(k - 2)
                        v.wait_ge(self.lo_done, self.at['lo_done'] + k - 1)
                    v.scalar_tensor_tensor(out=dst, in0=self.src[:, k], scalar=self.gcol[:, k:k + 1],
                                           in1=self.rs[:], op0=ALU.mult, op1=ALU.mult).then_inc(self.scaled, 1)
                if self.hi is not None:
                    low(self.n - 2)
                    low(self.n - 1)

        class Split:

            def __init__(self, name, src, n, hi, lo):
                self.src, self.n, self.hi, self.lo = src, n, hi, lo
                self.hi_done = shared("split_hi")
                self.at = since("split", hi_done=n)

            def act(self, act):
                for k in range(self.n):
                    act.activation(self.hi[:, k], self.src[:, k], ACT.Copy).then_inc(self.hi_done, 1)

            def dve(self, v):
                for k in range(self.n):
                    v.wait_ge(self.hi_done, self.at['hi_done'] + k + 1)
                    v.tensor_tensor(self.lo[:, k], self.src[:, k], self.hi[:, k].bitcast(F32), ALU.subtract)

        eps_cols = {RMS_EPS: 0, LN_EPS: 1}

        def eps_col(e):
            return cols[:, eps_cols[e]:eps_cols[e] + 1]

        C_NG, C_FG, C_MOD, C_GS, C_EG, C_CT = 4, 12, 20, 44, 52, 60
        aux_n = [0]

        def load(act, dst, src):
            act.dma_start(dst, src).then_inc(aux, 16)
            aux_n[0] += 16

        c_hi = sb("c_hi", V, [P, NT, 2], F32R)
        c_lo = sb("c_lo", V + 0.125, [P, NT, 2], F32R)
        c_sig = sb("c_sig", V + 0.25, [P, NT])
        c_sil = sb("c_sil", V + 0.5, [P, NT])
        b_ada = sb("b_ada", V + 0.75, [P, 24])
        sem_c = sem("sem_c")
        sem_mod = sem("sem_mod")
        eps_set = sem("eps_set")

        def act_mod(act):
            load(act, cols[:, C_NG:C_NG + 8], io["norm_g"])
            load(act, cols[:, C_FG:C_FG + 8], io["final_g"])
            load(act, cols[:, C_EG:C_EG + 8], io["even_g_pre_2"])
            load(act, cols[:, C_CT:C_CT + 8], io["c"])
            load(act, b_ada[:], io["b_ada"])
            load(act, cols2[:], io["gains"])
            load(act, ident[:], io["consts"][CI["ident"]])
            load(act, ones_d[:], io["consts"][CI["ones_d"]])
            for k in range(NT):
                load(act, ACC[:, k], io["x"][k])
            act.wait_ge(aux, aux_n[0])
            act.activation(c_sig[:], cols[:, C_CT:C_CT + 8], ACT.Sigmoid).then_inc(sem_c, 1)

        def dve_mod(v):
            v.memset(cols[:, 0:1], RMS_EPS).then_inc(eps_set, 1)
            v.memset(cols[:, 1:2], LN_EPS).then_inc(eps_set, 1)
            v.wait_ge(sem_c, 1)
            link(v, "dve", v.tensor_tensor(c_sil[:], c_sig[:], cols[:, C_CT:C_CT + 8], ALU.mult))
            for r in range(2):
                link(v, "dve", v.tensor_copy(c_hi[:, :, r], c_sil[:]))
            for r in range(2):
                ins = v.tensor_tensor(c_lo[:, :, r], c_sil[:], c_hi[:, :, r].bitcast(F32), ALU.subtract)
            ins.then_inc(sem_c, 1)
            v.wait_ge(sem_mod, 1)
            link(v, "dve", v.tensor_tensor(cols[:, C_MOD:C_MOD + 24],
                                           ps[2][:, 0:48].rearrange("p (c r) -> p c r", r=2)[:, :, 0], b_ada[:], ALU.add))
            v.scalar_tensor_tensor(out=cols[:, C_GS:C_GS + 8], in0=cols[:, C_MOD + 8:C_MOD + 16], scalar=1.0,
                                   in1=cols[:, C_NG:C_NG + 8], op0=ALU.add, op1=ALU.mult)

        def pe_mod(pe):
            pe.wait_ge(sem_c, 2)

            def chunk(j, s):
                pe.wait_ge(w_split, 1 + j)
                for k in range(NT):
                    mm = mm3(pe, ps[2][:, bass.ds(2 * j, 2)], w_hi[s][:, k * P:(k + 1) * P], w_lo[s][:, k * P:(k + 1) * P],
                             c_hi[:, k, :], c_lo[:, k, :], k == 0, k == NT - 1, opens=k == 0)
            pairs(pe, 24, chunk)
            pe.drain().then_inc(sem_mod, 1)

        norm1 = Norm("norm1", ACC, NT, ones_d, cols[:, C_GS:C_GS + 8], shift=cols[:, C_MOD:C_MOD + 8], hi=H_hi, lo=H_lo)

        class Soft:

            def __init__(self, name, units, T, PT, st, finish=None, groups=0):
                self.units, self.T, self.PT, self.st, self.finish = units, T, PT, st, finish
                self.s_ready, self.max_done, self.exp_done, self.p_done, self.t_ready, self.pt_done, self.o_ready, \
                    self.o_out = (sem(f"{name}_{x}") for x in ("scores", "max", "exp", "p", "turned", "pt", "o", "oout"))
                self.groups = sum(u["last"] for u in units)

            def pe(self, pe, b=0, gb=0):
                U = self.units

                def scores(j):
                    u = U[j]
                    if j >= 2:
                        pe.wait_ge(self.exp_done if u["rel"] is None else self.max_done, b + j - 1)
                    t = ps[j % 2]
                    for h0 in range(0, u["L"], HALF):
                        h1 = min(u["L"], h0 + HALF)
                        n = len(u["qk"])
                        for x, (q, k) in enumerate(u["qk"]):
                            mm = pe.matmul(t[:, h0:h1], q, k[:, h0:h1], start=x == 0, stop=x == n - 1)
                    mm.then_inc(self.s_ready, 1)

                scores(0)
                if len(U) > 1:
                    scores(1)
                g = [0]

                def values(j):
                    u = U[j]
                    pe.wait_ge(self.pt_done, b + j + 1)
                    if u["first"] and g[0] >= 2:
                        pe.wait_ge(self.o_out, gb + g[0] - 1)
                    nb = len(u["v"])
                    for x, vv in enumerate(u["v"]):
                        kk = vv.shape[0]
                        mm = pe.matmul(u["o"](g[0]), vv, self.PT[0:kk, j % 2, x * P:(x + 1) * P],
                                       start=u["start"] and x == 0, stop=u["stop"] and x == nb - 1)
                    if u["last"]:
                        mm.then_inc(self.o_ready, 1)
                        g[0] += 1

                for j, u in enumerate(U):
                    if j + 2 < len(U):
                        scores(j + 2)
                    pe.wait_ge(self.p_done, b + j + 1)
                    if j >= 1:
                        pe.wait_ge(self.pt_done, b + j)
                    for x in range(len(u["v"])):
                        mm = pe.transpose(ps[2][:, x * P:(x + 1) * P], self.T[:, j % 3, x * P:(x + 1) * P], ident[:])
                    mm.then_inc(self.t_ready, 1)
                    if j >= 1:
                        values(j - 1)
                values(len(U) - 1)

            def act(self, act, b=0):
                U = self.units

                def exp(j):
                    u = U[j]
                    act.wait_ge(self.max_done, b + j + 1)
                    src = ps[j % 2] if u["rel"] is None else self.T[:, j % 3]
                    st = self.st[:, j % 3]
                    if u.get("sink") is not None:
                        act.activation(st[:, 3:4], u["sink"], ACT.Exp, bias=st[:, 0:1])
                    act.activation(self.T[:, j % 3, 0:u["L"]], src[:, 0:u["L"]], ACT.Exp, bias=st[:, 0:1],
                                   scale=u["scale"], accum_out=st[:, 1:2]).then_inc(self.exp_done, 1)
                exp(0)
                if len(U) > 1:
                    exp(1)
                for j, u in enumerate(U):
                    act.wait_ge(self.t_ready, b + j + 1)
                    w = len(u["v"]) * P
                    act.activation(self.PT[:, j % 2, 0:w], ps[2][:, 0:w], ACT.Copy).then_inc(self.pt_done, 1)
                    if j + 2 < len(U):
                        exp(j + 2)

            def dve(self, v, b=0, gb=0):
                U = self.units

                def top(j):
                    u = U[j]
                    L, st, T = u["L"], self.st[:, j % 3], self.T[:, j % 3]
                    v.wait_ge(self.s_ready, b + j + 1)
                    src = ps[j % 2]
                    if u["rel"] is not None:
                        link(v, "dve", v.scalar_tensor_tensor(
                            out=T[:, 0:L], in0=u["rel"], scalar=-u["slope"] / u["scale"], in1=src[:, 0:L],
                            op0=ALU.mult, op1=ALU.add))
                        src = T
                    link(v, "dve", v.reduce_max(st[:, 2:3], src[:, 0:L], AX.X))
                    if u.get("sink") is not None:
                        link(v, "dve", v.tensor_scalar(st[:, 2:3], st[:, 2:3], u["scale"], u["sink"], ALU.mult, ALU.max))
                        v.tensor_scalar(st[:, 0:1], st[:, 2:3], -1.0, None, ALU.mult).then_inc(self.max_done, 1)
                    elif u.get("clamp"):
                        v.tensor_scalar(st[:, 0:1], st[:, 2:3], -1e20, -u["scale"], ALU.max, ALU.mult).then_inc(
                            self.max_done, 1)
                    else:
                        v.tensor_scalar(st[:, 0:1], st[:, 2:3], -u["scale"], None, ALU.mult).then_inc(self.max_done, 1)

                def fin(g, u):
                    v.wait_ge(self.o_ready, gb + g + 1)
                    self.finish(v, g, u).then_inc(self.o_out, 1)

                top(0)
                if len(U) > 1:
                    top(1)
                g, late = 0, []
                for j, u in enumerate(U):
                    st, T = self.st[:, j % 3], self.T[:, j % 3]
                    v.wait_ge(self.exp_done, b + j + 1)
                    if u.get("sink") is not None:
                        link(v, "dve", v.tensor_tensor(st[:, 1:2], st[:, 1:2], st[:, 3:4], ALU.add))
                    if u.get("clamp"):
                        link(v, "dve", v.tensor_scalar(st[:, 1:2], st[:, 1:2], TINY, None, ALU.max))
                    link(v, "dve", v.reciprocal(st[:, 4:5], st[:, 1:2]))
                    if u.get("gate") is not None:
                        v.tensor_scalar(T[:, 0:u["L"]], T[:, 0:u["L"]], st[:, 4:5], u["gate"], ALU.mult,
                                        ALU.mult).then_inc(self.p_done, 1)
                    else:
                        v.tensor_scalar(T[:, 0:u["L"]], T[:, 0:u["L"]], st[:, 4:5], None, ALU.mult).then_inc(
                            self.p_done, 1)
                    if j + 2 < len(U):
                        top(j + 2)
                    if late and late[0][0] <= j - 2:
                        fin(*late.pop(0)[1:])
                    if u["last"]:
                        late.append((j, g, u))
                        g += 1
                for _, x, u in late:
                    fin(x, u)

        T3 = sb("T3", X, [P, 3, S])
        PT2 = sb("PT2", X + 12, [P, 2, S])
        st3 = sb("st3", X + 20, [P, 3, 8])
        rel_sel = sb("rel_sel", X + 20.125, [P, S])
        rel_win = sb("rel_win", X + 24.125, [P, 640])
        rel_cmp = sb("rel_cmp", X + 26.625, [P, NT, 32])
        v_sel = sb("v_sel", X + 27.625, [P, NT, HD])
        v_win = sb("v_win", X + 29.625, [P, NT, HD])
        gates = sb("gates", X + 31.625, [P, NT, 12])
        pos2 = sb("pos2", X + 32.125, [P, 32])
        kc2 = sb("kc2", X + 32.25, [P, 32])
        vc = sb("vc", X + 32.375, [P, P])
        w2bd = sb("w2bd", X + 32.875, [P, P])
        chid = sb("chid", X + 33.375, [P, 32])
        chid2 = sb("chid2", X + 33.5, [P, 32])
        w1bd = sb("w1bd", V + 32, [P, 32, P])
        prepA = sem("prepA")
        gT = proj[:, 7]

        def act_prepA(act):
            load(act, rel_sel[:], io["rel_sel"])
            load(act, rel_win[:], io["rel_win"])
            load(act, rel_cmp[:], io["rel_cmp"])
            load(act, pos2[:], io["cmp_pos"])
            load(act, w2bd[:], io["cmp_w2"])
            load(act, w1bd[:], io["cmp_w1"])
            act.wait_ge(aux, aux_n[0])
            act.activation(gT, gT, ACT.Sigmoid).then_inc(prepA, 1)
            act.wait_ge(prepA, 3)
            act.activation(v_sel[:], ps[0][:].rearrange("p (t c) -> p t c", c=P)[:, :, HD:P], ACT.Copy)
            act.activation(proj[HD:P, 3], proj[0:HD, 3], ACT.Copy).then_inc(prepA, 1)
            act.wait_ge(prepA, 5)
            act.activation(v_win[:], ps[1][:].rearrange("p (t c) -> p t c", c=P)[:, :, HD:P], ACT.Copy)
            act.activation(proj[HD:P, 4], proj[0:HD, 4], ACT.Copy).then_inc(prepA, 1)
            act.wait_ge(prepA, 7)
            act.activation(chid[:], ps[2][:, 0:32], ACT.Sigmoid).then_inc(prepA, 1)
            act.wait_ge(prepA, 10)
            act.activation(vc[0:32, :], ps[2][0:32, 0:P], ACT.Copy)
            act.activation(kc2[0:HD, :], ps[3][0:HD, 0:32], ACT.Copy)
            act.activation(kc2[HD:P, :], ps[3][0:HD, 0:32], ACT.Copy).then_inc(prepA, 1)
            for z in (5, 6):
                act.activation(T3[:, z - 5], proj[:, z], ACT.Sigmoid)
            act.wait_ge(prepA, 12)

        def dve_prepA(v):
            v.wait_ge(prepA, 1)
            kv = proj[:, 2].rearrange("p (b l) -> p b l", l=32)
            v.tensor_tensor(kv, kv, pos2[:].unsqueeze(1).to_broadcast([P, 32, 32]), ALU.add).then_inc(prepA, 1)
            v.wait_ge(prepA, 8)
            v.tensor_tensor(chid2[:], chid[:], ps[2][:, 0:32], ALU.mult).then_inc(prepA, 1)
            v.wait_ge(prepA, 11)
            v.tensor_copy(gates[:], ps[0][:].rearrange("p (t c) -> p t c", c=P)[:, :, 0:12]).then_inc(prepA, 1)
            v.memset(T3[:, 2, 0:P], 0.0)

        def pe_prepA(pe):
            pe.wait_ge(prepA, 2)
            for t in range(NT):
                mm = pe.transpose(ps[0][:, t * P:(t + 1) * P], proj[:, 3, t * P:(t + 1) * P], ident[:])
            mm.then_inc(prepA, 1)
            pe.wait_ge(prepA, 4)
            for t in range(NT):
                mm = pe.transpose(ps[1][:, t * P:(t + 1) * P], proj[:, 4, t * P:(t + 1) * P], ident[:])
            mm.then_inc(prepA, 1)
            pe.wait_ge(prepA, 6)
            for l in range(32):
                mm = pe.matmul(ps[2][:, 0:32], w1bd[:, l], proj[:, 2].rearrange("p (b l) -> p l b", l=32)[:, l],
                               start=l == 0, stop=l == 31)
            mm.then_inc(prepA, 1)
            pe.wait_ge(prepA, 9)
            for t in range(NT):
                pe.transpose(ps[0][:, t * P:(t + 1) * P], gT[:, t * P:(t + 1) * P], ident[:])
            pe.matmul(ps[2][0:32, 0:P], chid2[:], w2bd[:], start=True, stop=True)
            pe.matmul(ps[3][:, 0:32], w2bd[:], chid2[:], start=True, stop=True).then_inc(prepA, 1)

        def rows(h):
            return slice(HD * (h % 2), HD * (h % 2) + HD)

        def unitsA():
            U = []
            for p in range(2):
                for it in range(NT):
                    for hh in range(2):
                        h, r = 2 * p + hh, rows(hh)
                        q = proj[r, p, it * P:(it + 1) * P]
                        w0 = max(0, it - 4)
                        for br in ("win", "sel", "cmp"):
                            u = dict(scale=HD ** -0.5, slope=SLOPES[h], first=hh == 0 and br == "win",
                                     last=hh == 1 and br == "cmp", start=br == "win", stop=br == "cmp",
                                     o=lambda g, r=r: ps[3][r, g % 2 * HALF:g % 2 * HALF + P], pair=p, it=it)
                            if br == "sel":
                                u.update(L=(it + 1) * P, qk=[(q, proj[r, 3])], rel=rel_sel[:, (NT - 1 - it) * P:S],
                                         v=[v_sel[:, t] for t in range(it + 1)], gate=gates[:, it, 3 * h + 1:3 * h + 2])
                            elif br == "win":
                                u.update(L=(it + 1 - w0) * P, qk=[(q, proj[r, 4, w0 * P:(it + 1) * P])],
                                         rel=rel_win[:, 640 - (it + 1 - w0) * P:640],
                                         v=[v_win[:, t] for t in range(w0, it + 1)],
                                         gate=gates[:, it, 3 * h + 2:3 * h + 3])
                            else:
                                u.update(L=32, qk=[(q, kc2[r, :])], rel=rel_cmp[:, it], v=[vc[0:32, HD:P]], clamp=True,
                                         gate=gates[:, it, 3 * h:3 * h + 1])
                            U.append(u)
            return U

        def gated(z0):
            def f(v, g, u):
                z = proj[:, z0 + u["pair"], u["it"] * P:(u["it"] + 1) * P]
                return v.tensor_tensor(z, ps[3][:, g % 2 * HALF:g % 2 * HALF + P], z, ALU.mult)
            return f

        softA = Soft("nsa", unitsA(), T3, PT2, st3, gated(5))

        rel_swa = sb("rel_swa", X + 20.125, [P, 2 * P])
        v_swa = sb("v_swa", X + 21.125, [P, NT, P])
        sink_bc = sb("sink_bc", X + 25.125, [P, 4])
        prepB = sem("prepB")

        def act_prepB(act):
            load(act, rel_swa[:], io["rel_swa"])
            load(act, sink_bc[:], io["sink"].to_broadcast([P, 4]))
            act.wait_ge(aux, aux_n[0])
            act.wait_ge(prepB, 1)
            act.activation(v_swa[:], ps[0][:].rearrange("p (t c) -> p t c", c=P), ACT.Copy)
            act.activation(proj[0:HD, 3], proj[HD:P, 2], ACT.Copy)
            link(act, "act", act.activation(proj[HD:P, 3], proj[HD:P, 2], ACT.Copy))
            act.activation(proj[HD:P, 2], proj[0:HD, 2], ACT.Copy)
            for z in (4, 5):
                act.activation(T3[:, z - 4], proj[:, z], ACT.Sigmoid)

        def pe_prepB(pe):
            for t in range(NT):
                mm = pe.transpose(ps[0][:, t * P:(t + 1) * P], proj[:, 3, t * P:(t + 1) * P], ident[:])
            mm.then_inc(prepB, 1)

        def unitsB():
            U = []
            for p in range(2):
                for it in range(NT):
                    for hh in range(2):
                        h, r = 2 * p + hh, rows(hh)
                        w0 = max(0, it - 1)
                        U.append(dict(
                            scale=HD ** -0.5, slope=SLOPES[h], first=hh == 0, last=hh == 1, start=True, stop=True,
                            o=lambda g, r=r: ps[3][r, g % 2 * HALF:g % 2 * HALF + P], pair=p, it=it, L=(it + 1 - w0) * P,
                            qk=[(proj[r, p, it * P:(it + 1) * P], proj[r, 2 + p, w0 * P:(it + 1) * P])],
                            rel=rel_swa[:, 2 * P - (it + 1 - w0) * P:2 * P], sink=sink_bc[:, h:h + 1],
                            v=[v_swa[:, t, p * HD:(p + 1) * HD] for t in range(w0, it + 1)]))
            return U

        softB = Soft("swa", unitsB(), T3, PT2, st3, gated(4))

        def dve_silu(v, z0):
            for z in range(2):
                v.tensor_tensor(proj[:, z0 + z], proj[:, z0 + z], T3[:, z], ALU.mult)

        Lb = sb("Lb", X, [P, 2, S])
        Ls = sb("Ls", X + 8, [P, S])
        v_nat = sb("v_nat", X + 21, [P, NT, 2 * P])
        sum_neg = sb("sum_neg", X + 29, [P, P])
        negs = sb("negs", X + 29.5, [P, P])
        mask_lt = sb("mask_lt", X + 30, [P, P])
        neg_ge = sb("neg_ge", X + 30.5, [P, P])
        E2 = sb("E2", X + 31, [P, S])
        prepC, stk_z, stk_c, stk_e, stk_L, stk_s, stk_a, stk_o, stk_out = (
            sem(x) for x in ("prepC", "stk_z", "stk_c", "stk_e", "stk_L", "stk_s", "stk_a", "stk_o", "stk_out"))
        units4 = [(p, it, hh) for p in range(2) for it in range(NT) for hh in range(2)]

        def act_prep_v(act, sm, zdst):
            for x in range(2):
                act.wait_ge(sm, x + 1)
                act.activation(v_nat[:, :, x * P:(x + 1) * P], ps[x][:].rearrange("p (t c) -> p t c", c=P), ACT.Copy)
            for x in range(2):
                act.activation(zdst[:, x], proj[:, 6 + x], ACT.Sigmoid)
            for x in range(2):
                act.mul(proj[:, x], proj[:, x], HD ** -0.5)

        def pe_prep_v(pe, sm):
            for x in range(2):
                for t in range(NT):
                    mm = pe.transpose(ps[x][:, t * P:(t + 1) * P], proj[:, 4 + x, t * P:(t + 1) * P], ident[:])
                mm.then_inc(sm, 1)

        def act_prepC(act):
            for dst, name in ((sum_neg, "sum_neg"), (negs, "neg"), (mask_lt, "mask_lt"), (neg_ge, "neg_ge")):
                load(act, dst[:], io["consts"][CI[name]])
            act.wait_ge(aux, aux_n[0])
            act_prep_v(act, prepC, PT2)

        def dve_silu_cd(v, zsrc):
            for x in range(2):
                v.tensor_tensor(proj[:, 6 + x], proj[:, 6 + x], zsrc[:, x], ALU.mult)

        def pe_stick(pe):
            def z(j):
                p, it, hh = units4[j]
                r = rows(hh)
                if j >= 2:
                    pe.wait_ge(stk_a, j - 1)
                for d in range(it + 1):
                    mm = pe.matmul(ps[j % 2][:, d * P:(d + 1) * P], proj[r, 2 + p, (it - d) * P:(it - d + 1) * P],
                                   proj[r, p, it * P:(it + 1) * P], start=d % 4 == 0, stop=False, skip_group_check=True)
                mm.then_inc(stk_z, 1)

            def sums(j):
                p, it, hh = units4[j]
                pe.wait_ge(stk_s, j + 1)
                t = ps[j % 2]
                for d in range(it + 1):
                    if d == 0:
                        pe.matmul(t[:, 0:P], ident[:], neg_ge[:], start=False, stop=False, skip_group_check=True)
                    else:
                        pe.matmul(t[:, d * P:(d + 1) * P], negs[:], Ls[:, d * P:(d + 1) * P], start=False,
                                  stop=False, skip_group_check=True)
                    mm = pe.matmul(t[:, d * P:(d + 1) * P], sum_neg[:], Lb[:, j % 2, d * P:(d + 1) * P], start=False,
                                   stop=d == it or d % 4 == 3, skip_group_check=True)
                mm.then_inc(stk_L, 1)

            def pv(j):
                p, it, hh = units4[j]
                g = j // 2
                pe.wait_ge(stk_a, j + 1)
                if hh == 0 and g >= 2:
                    pe.wait_ge(stk_out, g - 1)
                for d in range(it + 1):
                    mm = pe.matmul(ps[3][rows(hh), g % 2 * HALF:g % 2 * HALF + P],
                                   v_nat[:, it - d, (2 * p + hh) * HD:(2 * p + hh + 1) * HD],
                                   PT2[:, j % 2, d * P:(d + 1) * P], start=d == 0, stop=d == it)
                if hh == 1:
                    mm.then_inc(stk_o, 1)
            N = len(units4)
            z(0)
            for j in range(N):
                if j + 1 < N:
                    z(j + 1)
                sums(j)
                if j >= 1:
                    pv(j - 1)
            pv(N - 1)

        def act_stick(act):
            act.preload_act_table_set("natural_log_exp_and_others")

            def soft(j):
                w = (units4[j][1] + 1) * P
                act.wait_ge(stk_c, j + 1)
                link(act, "act", act.activation(E2[:, 0:w], E2[:, 0:w], ACT.Exp))
                act.activation(E2[:, 0:w], E2[:, 0:w], ACT.Ln, bias=1.0).then_inc(stk_e, 1)

            def prob(j):
                w = (units4[j][1] + 1) * P
                act.wait_ge(stk_L, j + 1)
                act.activation(PT2[:, j % 2, 0:w], ps[j % 2][:, 0:w], ACT.Exp).then_inc(stk_a, 1)
            N = len(units4)
            soft(0)
            for j in range(N):
                if j + 1 < N:
                    soft(j + 1)
                prob(j)

        def dve_stick(v):
            def clip(j):
                w = (units4[j][1] + 1) * P
                v.wait_ge(stk_z, j + 1)
                if j >= 1:
                    v.wait_ge(stk_e, j)
                v.tensor_scalar(E2[:, 0:w], ps[j % 2][:, 0:w], 40.0, None, ALU.min).then_inc(stk_c, 1)

            def plus(j):
                it = units4[j][1]
                w = (it + 1) * P
                v.wait_ge(stk_e, j + 1)
                L, R = Lb[:, j % 2], Ls
                if j >= 1:
                    v.wait_ge(stk_L, j)
                link(v, "dve", v.tensor_tensor(L[:, 0:w], E2[:, 0:w], ps[j % 2][:, 0:w], ALU.max))
                ins = v.tensor_tensor(L[:, 0:P], L[:, 0:P], mask_lt[:], ALU.mult)
                for d in range(1, it + 1):
                    link(v, "dve", ins)
                    if d == 1:
                        ins = v.tensor_copy(R[:, P:2 * P], L[:, 0:P])
                    else:
                        ins = v.tensor_tensor(R[:, d * P:(d + 1) * P], R[:, (d - 1) * P:d * P], L[:, (d - 1) * P:d * P],
                                              ALU.add)
                ins.then_inc(stk_s, 1)

            def fin(g):
                p, it, _ = units4[2 * g]
                v.wait_ge(stk_o, g + 1)
                z = proj[:, 6 + p, it * P:(it + 1) * P]
                v.tensor_tensor(z, ps[3][:, g % 2 * HALF:g % 2 * HALF + P], z, ALU.mult).then_inc(stk_out, 1)
            N = len(units4)
            clip(0)
            for j in range(N):
                plus(j)
                if j + 1 < N:
                    clip(j + 1)
                if j >= 3 and j % 2 == 1:
                    fin(j // 2 - 1)
            fin(N // 2 - 1)

        decay = sb("decay", X + 4, [P, 4, S])
        rPT = sb("rPT", X, [P, S])
        rP = [rPT, sb("rP1", X + 31, [P, S])]
        o_ret = proj[:, 4:6]
        zsig = sb("zsig", V + 32, [P, 2, S])
        onesh = sb("onesh", X + 29, [P, P])
        prepD, ret_s, ret_p, ret_o, ret_out, ln = (sem(x) for x in ("prepD", "ret_s", "ret_p", "ret_o", "ret_out", "ln"))

        def act_prepD(act):
            load(act, decay[:], io["decay"])
            load(act, onesh[:], io["consts"][CI["ones_h"]])
            act.wait_ge(aux, aux_n[0])
            act_prep_v(act, prepD, zsig)

        def pe_ret(pe):
            def sc(j):
                p, it, hh = units4[j]
                r = rows(hh)
                if j >= 2:
                    pe.wait_ge(ret_p, j - 1)
                for d in range(it + 1):
                    mm = pe.matmul(ps[j % 2][:, d * P:(d + 1) * P], proj[r, 2 + p, (it - d) * P:(it - d + 1) * P],
                                   proj[r, p, it * P:(it + 1) * P], start=True, stop=True)
                mm.then_inc(ret_s, 1)

            def pv(j):
                p, it, hh = units4[j]
                g = j // 2
                pe.wait_ge(ret_p, j + 1)
                if hh == 0 and g >= 2:
                    pe.wait_ge(ret_out, g - 1)
                for d in range(it + 1):
                    mm = pe.matmul(ps[3][rows(hh), g % 2 * HALF:g % 2 * HALF + P],
                                   v_nat[:, it - d, (2 * p + hh) * HD:(2 * p + hh + 1) * HD],
                                   rP[j % 2][:, d * P:(d + 1) * P], start=d == 0, stop=d == it)
                mm.then_inc(ret_o, 1)
            sc(0)
            for j in range(len(units4)):
                if j + 1 < len(units4):
                    sc(j + 1)
                pv(j)
            for x in range(2):
                pe.wait_ge(ln, 5 * x + 1)
                for h in range(2):
                    mm = pe.matmul(ps[x][:, h * HALF:(h + 1) * HALF], onesh[:], o_ret[:, x, h * HALF:(h + 1) * HALF],
                                   start=True, stop=True)
                mm.then_inc(ln, 1)
                pe.wait_ge(ln, 5 * x + 4)
                for h in range(2):
                    mm = pe.matmul(ps[x][:, h * HALF:(h + 1) * HALF], onesh[:], rPT[:, h * HALF:(h + 1) * HALF],
                                   start=True, stop=True)
                mm.then_inc(ln, 1)

        def dve_ret(v):
            for j, (p, it, hh) in enumerate(units4):
                w = (it + 1) * P
                v.wait_ge(ret_s, j + 1)
                if j >= 2:
                    v.wait_ge(ret_o, j - 1)
                v.tensor_tensor(rP[j % 2][:, 0:w], ps[j % 2][:, 0:w], decay[:, 2 * p + hh, 0:w], ALU.mult).then_inc(ret_p, 1)
            for x in range(2):
                if x == 0:
                    v.wait_ge(ret_out, 2 * NT)
                    v.tensor_copy(rP[1][:, 0:2], onesh[:, 0:2]).then_inc(ln, 1)
                else:
                    v.tensor_copy(rP[1][:, 0:2], onesh[:, 0:2]).then_inc(ln, 1)
                v.wait_ge(ln, 5 * x + 2)
                v.tensor_tensor(o_ret[:, x], o_ret[:, x], ps[x][:], ALU.subtract).then_inc(ln, 1)
                v.wait_ge(ln, 5 * x + 5)
                v.wait_ge(ret_rt, x + 1)
                link(v, "dve", v.reciprocal(rP[1][:], rP[1][:]))
                link(v, "dve", v.tensor_tensor(o_ret[:, x], o_ret[:, x], rP[1][:], ALU.mult))
                link(v, "dve", v.tensor_tensor(proj[:, 6 + x], proj[:, 6 + x], o_ret[:, x], ALU.mult))

        ret_rt = sem("ret_rt")

        def act_ret(act):
            for g in range(2 * NT):
                p, it, _ = units4[2 * g]
                act.wait_ge(ret_o, 2 * g + 2)
                act.activation(o_ret[:, p, it * P:(it + 1) * P], ps[3][:, g % 2 * HALF:g % 2 * HALF + P],
                               ACT.Copy).then_inc(ret_out, 1)
            for x in range(2):
                act.wait_ge(ln, 5 * x + 3)
                act.activation(rPT[:], o_ret[:, x], ACT.Square).then_inc(ln, 1)
                act.wait_ge(ln, 5 * x + 5)
                act.activation(rP[1][:], ps[x][:], ACT.Sqrt, bias=eps_col(LN_EPS)).then_inc(ret_rt, 1)

        R = proj
        m_sig = sb("m_sig", X, [P, 2, S])
        m_t = sb("m_t", X + 8, [P, 2, S])
        ysplit = {b: Split(f"ysplit{b}", proj[:, z:z + 2], 2, Ya_hi, Ya_lo)
                  for b, z in (("A", 5), ("B", 4), ("C", 6), ("D", 6))}
        sig_done = sem("sig_done")
        sig_n = {"act": 0, "dve": 0}

        def act_merge(act):
            s0 = sig_n["act"]
            def one(j, t):
                par = 0 if t is ps[0] else 1
                act.wait_ge(evac_dve, tiles["act"] + 1 + j)
                act.activation(m_sig[:, par], t[:], ACT.Sigmoid).then_inc(evac_act, 1)
            each_tile(act, "act", 8, one)

        def dve_merge(v, first):
            g0 = tiles["dve"]
            c = own["dve"]

            def one(j, par):
                v.wait_ge(evac_act, g0 + 3 + j)
                t = m_sig[:, (g0 + par) % 2]
                if first:
                    v.tensor_tensor(ACC[:, j], t, R[:, j], ALU.mult).then_inc(evac_dve, 1)
                else:
                    link(v, "dve", v.tensor_tensor(m_t[:, par], t, R[:, j], ALU.mult))
                    v.tensor_tensor(ACC[:, j], ACC[:, j], m_t[:, par], ALU.add).then_inc(evac_dve, 1)
            if first:
                pairs(v, 8, one)
            else:
                with v.Fori(0, 4) as i:
                    c.enter(i, 2)
                    for s in range(2):
                        one(2 * i + s, s)
                c.leave(4)
            tiles["dve"] += 8

        merged = Split("merged", ACC, NT, Y_hi, Y_lo)
        x_back = sem("x_back")

        def act_out1(act):
            def one(j, t):
                act.activation(t[:, 0:2], t[:, 0:2], ACT.Copy)
            for k in range(NT):
                load(act, ACC[:, k], io["x"][k])
            act.wait_ge(aux, aux_n[0])
            act.drain().then_inc(x_back, 1)
            act_gemm_none(act, 8)

        def act_gemm_none(act, n):
            def one(j, t):
                act.sem_inc(evac_act, 1)
            each_tile(act, "act", n, one)

        def dve_out1(v):
            v.wait_ge(x_back, 1)

            def one(j, t):
                v.scalar_tensor_tensor(out=ACC[:, j], in0=t[:], scalar=cols[:, bass.ds(C_MOD + 16 + j, 1)], in1=ACC[:, j],
                                       op0=ALU.mult, op1=ALU.add).then_inc(evac_dve, 1)
            each_tile(v, "dve", 8, one)

        norm_f = Norm("norm_f", ACC, NT, ones_d, cols[:, C_FG:C_FG + 8], into=ACC)
        norm_e = Norm("norm_e", ACC, NT, ones_d, cols[:, C_EG:C_EG + 8], hi=H_hi, lo=H_lo)

        G_EPOST, G_OPRE, G_OPOST, G_GNG, G_GNB, G_CB, G_HN, G_Q, G_KV, G_BG, G_INV = (
            0, 8, 16, 24, 32, 40, 48, 56, 59, 61, 62)
        keep1 = nc.dram_tensor("keep1", (NT, P, S), F32).ap()
        keep2 = nc.dram_tensor("keep2", (NT, P, S), F32).ap()
        kept = sem("kept")
        kept_n = [0]

        def keep(act, dst):
            for k in range(NT):
                act.dma_start(dst[k], ACC[:, k]).then_inc(kept, 16)
                kept_n[0] += 16
            act.wait_ge(kept, kept_n[0])

        Dw = sb("Dw", V, [P, NT, S])
        Db = sb("Db", V + 32, [P, NT, P])
        QKV = sb("QKV", V + 36, [P, 4, S])
        hn = QKV[:, 2:4].rearrange("p a (t c) -> p (a t) c", c=256)
        Vn = sb("Vn", V + 52, [P, NT, 264])
        PTl = sb("PTl", V + 60.25, [P, 2, 9, P])
        Mrow = sb("Mrow", V + 69.25, [4, 2, S])
        lst = sb("lst", V + 77.25, [P, 160])
        a_col = lst[:, 0:64].rearrange("p (d t c) -> p d t c", d=2, t=NT)
        emm = lst[:, 64:128].rearrange("p (d t c) -> p d t c", d=2, t=NT)
        ss8 = lst[:, 128:136]
        rr8 = lst[:, 136:144]
        den = lst[:, 144:160]
        neg_f = sb("neg_f", V + 78, [P, P])
        neg_b = sb("neg_b", V + 78.5, [P, P])
        sel4 = sb("sel4", V + 79, [4, 4, P])
        OZ = sb("OZ", V, [P, 4, S])
        ozs = sb("ozs", V + 16, [P, 4, S])
        gT2 = sb("gT2", V, [P, 1, S])
        arow = sb("arow", V + 4, [4, 2, S])
        cum = [sb("cum_f", V + 12, [P, P]), sb("cum_b", V + 12.5, [P, P])]
        ones1 = sb("ones1", V + 13, [P, P])
        gw = sb("gw", V + 13.5, [P, 6, 128])
        gn = gw[:, 0]
        gn5 = gn.rearrange("p (t d x c) -> p d t x c", t=NT, d=2, x=2)
        fpre, ipre = gn5[:, :, :, 1], gn5[:, :, :, 0]

        def dtc(x):
            return gw[:, x, 0:64].rearrange("p (d t c) -> p d t c", d=2, t=NT)
        fab, flg, lf, lfs, Fc = dtc(1), dtc(2), dtc(3), dtc(4), dtc(5)
        gp = sem("gp")

        def act_gates(act):
            keep(act, keep1)
            for t, n in ((cum[0], "cum_f"), (cum[1], "cum_b"), (ones1, "ones"), (neg_f, "neg_f"), (neg_b, "neg_b")):
                load(act, t[:], io["consts"][CI[n]])
            load(act, sel4[:], io["sel4"])
            act.wait_ge(aux, aux_n[0])
            act.activation(gT2[:, 0], gT2[:, 0], ACT.Identity, bias=cols2[:, G_BG:G_BG + 1]).then_inc(gp, 1)
            act.wait_ge(gp, 3)
            link(act, "act", act.activation(flg, fab, ACT.Exp, scale=-1.0))
            act.activation(flg, flg, ACT.Ln, bias=1.0).then_inc(gp, 1)
            act.wait_ge(gp, 11)
            act.activation(emm, fab, ACT.Exp, scale=-1.0).then_inc(gp, 1)

        def pe_gates(pe):
            pe.wait_ge(gp, 1)
            for t in range(NT):
                mm = pe.transpose(ps[0][:, t * P:(t + 1) * P], gT2[:, 0, t * P:(t + 1) * P], ident[:])
            mm.then_inc(gp, 1)
            pe.wait_ge(gp, 5)
            for d in range(2):
                o = ps[1][:, d * 32:(d + 1) * 32]
                pe.matmul(o, cum[d][:], lf[:, d], start=True, stop=False)
                mm = pe.matmul(o, ones1[:], lfs[:, d], start=False, stop=True)
            mm.then_inc(gp, 1)
            pe.wait_ge(gp, 7)
            for d in range(2):
                for t in range(NT):
                    mm = pe.transpose(ps[2 + d][0:4, t * P:(t + 1) * P], a_col[:, d, t], ident[:])
            mm.then_inc(gp, 1)
            pe.wait_ge(gp, 9)
            for d in range(2):
                for t in range(NT):
                    x = (d * NT + t) * 4
                    mm = pe.transpose(ps[0][:, x:x + 4], Mrow[0:4, d, t * P:(t + 1) * P], ident[0:4, 0:4])
            mm.then_inc(gp, 1)

        def dve_gates(v):
            v.wait_ge(gp, 2)
            link(v, "dve", v.tensor_copy(gn.rearrange("p (t c) -> p t c", t=NT),
                                         ps[0][:].rearrange("p (t c) -> p t c", c=P)[:, :, 0:16]))
            for d in range(2):
                ins = v.scalar_tensor_tensor(out=fab[:, d], in0=fpre[:, d], scalar=-1.0, in1=fpre[:, d], op0=ALU.mult,
                                             op1=ALU.max)
            ins.then_inc(gp, 1)
            v.wait_ge(gp, 4)
            for d in range(2):
                ins = v.scalar_tensor_tensor(out=lf[:, d], in0=fpre[:, d], scalar=0.0, in1=flg[:, d], op0=ALU.min,
                                             op1=ALU.subtract)
            link(v, "dve", ins)
            for d in range(2):
                order = list(range(NT)) if d == 0 else list(range(NT - 1, -1, -1))
                link(v, "dve", v.memset(lfs[:, d, order[0]], 0.0))
                for a, b in zip(order, order[1:]):
                    link(v, "dve", v.tensor_tensor(lfs[:, d, b], lfs[:, d, a], lf[:, d, a], ALU.add))
            v.drain().then_inc(gp, 1)
            v.wait_ge(gp, 6)
            link(v, "dve", v.tensor_copy(gw[:, 5, 0:64], ps[1][:, 0:64]))
            for d in range(2):
                ins = v.tensor_tensor(a_col[:, d], ipre[:, d], Fc[:, d], ALU.subtract)
            ins.then_inc(gp, 1)
            v.wait_ge(gp, 8)
            for d in range(2):
                link(v, "dve", v.tensor_copy(arow[:, d], ps[2 + d][0:4, :]))
                a, m = arow[:, d], Mrow[:, d]
                if d:
                    a, m = a[:, ::-1], m[:, ::-1]
                ins = v.tensor_tensor_scan(m, a, a, 0.0, ALU.max, ALU.max)
                link(v, "dve", ins)
            v.drain().then_inc(gp, 1)
            v.wait_ge(gp, 10)
            v.tensor_tensor(gw[:, 1, 0:64], gw[:, 5, 0:64], ps[0][:, 0:64], ALU.add).then_inc(gp, 1)
            v.wait_ge(gp, 12)
            v.memset(Vn[:, :, 256:257], 1.0)

        DK = 128.0 ** -0.5

        class Lstm:
            def __init__(self, h):
                self.h = h
                self.turned, self.diag, self.s, self.p, self.o, self.o_out, self.t, self.g, self.f = (
                    shared(f"lstm_{x}") for x in ("turned", "diag", "scores", "p", "o", "oout", "t", "g", "f"))
                self.at = since("lstm", turned=3, diag=1, s=NT, p=NT, o=NT, o_out=NT, t=1, g=4, f=2)

            def pe_w(self, pe):
                h = self.h
                for x in range(2):
                    for t in range(NT):
                        mm = pe.transpose(ps[x][:, t * P:(t + 1) * P], QKV[:, 2 + x, t * P:(t + 1) * P], ident[:])
                    mm.then_inc(self.turned, 1)
                for d in range(2):
                    for k in range(2):
                        mm = pe.matmul(ps[2 + d][:, k * HALF:(k + 1) * HALF], sel4[:, h],
                                       Mrow[:, d, k * HALF:(k + 1) * HALF], start=True, stop=True)
                mm.then_inc(self.turned, 1)

            def act_w(self, act):
                h = self.h
                for x in range(2):
                    act.wait_ge(self.turned, self.at['turned'] + x + 1)
                    act.activation(Vn[:, :, x * P:(x + 1) * P], ps[x][:].rearrange("p (t c) -> p t c", c=P), ACT.Copy)
                act.wait_ge(self.diag, self.at['diag'] + 1)
                for st in range(NT):
                    if st < NT - 1:
                        act.activation(Dw[:, st, (st + 1) * P:S], ps[2][:, (st + 1) * P:S], ACT.Exp,
                                       bias=a_col[:, 0, st, h:h + 1])
                    if st > 0:
                        act.activation(Dw[:, st, 0:st * P], ps[3][:, 0:st * P], ACT.Exp, bias=a_col[:, 1, st, h:h + 1])
                for st in range(NT):
                    d = Dw[:, st, st * P:(st + 1) * P]
                    act.activation(d, d, ACT.Exp)
                act.activation(Db[:], Db[:], ACT.Exp)

            def dve_w(self, v):
                h = self.h
                v.wait_ge(self.turned, self.at['turned'] + 3)
                for st in range(NT):
                    c = slice(st * P, (st + 1) * P)
                    v.scalar_tensor_tensor(out=Dw[:, st, c], in0=ps[2][:, c], scalar=a_col[:, 0, st, h:h + 1],
                                           in1=neg_f[:], op0=ALU.add, op1=ALU.add)
                    ins = v.scalar_tensor_tensor(out=Db[:, st], in0=ps[3][:, c], scalar=a_col[:, 1, st, h:h + 1],
                                                 in1=neg_b[:], op0=ALU.add, op1=ALU.add)
                ins.then_inc(self.diag, 1)

            def pe(self, pe):
                def sc(it):
                    if it >= 2:
                        pe.wait_ge(self.p, self.at['p'] + it - 1)
                    for st in range(NT):
                        mm = pe.matmul(ps[it % 2][:, st * P:(st + 1) * P], QKV[:, 1, st * P:(st + 1) * P],
                                       QKV[:, 0, it * P:(it + 1) * P], start=True, stop=True)
                    mm.then_inc(self.s, 1)
                sc(0)
                for it in range(NT):
                    if it + 1 < NT:
                        sc(it + 1)
                    pe.wait_ge(self.p, self.at['p'] + it + 1)
                    if it >= 2:
                        pe.wait_ge(self.o_out, self.at['o_out'] + it - 1)
                    c = it % 2 * HALF
                    for st in range(it + 1):
                        pe.matmul(ps[2][:, c:c + 257], PTl[:, it % 2, st], Vn[:, st, 0:257], start=st == 0, stop=st == it)
                    for st in range(it, NT):
                        mm = pe.matmul(ps[3][:, c:c + 257], PTl[:, it % 2, st + 1], Vn[:, st, 0:257], start=st == it,
                                       stop=st == NT - 1)
                    mm.then_inc(self.o, 1)

            def dve(self, v):
                h = self.h

                def probs(it):
                    v.wait_ge(self.s, self.at['s'] + it + 1)
                    if it >= 2:
                        v.wait_ge(self.o, self.at['o'] + it - 1)
                    q3 = ps[it % 2][:].rearrange("p (s c) -> p s c", c=P)
                    c = slice(it * P, (it + 1) * P)
                    o = PTl[:, it % 2]
                    v.scalar_tensor_tensor(out=o[:, 0:it + 1], in0=q3[:, 0:it + 1], scalar=DK, in1=Dw[:, 0:it + 1, c],
                                           op0=ALU.mult, op1=ALU.mult)
                    if it < NT - 1:
                        v.scalar_tensor_tensor(out=o[:, it + 2:9], in0=q3[:, it + 1:NT], scalar=DK,
                                               in1=Dw[:, it + 1:NT, c], op0=ALU.mult, op1=ALU.mult)
                    v.scalar_tensor_tensor(out=o[:, it + 1], in0=q3[:, it], scalar=DK, in1=Db[:, it],
                                           op0=ALU.mult, op1=ALU.mult).then_inc(self.p, 1)

                def outs(it):
                    v.wait_ge(self.o, self.at['o'] + it + 1)
                    c = it % 2 * HALF
                    for d in range(2):
                        ins = v.tensor_scalar(den[:, d:d + 1], ps[2 + d][:, c + 256:c + 257], -1.0,
                                              emm[:, d, it, h:h + 1], ALU.mult, ALU.max)
                    link(v, "dve", ins)
                    for d in range(2):
                        ins = v.tensor_tensor(den[:, 2 + d:3 + d], den[:, d:d + 1], ps[2 + d][:, c + 256:c + 257],
                                              ALU.max)
                    link(v, "dve", ins)
                    link(v, "dve", v.reciprocal(den[:, 4:6], den[:, 2:4]))
                    link(v, "dve", v.tensor_scalar(hn[:, it], ps[2][:, c:c + 256], den[:, 4:5], None, ALU.mult))
                    v.scalar_tensor_tensor(out=hn[:, it], in0=ps[3][:, c:c + 256], scalar=den[:, 5:6], in1=hn[:, it],
                                           op0=ALU.mult, op1=ALU.add).then_inc(self.o_out, 1)
                for it in range(NT):
                    probs(it)
                    if it >= 1:
                        outs(it - 1)
                outs(NT - 1)
                v.wait_ge(self.t, self.at['t'] + 1)
                link(v, "dve", v.reciprocal(rr8, ss8))
                v.tensor_tensor(hn, hn, rr8.unsqueeze(2).to_broadcast([P, NT, 256]), ALU.mult)

            def act(self, act):
                for it in range(NT):
                    act.wait_ge(self.o_out, self.at['o_out'] + it + 1)
                    link(act, "act", act.activation(lsq, hn[:, it], ACT.Square, accum_out=ss8[:, it:it + 1]))
                act.activation(ss8, ss8, ACT.Sqrt, bias=eps_col(RMS_EPS), scale=1.0 / 256).then_inc(self.t, 1)

            def pe_f(self, pe):
                for x in range(2):
                    for t in range(NT):
                        mm = pe.transpose(ps[x][:, t * P:(t + 1) * P], hn[:, t, x * P:(x + 1) * P], ident[:])
                    mm.then_inc(self.f, 1)

            def act_f(self, act):
                for x in (0, 2, 1, 3):
                    act.activation(ozs[:, x], OZ[:, x], ACT.Sigmoid).then_inc(self.g, 1)

            def dve_f(self, v):
                h = self.h
                for x in range(2):
                    y = ACC[:, 2 * h + x]
                    v.wait_ge(self.g, self.at['g'] + 2 * x + 2)
                    v.wait_ge(self.f, self.at['f'] + x + 1)
                    link(v, "dve", v.scalar_tensor_tensor(out=y, in0=ps[x][:], scalar=cols2[:, G_HN + 2 * h + x:G_HN + 2 * h + x + 1],
                                                          in1=ozs[:, x], op0=ALU.mult, op1=ALU.mult))
                    link(v, "dve", v.tensor_tensor(OZ[:, 2 + x], OZ[:, 2 + x], ozs[:, 2 + x], ALU.mult))
                    v.tensor_tensor(y, y, OZ[:, 2 + x], ALU.mult)

        lsq = sb("lsq", V + 81, [P, 256])[:]
        lstm = [Lstm(h) for h in range(H_B)]
        split_b = Split("split_b", ACC, NT, Y_hi, Y_lo)

        Z_hi = sb("Z_hi", 0, [P, NT, S], F32R)
        Z_lo = sb("Z_lo", 32, [P, NT, S], F32R)
        ya = sb("ya", V, [P, NT, S])
        W = V + 32
        Uc = sb("Uc", W, [P, S + 32])
        cacc = [sb("cacc0", W + 4.25, [P, S]), sb("cacc1", W + 42, [P, S])]
        c_sg = sb("c_sg", W + 8.25, [P, S])
        c_sz = sb("c_sz", W + 12.25, [P, S])
        c_zs = [sb("c_zs0", W + 16.25, [P, S]), sb("c_zs1", W + 46, [P, S])]
        c_sq = sb("c_sq", W + 20.25, [P, S])
        c_rt = sb("c_rt", W + 24.25, [P, S])
        c_v = sb("c_v", W + 28.25, [P, S])
        c_s = sb("c_s", W + 32.25, [P, S])
        c_rs = sb("c_rs", W + 36.25, [P, S])
        conv_w = sb("conv_w", W + 40.25, [P, NT, CONV_K + 1])
        ones_c = sb("ones_c", W + 41.5, [P, P])
        conv_in, gn_s = sem("conv_in"), sem("gn_s")

        def act_conv(act):
            g0 = tiles["act"]

            def gate(c):
                g = g0 + 3 * c
                act.wait_ge(out_ready, g + 1)
                if c:
                    act.wait_ge(conv_in, c)
                act.activation(c_sg[:], ps[g % 2][:], ACT.Sigmoid).then_inc(evac_act, 1)
                act.drain().then_inc(evac_act, 1)

            def zgate(c):
                g = g0 + 3 * c
                act.wait_ge(out_ready, g + 3)
                act.activation(c_sz[:], ps[(g + 2) % 2][:], ACT.Sigmoid).then_inc(evac_act, 1)
            gate(0)
            zgate(0)
            for c in range(NT + 1):
                b = 7 * (c - 1)
                if c:
                    act.wait_ge(gn_s, b + 3)
                    act.activation(c_sq[:], cacc[(c - 1) % 2][:], ACT.Square).then_inc(gn_s, 1)
                if c + 1 < NT:
                    gate(c + 1)
                if c:
                    act.wait_ge(gn_s, b + 5)
                    act.activation(c_rt[:], ps[3][:], ACT.Sqrt, bias=eps_col(LN_EPS)).then_inc(gn_s, 1)
                    act.wait_ge(gn_s, b + 7)
                    x = c - 1
                    link(act, "act", act.activation(c_v[:], cacc[x % 2][:], ACT.Identity,
                                                    scale=cols2[:, G_GNG + x:G_GNG + x + 1],
                                                    bias=cols2[:, G_GNB + x:G_GNB + x + 1]))
                    act.activation(c_s[:], c_v[:], ACT.Sigmoid).then_inc(gn_v, 1)
                if c + 1 < NT:
                    zgate(c + 1)
            tiles["act"] += 24

        gn_v = sem("gn_v")

        def pe_conv(pe):
            n0, g0 = CHUNK0["conv"], tiles["pe"]

            def product(c, o):
                n, g = n0 + 3 * c + o, g0 + 3 * c + o
                s, t = n % 2, ps[g % 2]
                pe.wait_ge(w_split, n + 1)
                pe.wait_ge(evac_act, g + 1)
                pe.wait_ge(evac_dve, g + 1)
                for k in range(NT):
                    for h in range(2):
                        mm = mm3(pe, t[:, h * HALF:(h + 1) * HALF], w_hi[s][:, k * P:(k + 1) * P],
                                 w_lo[s][:, k * P:(k + 1) * P], H_hi[:, k, h * HALF:(h + 1) * HALF],
                                 H_lo[:, k, h * HALF:(h + 1) * HALF], k == 0, k == NT - 1, opens=k == 0 and h == 0)
                mm.then_inc(out_ready, 1)

            def mean(c, src, x, at):
                pe.wait_ge(gn_s, 7 * c + at)
                for h in range(2):
                    mm = pe.matmul(ps[2 + x][:, h * HALF:(h + 1) * HALF], ones_c[:], src[:, h * HALF:(h + 1) * HALF],
                                   start=True, stop=True)
                mm.then_inc(gn_s, 1)
            for o in range(3):
                product(0, o)
            for c in range(NT + 1):
                if c:
                    mean(c - 1, cacc[(c - 1) % 2], 0, 1)
                if c + 1 < NT:
                    product(c + 1, 0)
                if c:
                    mean(c - 1, c_sq, 1, 4)
                if c + 1 < NT:
                    product(c + 1, 1)
                    product(c + 1, 2)
            tiles["pe"] += 24

        def dve_conv(v):
            g0 = tiles["dve"]
            link(v, "dve", v.memset(Uc[:], 0.0))
            v.sem_inc(evac_dve, 1)

            def centre(c):
                v.wait_ge(gn_s, 7 * c + 2)
                v.tensor_tensor(cacc[c % 2][:], cacc[c % 2][:], ps[2][:], ALU.subtract).then_inc(gn_s, 1)

            def scale(c):
                v.wait_ge(gn_s, 7 * c + 6)
                link(v, "dve", v.reciprocal(c_rs[:], c_rt[:]))
                v.tensor_tensor(cacc[c % 2][:], cacc[c % 2][:], c_rs[:], ALU.mult).then_inc(gn_s, 1)

            def leave(c):
                v.wait_ge(gn_v, c + 1)
                link(v, "dve", v.tensor_tensor(ya[:, c], c_v[:], c_s[:], ALU.mult))
                v.tensor_tensor(ya[:, c], ya[:, c], c_zs[c % 2][:], ALU.mult)
            between = {4: centre, 18: scale, 26: leave}
            for c in range(NT):
                g = g0 + 3 * c
                v.wait_ge(evac_act, g + 3)
                v.wait_ge(out_ready, g + 2)
                if c:
                    v.wait_ge(gn_s, 7 * c - 6)
                v.tensor_tensor(Uc[:, 15:15 + S], ps[(g + 1) % 2][:], c_sg[:], ALU.mult).then_inc(evac_dve, 1)
                v.wait_ge(evac_act, g + 5)
                v.tensor_tensor(c_zs[c % 2][:], ps[(g + 2) % 2][:], c_sz[:], ALU.mult).then_inc(evac_dve, 1)
                v.wait_ge(evac_dve, g + 5)
                v.sem_inc(conv_in, 1)
                if c < NT - 1:
                    v.sem_inc(evac_dve, 1)
                acc = cacc[c % 2]
                ins = v.tensor_scalar(acc[:], Uc[:, 0:S], conv_w[:, c, 0:1], cols2[:, G_CB + c:G_CB + c + 1],
                                      ALU.mult, ALU.add)
                for k in range(1, CONV_K):
                    link(v, "dve", ins)
                    if c and k in between:
                        between[k](c - 1)
                    ins = v.scalar_tensor_tensor(out=acc[:], in0=Uc[:, k:k + S], scalar=conv_w[:, c, k:k + 1],
                                                 in1=acc[:], op0=ALU.mult, op1=ALU.add)
                ins.then_inc(gn_s, 1)
            for step in (centre, scale, leave):
                step(NT - 1)
            tiles["dve"] += 24

        split_a = Split("split_a", ya, NT, Z_hi, Z_lo)

        def dve_add(v, n):
            def one(j, t):
                v.tensor_tensor(ACC[:, j], ACC[:, j], t[:], ALU.add).then_inc(evac_dve, 1)
            each_tile(v, "dve", n, one)

        xk = sb("xk", V + 24, [P, NT, S])
        norm_ep = Norm("norm_ep", ACC, NT, ones_d, cols2[:, G_EPOST:G_EPOST + 8], into=ACC)
        norm_o = Norm("norm_o", ACC, NT, ones_d, cols2[:, G_OPRE:G_OPRE + 8], hi=H_hi, lo=H_lo)
        back = sem("back")
        back_n = {"act": 0, "dve": 0}

        def act_back(act, src):
            for k in range(NT):
                load(act, xk[:, k], src[k])
            act.wait_ge(aux, aux_n[0])
            act.drain().then_inc(back, 1)

        def dve_back(v):
            back_n["dve"] += 1
            v.wait_ge(back, back_n["dve"])
            for k in range(NT):
                v.tensor_tensor(ACC[:, k], ACC[:, k], xk[:, k], ALU.add)

        class Silu:

            def __init__(self, name, x, n, t):
                self.x, self.n, self.t = x, n, t
                self.sig, self.used = sem(f"{name}_sig"), sem(f"{name}_used")

            def act(self, act):
                for k in range(self.n):
                    if k >= 2:
                        act.wait_ge(self.used, k - 1)
                    act.activation(self.t[:, k % 2], self.x[:, k], ACT.Sigmoid).then_inc(self.sig, 1)

            def dve(self, v):
                for k in range(self.n):
                    v.wait_ge(self.sig, k + 1)
                    v.tensor_tensor(self.x[:, k], self.x[:, k], self.t[:, k % 2], ALU.mult).then_inc(self.used, 1)

        L6 = sb("L6", V, [P, 6, S])
        FZ = sb("FZ", V + 53, [P, 8, S])
        o_sq = sb("o_sq", V + 24, [P, 2, S])
        o_t = sb("o_t", V + 32, [P, 2, S])
        o_rs = sb("o_rs", V + 40, [P, S])
        o_rt = sb("o_rt", V + 44, [P, S])
        ones_q = sb("ones_q", V + 48, [P, P])
        ones_kv = sb("ones_kv", V + 48.5, [P, P])
        CQ_hi = sb("CQ_hi", 0, [P, 3, S], F32R)
        CQ_lo = sb("CQ_lo", 12, [P, 3, S], F32R)
        CK_hi = sb("CK_hi", 24, [P, 2, S], F32R)
        CK_lo = sb("CK_lo", 32, [P, 2, S], F32R)
        cos2 = sb("cos2", 40, [P, S])
        sin2 = sb("sin2", 44, [P, S])
        KR = sb("KR", 48, [P, S])
        QN = sb("QN", 52, [P, S])
        QR = sb("QR", 56, [P, S])
        KN = sb("KN", 60, [P, S])
        rp_i = sb("rp_i", V + 24, [P, S], I32)
        rp_a = sb("rp_a", V + 28, [P, S])
        rp_k = sb("rp_k", V + 32, [P, S])
        rp_r = sb("rp_r", V + 36, [P, S])
        rot = sb("rot", V + 52, [P, P])
        VT = sb("VT", V, [P, S])
        VN = sb("VN", V + 4, [P, NT, P])
        mT3 = sb("mT3", V + 8, [P, 3, S])
        mPT = sb("mPT", V + 20, [P, 2, S])
        rt1 = sb("rt1", V + 28, [P, S])
        rt2 = sb("rt2", V + 32, [P, S])
        mst = sb("mst", V + 36, [P, 3, 8])

        silu_c = Silu("silu_c", ACC, 8, o_sq)
        norm_q = Norm("norm_q", L6, 3, ones_q, cols2[:, G_Q:G_Q + 3], hi=CQ_hi, lo=CQ_lo, sq=o_sq, t=o_t, rs=o_rs, rt=o_rt)
        norm_kv = Norm("norm_kv", L6[:, 3:5], 2, ones_kv, cols2[:, G_KV:G_KV + 2], hi=CK_hi, lo=CK_lo, sq=o_sq, t=o_t,
                       rs=o_rs, rt=o_rt)
        norm_op = Norm("norm_op", ACC, NT, ones_d, cols2[:, G_OPOST:G_OPOST + 8], into=ACC)
        rope = sem("rope")
        TWO_PI_1, TWO_PI_2 = 6.28125, 1014.0 / 2 ** 19
        TWO_PI_3 = 2 * np.pi - TWO_PI_1 - TWO_PI_2
        ROUND = 1.5 * 2 ** 23
        PI = 3.1415925

        def act_rope(act):
            load(act, rp_i[:], io["positions_2"].to_broadcast([P, S]))
            load(act, rot[:], io["consts"][CI["rot"]])
            act.wait_ge(aux, aux_n[0])
            act.drain().then_inc(rope, 1)
            for x, dst in enumerate((sin2, cos2)):
                act.wait_ge(rope, 2 * x + 2)
                act.activation(dst[:], rp_r[:], ACT.Sin).then_inc(rope, 1)

        def dve_rope(v):
            v.wait_ge(rope, 1)
            link(v, "dve", v.tensor_copy(rp_k[:], rp_i[:]))
            link(v, "dve", v.tensor_scalar(rp_a[:], rp_k[:], cols2[:, G_INV:G_INV + 1], None, ALU.mult))
            for x in range(2):
                if x:
                    v.wait_ge(rope, 3)
                link(v, "dve", v.tensor_scalar(rp_k[:], rp_a[:], 1 / (2 * np.pi), 0.25 * x, ALU.mult, ALU.add))
                link(v, "dve", v.tensor_scalar(rp_k[:], rp_k[:], ROUND, None, ALU.add))
                link(v, "dve", v.tensor_scalar(rp_k[:], rp_k[:], ROUND, None, ALU.subtract))
                link(v, "dve", v.scalar_tensor_tensor(out=rp_r[:], in0=rp_k[:], scalar=-TWO_PI_1, in1=rp_a[:],
                                                      op0=ALU.mult, op1=ALU.add))
                for c in (TWO_PI_2, TWO_PI_3):
                    link(v, "dve", v.scalar_tensor_tensor(out=rp_r[:], in0=rp_k[:], scalar=-c, in1=rp_r[:],
                                                          op0=ALU.mult, op1=ALU.add))
                if x:
                    link(v, "dve", v.tensor_scalar(rp_r[:], rp_r[:], np.pi / 2, None, ALU.add))
                v.tensor_scalar(rp_r[:], rp_r[:], PI, -PI, ALU.min, ALU.max).then_inc(rope, 1)
            v.wait_ge(rope, 6)
            r = slice(0, ROPE)
            v.tensor_tensor(KR[r], L6[r, 5], cos2[r], ALU.mult)
            link(v, "dve", v.tensor_tensor(rp_k[r], ps[2][r], sin2[r], ALU.mult))
            v.tensor_tensor(KR[r], KR[r], rp_k[r], ALU.add)

        def pe_rope(pe):
            pe.wait_ge(rope, 5)
            for h in range(2):
                mm = pe.matmul(ps[2][0:ROPE, h * HALF:(h + 1) * HALF], rot[0:ROPE, 0:ROPE],
                               L6[0:ROPE, 5, h * HALF:(h + 1) * HALF], start=True, stop=True)
            mm.then_inc(rope, 1)

        def unitsM(dst):
            return [dict(scale=192.0 ** -0.5, first=True, last=True, start=True, stop=True, L=S, rel=None,
                         qk=[(QN[:, it * P:(it + 1) * P], KN), (QR[0:ROPE, it * P:(it + 1) * P], KR[0:ROPE, :])],
                         v=[VN[:, t] for t in range(NT)], it=it,
                         o=lambda g: ps[3][:, g % 2 * HALF:g % 2 * HALF + P]) for it in range(NT)]

        mla_head = [None]

        def mla_fin(v, g, u):
            z = ACC[:, mla_head[0], u["it"] * P:(u["it"] + 1) * P]
            return v.tensor_tensor(z, ps[3][:, g % 2 * HALF:g % 2 * HALF + P], z, ALU.mult)

        softM = Soft("mla", unitsM(None), mT3, mPT, mst, mla_fin)
        m_pre, m_vn, m_qr = sem("m_pre"), sem("m_vn"), sem("m_qr")

        def pe_mla(pe):
            n0, g0 = CHUNK0["mla"], tiles["pe"]
            with pe.Fori(0, H_C) as i:
                for o, (ch, b0, kt, hi, lo) in enumerate(((0, 0, 3, CQ_hi, CQ_lo), (0, 3, 3, CQ_hi, CQ_lo),
                                                          (0, 6, 2, CK_hi, CK_lo), (1, 0, 2, CK_hi, CK_lo))):
                    s = (n0 + ch) % 2
                    if b0 == 0:
                        pe.wait_ge(w_split, 2 * i + (n0 + ch + 1))
                    pe.wait_ge(evac_act, 4 * i + (g0 + o + 1))
                    pe.wait_ge(evac_dve, 4 * i + (g0 + o + 1))
                    for k in range(kt):
                        b = (b0 + k) * P
                        for h in range(2):
                            mm = mm3(pe, ps[(g0 + o) % 2][:, h * HALF:(h + 1) * HALF], w_hi[s][:, b:b + P],
                                     w_lo[s][:, b:b + P], hi[:, k, h * HALF:(h + 1) * HALF],
                                     lo[:, k, h * HALF:(h + 1) * HALF], k == 0, k == kt - 1,
                                     opens=b0 == 0 and k == 0 and h == 0)
                    mm.then_inc(out_ready, 1)
                pe.wait_ge(evac_act, 4 * i + (g0 + 6))
                pe.wait_ge(evac_dve, 4 * i + (g0 + 6))
                for t in range(NT):
                    pe.transpose(ps[3][:, t * P:(t + 1) * P], VT[:, t * P:(t + 1) * P], ident[:])
                for h in range(2):
                    mm = pe.matmul(ps[2][0:ROPE, h * HALF:(h + 1) * HALF], rot[0:ROPE, 0:ROPE],
                                   QR[0:ROPE, h * HALF:(h + 1) * HALF], start=True, stop=True)
                mm.then_inc(m_pre, 1)
                pe.wait_ge(m_vn, i + 1)
                pe.wait_ge(m_qr, i + 1)
                softM.pe(pe, 8 * i, 8 * i)
                pe.wait_ge(softM.o_out, 8 * i + 8)
            tiles["pe"] += 4 * H_C

        def evac_mla(eng, which, i, g0):
            for o, dst in enumerate((QN, QR, KN, VT)):
                eng.wait_ge(out_ready, 4 * i + (g0 + o + 1))
                t = ps[(g0 + o) % 2]
                if which == "act":
                    eng.activation(dst[:, 0:HALF], t[:, 0:HALF], ACT.Copy).then_inc(evac_act, 1)
                else:
                    eng.tensor_copy(dst[:, HALF:S], t[:, HALF:S]).then_inc(evac_dve, 1)

        def act_mla(act):
            g0 = tiles["act"]
            with act.Fori(0, H_C) as i:
                evac_mla(act, "act", i, g0)
                act.wait_ge(m_pre, i + 1)
                act.activation(VN[:], ps[3][:].rearrange("p (t c) -> p t c", c=P), ACT.Copy).then_inc(m_vn, 1)
                softM.act(act, 8 * i)
            tiles["act"] += 4 * H_C

        def dve_mla(v):
            g0 = tiles["dve"]
            c = own["dve"]
            r = slice(0, ROPE)
            with v.Fori(0, H_C) as i:
                c.enter(i, 18)
                mla_head[0] = i
                evac_mla(v, "dve", i, g0)
                v.wait_ge(m_pre, i + 1)
                v.tensor_tensor(rt1[r], QR[r], cos2[r], ALU.mult)
                link(v, "dve", v.tensor_tensor(rt2[r], ps[2][r], sin2[r], ALU.mult))
                link(v, "dve", v.tensor_tensor(QR[r], rt1[r], rt2[r], ALU.add))
                v.sem_inc(m_qr, 1)
                softM.dve(v, 8 * i, 8 * i)
            c.leave(H_C)
            tiles["dve"] += 4 * H_C

        split_c = Split("split_c", ACC, NT, Z_hi, Z_lo)

        silu_d = Silu("silu_d", FZ[:, 4:8], 4, o_sq)
        UV_hi = sb("UV_hi", 0, [P, 16, HALF], F32R)
        UV_lo = sb("UV_lo", 32, [P, 16, HALF], F32R)
        dft_c = sb("dft_c", V + 48.5, [P, 2 * P])
        FRN = sb("FRN", V, [P, NT, HALF])
        FT_hi = sb("FT_hi", V + 16, [P, 4, S], F32R)
        FT_lo = sb("FT_lo", V + 32, [P, 4, S], F32R)
        YD_hi = sb("YD_hi", 0, [P, 4, S], F32R)
        YD_lo = sb("YD_lo", 16, [P, 4, S], F32R)
        fu, fu_hi, fu_lo, ft, ft_hi, ft_lo = (sem(x) for x in ("fu", "fu_hi", "fu_lo", "ft", "ft_hi", "ft_lo"))

        def pe_fft1(pe):
            for t in range(NT):
                if t >= 2:
                    pe.wait_ge(fu_lo, t - 1)
                for g in range(4):
                    mm = pe.matmul(ps[t % 2][:, g * 256:(g + 1) * 256], FZ[:, g, t * P:(t + 1) * P], dft_c[:],
                                   start=True, stop=True)
                mm.then_inc(fu, 1)

        def act_fft1(act):
            for t in range(NT):
                act.wait_ge(fu, t + 1)
                act.activation(uv(UV_hi, t), ps[t % 2][:].rearrange("p (g x c) -> p x g c", g=4, x=2),
                               ACT.Copy).then_inc(fu_hi, 1)

        def uv(x, t):
            return x[:].rearrange("p (x t) (g c) -> p t x g c", x=2, g=4)[:, t]

        def dve_fft1(v):
            for t in range(NT):
                v.wait_ge(fu_hi, t + 1)
                src = ps[t % 2][:].rearrange("p (g x c) -> p x g c", g=4, x=2)
                v.tensor_tensor(uv(UV_lo, t), src, uv(UV_hi, t).bitcast(F32), ALU.subtract).then_inc(fu_lo, 1)

        def pe_dft(pe):
            n0, g0 = CHUNK0["dft"], tiles["pe"]
            with pe.Fori(0, NT // 2) as i:
                for par in range(2):
                    t = ps[(g0 + par) % 2]
                    pe.wait_ge(evac_act, 2 * i + (g0 + par + 1))
                    pe.wait_ge(evac_dve, 2 * i + (g0 + par + 1))
                    for x in range(2):
                        s = (n0 + x) % 2
                        pe.wait_ge(w_split, 4 * i + (n0 + 2 * par + x + 1))
                        for k in range(NT):
                            mm = mm3(pe, t[:, 0:HALF], w_hi[s][:, k * P:(k + 1) * P], w_lo[s][:, k * P:(k + 1) * P],
                                     UV_hi[:, x * NT + k], UV_lo[:, x * NT + k], x == 0 and k == 0,
                                     x == 1 and k == NT - 1, opens=k == 0)
                    mm.then_inc(out_ready, 1)
            tiles["pe"] += NT

        def dve_dft(v):
            def one(j, t):
                v.tensor_copy(FRN[:, j], t[:, 0:HALF]).then_inc(evac_dve, 1)
            each_tile(v, "dve", NT, one)

        def pe_ft(pe):
            for g in range(4):
                if g >= 2:
                    pe.wait_ge(ft_lo, g - 1)
                for t in range(NT):
                    mm = pe.transpose(ps[g % 2][:, t * P:(t + 1) * P], FRN[:, t, g * P:(g + 1) * P], ident[:])
                mm.then_inc(ft, 1)

        def act_ft(act):
            for g in range(4):
                act.wait_ge(ft, g + 1)
                act.activation(FT_hi[:, g], ps[g % 2][:], ACT.Copy).then_inc(ft_hi, 1)

        def dve_ft(v):
            for g in range(4):
                v.wait_ge(ft_hi, g + 1)
                v.tensor_tensor(FT_lo[:, g], ps[g % 2][:], FT_hi[:, g].bitcast(F32), ALU.subtract).then_inc(ft_lo, 1)

        def dve_fd(v):
            def one(j, t):
                v.tensor_tensor(FZ[:, 4 + j], FZ[:, 4 + j], t[:], ALU.mult).then_inc(evac_dve, 1)
            each_tile(v, "dve", 4, one)

        split_d = Split("split_d", FZ[:, 4:8], 4, YD_hi, YD_lo)
        stored = sem("stored")


        @block.tensor
        def _(pe):
            pe.sem_inc(slot_free, 1)
            pe_mod(pe)
            end_phase(pe, "pe")
            norm1.pe(pe)
            end_phase(pe, "pe")
            for b in "ABCD":
                pe_gemm(pe, "proj" + b, PROJ[b], 8, H_hi, H_lo)
                end_phase(pe, "pe")
                if b == "A":
                    pe_prepA(pe)
                    end_phase(pe, "pe")
                    softA.pe(pe)
                elif b == "B":
                    pe_prepB(pe)
                    end_phase(pe, "pe")
                    softB.pe(pe)
                elif b == "C":
                    pe_prep_v(pe, prepC)
                    end_phase(pe, "pe")
                    pe_stick(pe)
                else:
                    pe_prep_v(pe, prepD)
                    end_phase(pe, "pe")
                    pe_ret(pe)
                end_phase(pe, "pe")
                end_phase(pe, "pe")
                pe_gemm(pe, "br" + b, 2, 2, Ya_hi, Ya_lo)
                end_phase(pe, "pe")
                pe_gemm(pe, "merge" + b, 8, 8, H_hi, H_lo)
                end_phase(pe, "pe")
            end_phase(pe, "pe")
            pe_gemm(pe, "out1", 8, 8, Y_hi, Y_lo)
            end_phase(pe, "pe")
            norm_f.pe(pe)
            end_phase(pe, "pe")
            norm_e.pe(pe)
            end_phase(pe, "pe")
            pe_gemm(pe, "gates", 1, 8, H_hi, H_lo)
            end_phase(pe, "pe")
            pe_gates(pe)
            end_phase(pe, "pe")
            for l in lstm:
                pe_gemm(pe, CHUNK0[f"lstm{l.h}"], 4, 8, H_hi, H_lo)
                end_phase(pe, "pe")
                l.pe_w(pe)
                end_phase(pe, "pe")
                l.pe(pe)
                end_phase(pe, "pe")
                pe_gemm(pe, CHUNK0[f"lstm{l.h}"] + 4, 4, 8, H_hi, H_lo)
                end_phase(pe, "pe")
                l.pe_f(pe)
                end_phase(pe, "pe")
            end_phase(pe, "pe")
            pe_gemm(pe, "out_b", 8, 8, Y_hi, Y_lo)
            end_phase(pe, "pe")
            pe_conv(pe)
            end_phase(pe, "pe")
            end_phase(pe, "pe")
            pe_gemm(pe, "out_a", 8, 8, Z_hi, Z_lo)
            end_phase(pe, "pe")
            norm_ep.pe(pe)
            end_phase(pe, "pe")
            end_phase(pe, "pe")
            norm_o.pe(pe)
            end_phase(pe, "pe")
            pe_gemm(pe, "zc", 8, 8, H_hi, H_lo)
            end_phase(pe, "pe")
            pe_gemm(pe, "lat", 6, 8, H_hi, H_lo)
            end_phase(pe, "pe")
            pe_gemm(pe, "fin", 8, 8, H_hi, H_lo)
            end_phase(pe, "pe")
            norm_q.pe(pe)
            end_phase(pe, "pe")
            norm_kv.pe(pe)
            end_phase(pe, "pe")
            pe_rope(pe)
            end_phase(pe, "pe")
            pe_mla(pe)
            end_phase(pe, "pe")
            end_phase(pe, "pe")
            pe_gemm(pe, "out_c", 8, 8, Z_hi, Z_lo)
            end_phase(pe, "pe")
            pe_fft1(pe)
            end_phase(pe, "pe")
            pe_dft(pe)
            end_phase(pe, "pe")
            pe_ft(pe)
            end_phase(pe, "pe")
            pe_gemm(pe, "fd", 2, 4, FT_hi, FT_lo)
            end_phase(pe, "pe")
            end_phase(pe, "pe")
            pe_gemm(pe, "out_d", 4, 4, YD_hi, YD_lo)
            end_phase(pe, "pe")
            norm_op.pe(pe)
            end_phase(pe, "pe")
            end_phase(pe, "pe")

        @block.scalar
        def _(act):
            act.sem_inc(evac_act, 2)
            act_mod(act)
            end_phase(act, "act")
            norm1.act(act)
            end_phase(act, "act")
            for b in "ABCD":
                copy_half(act, "act", PROJ[b], proj)
                end_phase(act, "act")
                if b == "A":
                    act_prepA(act)
                    end_phase(act, "act")
                    softA.act(act)
                elif b == "B":
                    act_prepB(act)
                    end_phase(act, "act")
                    softB.act(act)
                elif b == "C":
                    act_prepC(act)
                    end_phase(act, "act")
                    act_stick(act)
                else:
                    act_prepD(act)
                    end_phase(act, "act")
                    act_ret(act)
                end_phase(act, "act")
                ysplit[b].act(act)
                end_phase(act, "act")
                copy_half(act, "act", 8, R)
                end_phase(act, "act")
                act_merge(act)
                end_phase(act, "act")
            merged.act(act)
            end_phase(act, "act")
            act_out1(act)
            end_phase(act, "act")
            norm_f.act(act)
            end_phase(act, "act")
            norm_e.act(act)
            end_phase(act, "act")
            copy_half(act, "act", 1, gT2)
            end_phase(act, "act")
            act_gates(act)
            end_phase(act, "act")
            for l in lstm:
                copy_half(act, "act", 4, QKV)
                end_phase(act, "act")
                l.act_w(act)
                end_phase(act, "act")
                l.act(act)
                end_phase(act, "act")
                copy_half(act, "act", 4, OZ)
                end_phase(act, "act")
                l.act_f(act)
                end_phase(act, "act")
            split_b.act(act)
            end_phase(act, "act")
            copy_half(act, "act", 8, ACC)
            load(act, conv_w[:], io["conv_w"])
            load(act, ones_c[:], io["consts"][CI["ones_c"]])
            act.wait_ge(aux, aux_n[0])
            end_phase(act, "act")
            act_conv(act)
            end_phase(act, "act")
            split_a.act(act)
            end_phase(act, "act")
            act_gemm_none(act, 8)
            end_phase(act, "act")
            norm_ep.act(act)
            end_phase(act, "act")
            act_back(act, keep1)
            end_phase(act, "act")
            norm_o.act(act)
            keep(act, keep2)
            end_phase(act, "act")
            copy_half(act, "act", 8, ACC)
            end_phase(act, "act")
            silu_c.act(act)
            copy_half(act, "act", 6, L6)
            end_phase(act, "act")
            copy_half(act, "act", 8, FZ)
            load(act, ones_q[:], io["consts"][CI["ones_q"]])
            load(act, ones_kv[:], io["consts"][CI["ones_kv"]])
            act.wait_ge(aux, aux_n[0])
            end_phase(act, "act")
            norm_q.act(act)
            end_phase(act, "act")
            norm_kv.act(act)
            end_phase(act, "act")
            act_rope(act)
            end_phase(act, "act")
            act_mla(act)
            end_phase(act, "act")
            split_c.act(act)
            end_phase(act, "act")
            copy_half(act, "act", 8, ACC)
            load(act, dft_c[:], io["dft_c"])
            act.wait_ge(aux, aux_n[0])
            end_phase(act, "act")
            act_fft1(act)
            silu_d.act(act)
            end_phase(act, "act")
            act_gemm_none(act, 8)
            end_phase(act, "act")
            act_ft(act)
            end_phase(act, "act")
            act_gemm_none(act, 4)
            end_phase(act, "act")
            split_d.act(act)
            end_phase(act, "act")
            act_gemm_none(act, 8)
            end_phase(act, "act")
            norm_op.act(act)
            end_phase(act, "act")
            act_back(act, keep2)
            end_phase(act, "act")
            for k in range(NT):
                act.dma_start(out[k], ACC[:, k]).then_inc(stored, 16)
            act.wait_ge(stored, 16 * NT)

        @block.vector
        def _(v):
            v.sem_inc(evac_dve, 2)
            dve_mod(v)
            end_phase(v, "dve")
            norm1.dve(v)
            end_phase(v, "dve")
            for b in "ABCD":
                copy_half(v, "dve", PROJ[b], proj)
                end_phase(v, "dve")
                if b == "A":
                    dve_prepA(v)
                    end_phase(v, "dve")
                    dve_silu(v, 5)
                    v.drain()
                    softA.dve(v)
                elif b == "B":
                    end_phase(v, "dve")
                    dve_silu(v, 4)
                    v.drain()
                    softB.dve(v)
                elif b == "C":
                    end_phase(v, "dve")
                    dve_silu_cd(v, PT2)
                    v.drain()
                    dve_stick(v)
                else:
                    end_phase(v, "dve")
                    dve_silu_cd(v, zsig)
                    v.drain()
                    dve_ret(v)
                end_phase(v, "dve")
                ysplit[b].dve(v)
                end_phase(v, "dve")
                copy_half(v, "dve", 8, R)
                end_phase(v, "dve")
                dve_merge(v, b == "A")
                end_phase(v, "dve")
            merged.dve(v)
            end_phase(v, "dve")
            dve_out1(v)
            end_phase(v, "dve")
            norm_f.dve(v)
            end_phase(v, "dve")
            norm_e.dve(v)
            end_phase(v, "dve")
            copy_half(v, "dve", 1, gT2)
            end_phase(v, "dve")
            dve_gates(v)
            end_phase(v, "dve")
            for l in lstm:
                copy_half(v, "dve", 4, QKV)
                end_phase(v, "dve")
                l.dve_w(v)
                end_phase(v, "dve")
                l.dve(v)
                end_phase(v, "dve")
                copy_half(v, "dve", 4, OZ)
                end_phase(v, "dve")
                l.dve_f(v)
                end_phase(v, "dve")
            split_b.dve(v)
            end_phase(v, "dve")
            copy_half(v, "dve", 8, ACC)
            end_phase(v, "dve")
            dve_conv(v)
            end_phase(v, "dve")
            split_a.dve(v)
            end_phase(v, "dve")
            dve_add(v, 8)
            end_phase(v, "dve")
            norm_ep.dve(v)
            end_phase(v, "dve")
            dve_back(v)
            end_phase(v, "dve")
            norm_o.dve(v)
            end_phase(v, "dve")
            copy_half(v, "dve", 8, ACC)
            end_phase(v, "dve")
            silu_c.dve(v)
            copy_half(v, "dve", 6, L6)
            end_phase(v, "dve")
            copy_half(v, "dve", 8, FZ)
            end_phase(v, "dve")
            norm_q.dve(v)
            end_phase(v, "dve")
            norm_kv.dve(v)
            end_phase(v, "dve")
            dve_rope(v)
            end_phase(v, "dve")
            dve_mla(v)
            end_phase(v, "dve")
            split_c.dve(v)
            end_phase(v, "dve")
            copy_half(v, "dve", 8, ACC)
            end_phase(v, "dve")
            dve_fft1(v)
            silu_d.dve(v)
            end_phase(v, "dve")
            dve_dft(v)
            end_phase(v, "dve")
            dve_ft(v)
            end_phase(v, "dve")
            dve_fd(v)
            end_phase(v, "dve")
            split_d.dve(v)
            end_phase(v, "dve")
            dve_add(v, 8)
            end_phase(v, "dve")
            norm_op.dve(v)
            end_phase(v, "dve")
            dve_back(v)
            end_phase(v, "dve")


def _blocks(w):
    k, n = w.shape
    return w.reshape(k // P, P, n // P, P).transpose(2, 0, 1, 3).reshape(-1, P, P)


def _pad_cols(w, n):
    return np.concatenate([w, np.zeros((w.shape[0], n - w.shape[1]), w.dtype)], axis=1)


def _chunks(blocks):
    b = np.concatenate(blocks, axis=0)
    assert b.shape[0] % BLK == 0
    return b.reshape(-1, BLK, P, P).transpose(0, 2, 1, 3).reshape(-1, P, BLK * P)


def _dft():
    n = np.arange(S)
    a = 2 * np.pi * (np.outer(n, n) % S) / S
    m = np.arange(P)
    b = 2 * np.pi * (np.outer(m, m) % P) / P
    scale = 1.0 / np.sqrt(float(S * P))
    return (np.cos(a).astype(np.float32), np.sin(a).astype(np.float32),
            (np.cos(b) * scale).astype(np.float32), (-np.sin(b) * scale).astype(np.float32))


def _stream(i, dft_cos, dft_sin):
    w_in = i["w_in"][0]
    out = {}
    out["mod"] = _blocks(i["w_ada"][0])
    z = lambda a, b: w_in[:, a:b]
    a_kv = 256
    order = {
        "A": [z(0, 256), z(a_kv, a_kv + 128), z(a_kv + 128, a_kv + 256), z(a_kv + 256, a_kv + 384), z(652, 908),
              _pad_cols(z(640, 652), P)],
        "B": [z(908, 1676)], "C": [z(1676, 2700)], "D": [z(2700, 3724)],
    }
    for n, b in enumerate("ABCD"):
        out["proj" + b] = _blocks(np.concatenate(order[b], axis=1))
        out["br" + b] = _blocks(i["w_br"][0, n])
        out["merge" + b] = _blocks(i["w_merge"][0, n])
    out["out1"] = _blocks(i["w_out"][0])
    we = i["even_w_in_2"][0]
    out["gates"] = _blocks(_pad_cols(we[:, 7168:7184], P))
    for h in range(H_B):
        out[f"lstm{h}"] = _blocks(np.concatenate(
            [we[:, 3072 + 128 * h:3200 + 128 * h], we[:, 3584 + 128 * h:3712 + 128 * h],
             we[:, 4096 + 256 * h:4352 + 256 * h], we[:, 5120 + 256 * h:5376 + 256 * h],
             we[:, 6144 + 256 * h:6400 + 256 * h]], axis=1))
    wo = i["even_w_out_2"][0]
    out["out_b"] = _blocks(wo[1024:])
    out["conv"] = _blocks(np.concatenate(
        [we[:, g + 128 * c:g + 128 * c + 128] for c in range(8) for g in (1024, 0, 2048)], axis=1))
    out["out_a"] = _blocks(wo[:1024])
    wd = i["odd_w_in_2"][0]
    out["zc"] = _blocks(wd[:, 1216:2240])
    out["lat"] = _blocks(np.concatenate([wd[:, 0:640], _pad_cols(wd[:, 640:704], P)], axis=1))
    out["fin"] = _blocks(np.concatenate([wd[:, 704:1216], wd[:, 2240:2752]], axis=1))
    uq, ukv = i["odd_w_uq_2"][0], i["odd_w_ukv_2"][0]
    mla = []
    for h in range(H_C):
        q = uq[:, 192 * h:192 * h + 192]
        kv = ukv[:, 256 * h:256 * h + 256]
        mla += [_blocks(q[:, :128]), _blocks(_pad_cols(q[:, 128:], P)), _blocks(kv[:, :128]), _blocks(kv[:, 128:]),
                np.zeros((6, P, P), np.float32)]
    out["mla"] = np.concatenate(mla)
    wc = i["odd_w_out_2"][0]
    out["out_c"] = _blocks(wc[:1024])
    c, s = dft_cos.reshape(NT, P, NT, P), dft_sin.reshape(NT, P, NT, P)
    out["dft"] = np.stack([c, s]).transpose(3, 0, 1, 2, 4).reshape(-1, P, P)
    out["fd"] = _blocks(i["odd_w_fd_2"][0])
    out["out_d"] = _blocks(wc[1024:])
    for name, n in STREAM:
        assert out[name].shape[0] == n * BLK, (name, out[name].shape, n)
    pad = [np.zeros((BLK * (N_CHUNKS_PADDED - N_CHUNKS), P, P), np.float32)]
    return _chunks([out[name] for name, _ in STREAM] + pad)


def _consts():
    r, c = np.arange(P)[:, None], np.arange(P)[None, :]
    z = np.zeros((P, P))
    rot = z.copy()
    for k in range(32):
        rot[k + 32, k] = -1
        rot[k, k + 32] = 1
    m = {
        "ident": np.eye(P), "ones_d": z + 1.0 / D, "ones_c": z + 1.0 / P, "ones_h": (r // HD == c // HD) / HD,
        "ones": z + 1, "sum_neg": -1.0 * (r >= c), "neg": z - 1, "mask_lt": r < c, "neg_ge": NEG * (r >= c),
        "cum_f": r <= c, "cum_b": r >= c, "neg_f": NEG * (r > c), "neg_b": NEG * (r < c), "rot": rot, "ones_q": z + 1.0 / 384, "ones_kv": z + 1.0 / 256,
    }
    return np.stack([m[n].astype(np.float32) for n in CONST])


def _rel(width, window):
    d = np.arange(P)[:, None] + (width - P) - np.arange(width)[None, :]
    return np.where((d >= 0) & (d < window), d, -NEG).astype(np.float32)


def layout(i):
    i = {k: np.asarray(v) for k, v in i.items()}
    col = lambda v, n: np.ascontiguousarray(v.reshape(n, P).T)
    dc, ds_, cc, cs = _dft()
    t = np.arange(S).reshape(NT, P).T[:, :, None]
    dist = t - (32 * np.arange(32) + 31)[None, None, :]
    log_g = np.log(1.0 - 2.0 ** (-5.0 - np.arange(4)))
    u = np.arange(S)[None, None, :] - np.arange(P)[:, None, None]
    decay = np.where(u >= 0, np.exp(log_g[None, :, None] * np.maximum(u, 0)), 0.0)
    bd = lambda w: np.block([[w[0], np.zeros_like(w[0])], [np.zeros_like(w[1]), w[1]]])
    w1 = i["cmp_w1"][0].reshape(2, 32, HD, HD)
    f = {
        "x": i["x"][0].T.reshape(NT, P, S),
        "wstream": _stream(i, dc, ds_),
        "consts": _consts(),
        "c": col(i["c"][0], 8), "b_ada": col(i["b_ada"][0], 24), "norm_g": col(i["norm_g"][0], 8),
        "final_g": col(i["final_g"], 8), "even_g_pre_2": col(i["even_g_pre_2"][0], 8),
        "rel_sel": _rel(S, S), "rel_win": _rel(640, 512), "rel_swa": _rel(256, 128),
        "rel_cmp": np.where(dist >= 0, dist, -NEG).astype(np.float32),
        "cmp_pos": i["cmp_pos"][0].transpose(0, 2, 1).reshape(P, 32),
        "cmp_w1": np.stack([bd(w1[:, l]) for l in range(32)], axis=1),
        "cmp_w2": bd(i["cmp_w2"][0]),
        "sink": i["sink"][0:1],
        "decay": decay.astype(np.float32),
    }
    f.update(layout2(i, cc, cs, col))
    return {k: np.ascontiguousarray(v) for k, v in f.items()}


def layout2(i, cc, cs, col):
    inv = np.float32(10000.0) ** (-np.arange(0, ROPE, 2, dtype=np.float32) / np.float32(ROPE))
    one = np.zeros((P, 1), np.float32)
    bg = one.copy()
    bg[:16, 0] = i["even_b_gate_2"][0]
    parts = [col(i["even_g_post_2"][0], 8), col(i["odd_g_pre_2"][0], 8), col(i["odd_g_post_2"][0], 8),
             col(i["even_gn_g_2"][0], 8), col(i["even_gn_b_2"][0], 8), col(i["even_conv_b_2"][0], 8),
             col(i["even_hn_g_2"][0], 8), col(i["odd_g_q_2"][0], 3), col(i["odd_g_kv_2"][0], 2), bg,
             np.tile(inv, 4)[:, None]]
    g = np.concatenate(parts, axis=1)
    sel4 = np.zeros((4, 4, P), np.float32)
    for h in range(4):
        sel4[h, h] = -1
    w = i["even_conv_w_2"][0].T.reshape(NT, P, CONV_K).transpose(1, 0, 2)
    return {"gains": np.concatenate([g, np.zeros((P, 96 - g.shape[1]), np.float32)], axis=1).astype(np.float32),
            "sel4": sel4, "dft_c": np.concatenate([cc, cs], axis=1), "positions_2": i["positions_2"],
            "conv_w": np.concatenate([w, np.zeros((P, NT, 1), w.dtype)], axis=2)}


def kernel(**inputs):
    import concourse.bacc as _bacc
    from concourse.bass_utils import run_bass_kernel_spmd as _run

    nc = _bacc.Bacc("TRN2", target_bir_lowering=False, num_devices=1)
    arrays = {f"in_{n}": a for n, a in layout(inputs).items()}
    io = {n[3:]: nc.dram_tensor(n, a.shape, mybir.dt.from_np(a.dtype), kind="ExternalInput").ap()
          for n, a in arrays.items()}
    out = nc.dram_tensor("out", (NT, P, S), F32, kind="ExternalOutput").ap()
    build(nc, io, out)
    r = _run(nc, [arrays], core_ids=[0])
    return r.results[0]["out"].reshape(D, S).T.reshape(1, S, D)
```

```python
from contextlib import ExitStack

import numpy as np
import concourse.bass as bass
from concourse import mybir

P = 128
D = 1024
S = 1024
NT = S // P
HALF = 512
BLK = 8
HD = 64
NEG = -1e30
TINY = 1e-30
RMS_EPS = 1e-6
LN_EPS = 1e-5
SLOPES = [2.0 ** (-8.0 * (h + 1) / 4) for h in range(4)]
CONV_K = 31
H_B = 4
H_C = 8
ROPE = 64

F32 = mybir.dt.float32
F32R = mybir.dt.float32r
I32 = mybir.dt.int32
ALU = mybir.AluOpType
ACT = mybir.ActivationFunctionType
AX = mybir.AxisListType

PROJ = {"A": 8, "B": 6, "C": 8, "D": 8}
STREAM = []
for _b in "ABCD":
    STREAM += [("proj" + _b, PROJ[_b]), ("br" + _b, 2), ("merge" + _b, 8)]
STREAM += [("out1", 8), ("gates", 1)]
STREAM += [(f"lstm{h}", 8) for h in range(H_B)]
STREAM += [("out_b", 8), ("conv", 24), ("out_a", 8)]
STREAM += [("zc", 8), ("lat", 6), ("fin", 8), ("mla", 16), ("out_c", 8), ("dft", 8), ("fd", 2), ("out_d", 4)]
CHUNK0, _n = {}, 0
for _name, _c in STREAM:
    CHUNK0[_name] = _n
    _n += _c
N_CHUNKS = _n
N_CHUNKS_PADDED = N_CHUNKS + N_CHUNKS % 2

CONST = ["ident", "ones_d", "ones_c", "ones_h", "ones", "sum_neg", "neg", "mask_lt", "neg_ge",
         "cum_f", "cum_b", "neg_f", "neg_b", "rot", "ones_q", "ones_kv"]
CI = {n: i for i, n in enumerate(CONST)}


def build(nc, io, out):
    ctx = ExitStack()
    with ctx:
        base = (nc.sbuf_base + 63) // 64 * 64
        n_pairs = N_CHUNKS_PADDED // 2

        def sb(name, kb, shape, dt=F32):
            return nc.alloc_sbuf_tensor_at(name, shape, dt, offset=base + int(kb * 1024))

        def sem(name):
            return ctx.enter_context(nc.semaphore(name))

        H_hi = sb("H_hi", 0, [P, NT, S], F32R)
        H_lo = sb("H_lo", 32, [P, NT, S], F32R)
        w_raw = [sb(f"w_raw{s}", 64 + 4 * s, [P, BLK * P]) for s in range(2)]
        w_hi = [sb(f"w_hi{s}", 72 + 4 * s, [P, BLK * P], F32R) for s in range(2)]
        w_lo = [sb(f"w_lo{s}", 80 + 4 * s, [P, BLK * P], F32R) for s in range(2)]
        ACC = sb("ACC", 88, [P, NT, S])
        cols = sb("cols", 120, [P, 120])
        zero = sb("zero", 120.46875, [P, 1])
        ident = sb("ident", 120.5, [P, P])
        ones_d = sb("ones_d", 121, [P, P])
        cols2 = sb("cols2", 121.5, [P, 96])
        V = 122
        Y_hi = sb("Y_hi", V, [P, NT, S], F32R)
        Y_lo = sb("Y_lo", V + 32, [P, NT, S], F32R)
        proj = sb("proj", V, [P, NT, S])
        Ya_hi = sb("Ya_hi", V + 32, [P, 2, S], F32R)
        Ya_lo = sb("Ya_lo", V + 40, [P, 2, S], F32R)
        X = V + 48
        n_sq = sb("n_sq", V + 64, [P, 2, S])
        n_t = sb("n_t", V + 8, [P, 2, S])
        n_rt = sb("n_rt", V + 72, [P, S])
        n_rs = sb("n_rs", V + 76, [P, S])

        ps = [nc.alloc_psum_tensor(f"ps{i}", [P, 2 * HALF], F32) for i in range(4)]

        w_loaded = [sem(f"w_loaded{s}") for s in range(2)]
        w_copied = sem("w_copied")
        w_split = sem("w_split")
        slot_free = sem("slot_free")
        out_ready = sem("out_ready")
        evac_act = sem("evac_act")
        evac_dve = sem("evac_dve")
        phase_end = sem("phase_end")
        zero_set = sem("zero_set")
        aux = sem("aux")
        act_own = sem("act_own")
        dve_own = sem("dve_own")

        block = ctx.enter_context(nc.Block())

        @block.sync
        def _(sp):
            for s in range(2):
                sp.dma_start(w_raw[s][:], io["wstream"][s]).then_inc(w_loaded[s], 16)
            with sp.Fori(1, n_pairs) as i:
                for s in range(2):
                    sp.wait_ge(w_split, 2 * i + s - 1)
                    sp.dma_start(w_raw[s][:], io["wstream"][2 * i + s]).then_inc(w_loaded[s], 16)

        @block.gpsimd
        def _(pool):
            pool.memset(zero[:], 0.0).then_inc(zero_set, 1)
            pool.wait_ge(zero_set, 1)
            with pool.Fori(0, n_pairs) as i:
                for s in range(2):
                    pool.wait_ge(w_loaded[s], 16 * i + 16)
                    pool.wait_ge(slot_free, 2 * i + s + 1)
                    pool.tensor_tensor(w_hi[s][:], w_raw[s][:], zero[:].to_broadcast([P, BLK * P]),
                                       ALU.add).then_inc(w_copied, 1)
                    pool.wait_ge(w_copied, 2 * i + s + 1)
                    pool.tensor_tensor(w_lo[s][:], w_raw[s][:], w_hi[s][:].bitcast(F32),
                                       ALU.subtract).then_inc(w_split, 1)

        class Count:

            def __init__(self, s):
                self.s, self.n, self.var, self.base, self.step = s, 0, None, 0, 0

            def inc(self, ins, by=1):
                ins.then_inc(self.s, by)
                self.n += by
                return self.now()

            def now(self):
                if self.var is None:
                    return self.n
                return self.base + self.step * self.var + (self.n - self.base)

            def enter(self, var, step):
                self.var, self.base, self.step = var, self.n, step

            def leave(self, times):
                assert self.n - self.base == self.step, (self.n - self.base, self.step)
                self.n = self.base + self.step * times
                self.var = None

        own = {}

        def link(eng, which, ins):
            c = own[which]
            eng.wait_ge(c.s, c.inc(ins))

        own["act"] = Count(act_own)
        own["dve"] = Count(dve_own)
        ended = {"pe": 0, "act": 0, "dve": 0}

        def end_phase(eng, which):
            ended[which] += 1
            eng.drain().then_inc(phase_end, 1)
            eng.wait_ge(phase_end, 3 * ended[which])

        def pairs(eng, n, body):
            if n < 4:
                for j in range(n):
                    body(j, j % 2)
                return
            with eng.Fori(0, n // 2) as i:
                for s in range(2):
                    body(2 * i + s, s)
            if n % 2:
                body(n - 1, 0)

        tiles = {"pe": 0, "act": 0, "dve": 0}

        def mm3(pe, out, wh, wl, ah, al, first, last, opens=False):

            mm = pe.matmul(out, wh, ah, start=first, stop=False)
            if opens:
                mm.then_inc(slot_free, 1)
            pe.matmul(out, wh, al, start=False, stop=False)
            return pe.matmul(out, wl, ah, start=False, stop=last)

        def pe_gemm(pe, name, n, kt, hi, lo, k0=0, after=None):
            if after is not None and n > 1:
                pe_gemm(pe, name, 1, kt, hi, lo, k0, after)
                pe_gemm(pe, CHUNK0[name] + 1, n - 1, kt, hi, lo, k0)
                return
            n0, g0, per = CHUNK0[name] if isinstance(name, str) else name, tiles["pe"], BLK // kt

            def chunk(j, par):
                s = (n0 + par) % 2
                pe.wait_ge(w_split, n0 + 1 + j)
                for o in range(per):
                    t = ps[(g0 + per * par + o) % 2]
                    g = g0 + per * j + o
                    pe.wait_ge(evac_act, g + 1)
                    pe.wait_ge(evac_dve, g + 1)
                    for k in range(kt):
                        b = (o * kt + k) * P
                        if after is not None and o == 0:
                            pe.wait_ge(after.lo_done, after.at['lo_done'] + k + 1)
                        for h in range(2):
                            mm = mm3(pe, t[:, h * HALF:(h + 1) * HALF], w_hi[s][:, b:b + P], w_lo[s][:, b:b + P],
                                     hi[:, k0 + k, h * HALF:(h + 1) * HALF], lo[:, k0 + k, h * HALF:(h + 1) * HALF],
                                     k == 0, k == kt - 1, opens=o == 0 and k == 0 and h == 0)
                    mm.then_inc(out_ready, 1)
            pairs(pe, n, chunk)
            tiles["pe"] += n * per

        def each_tile(eng, which, n, body):
            g0 = tiles[which]

            def one(j, par):
                eng.wait_ge(out_ready, g0 + 1 + j)
                body(j, ps[(g0 + par) % 2])
            pairs(eng, n, one)
            tiles[which] += n

        def copy_half(eng, which, n, dst):
            def one(j, t):
                if which == "act":
                    eng.activation(dst[:, j, 0:HALF], t[:, 0:HALF], ACT.Copy).then_inc(evac_act, 1)
                else:
                    eng.tensor_copy(dst[:, j, HALF:S], t[:, HALF:S]).then_inc(evac_dve, 1)
            each_tile(eng, which, n, one)

        shared_sems, counts = {}, {}

        def shared(name):
            if name not in shared_sems:
                shared_sems[name] = sem(name)
            return shared_sems[name]

        def since(kind, **adds):
            before = {x: counts.get((kind, x), 0) for x in adds}
            for x, n in adds.items():
                counts[kind, x] = before[x] + n
            return before

        class Norm:

            def __init__(self, name, src, n, ones, gcol, eps=RMS_EPS, shift=None, hi=None, lo=None, into=None,
                         sq=n_sq, t=n_t, rt=n_rt, rs=n_rs):
                self.name, self.src, self.n, self.ones, self.gcol, self.eps, self.shift = (
                    name, src, n, ones, gcol, eps, shift)
                self.hi, self.lo, self.into, self.sq, self.t, self.rt, self.rs = hi, lo, into, sq, t, rt, rs
                self.added, self.squared, self.summed, self.rooted, self.scaled, self.hi_done, self.lo_done = (
                    shared(f"norm_{x}") for x in ("added", "squared", "summed", "rooted", "scaled", "hi", "lo"))
                split = n if hi is not None else 0
                self.at = since("norm", added=n + 2, squared=n, summed=1, rooted=1, scaled=split, hi_done=split,
                                lo_done=split)

            def start(self, v):
                v.memset(self.rt[:], 0.0).then_inc(self.added, 2)

            def square(self, act, k, par):
                act.wait_ge(self.added, self.at['added'] + 1 + k)
                act.activation(self.sq[:, par], self.src[:, k], ACT.Square).then_inc(self.squared, 1)

            def add(self, v, k, par):
                v.wait_ge(self.squared, self.at['squared'] + 1 + k)
                v.wait_ge(self.added, self.at['added'] + 2 + k)
                v.tensor_tensor(self.rt[:], self.rt[:], self.sq[:, par], ALU.add).then_inc(self.added, 1)

            def pe_sum(self, pe):
                pe.sem_inc(self.added, 2)
                for k in range(self.n):
                    pe.wait_ge(self.squared, self.at['squared'] + k + 1)
                    for h in range(2):
                        mm = pe.matmul(ps[2][:, h * HALF:(h + 1) * HALF], self.ones[:],
                                       self.sq[:, k % 2, h * HALF:(h + 1) * HALF], start=k == 0, stop=k == self.n - 1)
                    mm.then_inc(self.added, 1)
                pe.wait_ge(self.added, self.at['added'] + self.n + 2)
                pe.sem_inc(self.summed, 1)

            def pe(self, pe):
                pe.wait_ge(self.added, self.at['added'] + self.n + 2)
                for h in range(2):
                    mm = pe.matmul(ps[2][:, h * HALF:(h + 1) * HALF], self.ones[:],
                                   self.rt[:, h * HALF:(h + 1) * HALF], start=True, stop=True)
                mm.then_inc(self.summed, 1)

            def root(self, act):
                act.wait_ge(self.summed, self.at['summed'] + 1)
                act.activation(self.rt[:], ps[2][:], ACT.Sqrt, bias=eps_col(self.eps)).then_inc(self.rooted, 1)

            def invert(self, v):
                v.wait_ge(self.rooted, self.at['rooted'] + 1)
                link(v, "dve", v.reciprocal(self.rs[:], self.rt[:]))

            def split_act(self, act):
                for k in range(self.n):
                    act.wait_ge(self.scaled, self.at['scaled'] + k + 1)
                    t = self.t[:, k % 2]
                    if self.shift is not None:
                        link(act, "act", act.activation(t, t, ACT.Identity, bias=self.shift[:, k:k + 1]))
                    act.activation(self.hi[:, k], t, ACT.Copy).then_inc(self.hi_done, 1)

            def scale(self, v, k):
                dst = self.into[:, k] if self.hi is None else self.t[:, k % 2]
                return v.scalar_tensor_tensor(out=dst, in0=self.src[:, k], scalar=self.gcol[:, k:k + 1],
                                              in1=self.rs[:], op0=ALU.mult, op1=ALU.mult)

            def split_dve(self, v):
                def low(k):
                    v.wait_ge(self.hi_done, self.at['hi_done'] + k + 1)
                    v.tensor_tensor(self.lo[:, k], self.t[:, k % 2], self.hi[:, k].bitcast(F32),
                                    ALU.subtract).then_inc(self.lo_done, 1)
                for k in range(self.n):
                    if k >= 2:
                        low(k - 2)
                        v.wait_ge(self.lo_done, self.at['lo_done'] + k - 1)
                    self.scale(v, k).then_inc(self.scaled, 1)
                low(self.n - 2)
                low(self.n - 1)

            def act(self, act):
                for k in range(self.n):
                    self.square(act, k, k % 2)
                self.root(act)
                self.split_act(act)

            def dve_stats(self, v):
                self.start(v)
                for k in range(self.n):
                    self.add(v, k, k % 2)

            def dve(self, v):
                self.dve_stats(v)
                self.invert(v)
                self.split_dve(v)

        class Chain:

            def __init__(self, first, second, keep_to, back=None):
                self.first, self.second, self.keep_to, self.back = first, second, keep_to, back
                self.ready = shared("chain_ready")
                self.at = since("chain", ready=NT)["ready"]

            def pe(self, pe):
                self.first.pe(pe)
                if self.second is not None:
                    self.second.pe_sum(pe)

            def act(self, act):
                self.first.root(act)
                for k in range(NT):
                    act.wait_ge(self.ready, self.at + k + 1)
                    act.dma_start(self.keep_to[k], ACC[:, k]).then_inc(kept, 16)
                    kept_n[0] += 16
                    if self.second is not None:
                        self.second.square(act, k, k % 2)
                if self.second is not None:
                    self.second.root(act)
                    self.second.split_act(act)

            def dve(self, v):
                self.first.invert(v)
                if self.back is not None:
                    v.wait_ge(aux, back_at[self.back])
                for k in range(NT):
                    ins = self.first.scale(v, k)
                    if self.back is not None:
                        link(v, "dve", ins)
                        ins = v.tensor_tensor(ACC[:, k], ACC[:, k], xk[:, k], ALU.add)
                    ins.then_inc(self.ready, 1)
                if self.second is not None:
                    self.second.invert(v)
                    self.second.split_dve(v)

        kept = sem("kept")
        kept_n = [0]
        keep1 = nc.dram_tensor("keep1", (NT, P, S), F32).ap()
        keep2 = nc.dram_tensor("keep2", (NT, P, S), F32).ap()
        xk = sb("xk", V + 24, [P, NT, S])
        back_at = {}

        def act_squares(act, norm):
            g0 = tiles["act"]

            def one(j, t):
                act.sem_inc(evac_act, 1)
                act.wait_ge(evac_dve, g0 + 3 + j)
                norm.square(act, j, 0 if t is ps[0] else 1)
            each_tile(act, "act", 8, one)

        class Split:

            def __init__(self, name, src, n, hi, lo):
                self.src, self.n, self.hi, self.lo = src, n, hi, lo
                self.hi_done, self.lo_done = shared("split_hi"), shared("split_lo")
                self.at = since("split", hi_done=n, lo_done=n)

            def act(self, act):
                for k in range(self.n):
                    act.activation(self.hi[:, k], self.src[:, k], ACT.Copy).then_inc(self.hi_done, 1)

            def dve(self, v):
                for k in range(self.n):
                    v.wait_ge(self.hi_done, self.at['hi_done'] + k + 1)
                    v.tensor_tensor(self.lo[:, k], self.src[:, k], self.hi[:, k].bitcast(F32),
                                    ALU.subtract).then_inc(self.lo_done, 1)

        eps_cols = {RMS_EPS: 0, LN_EPS: 1}

        def eps_col(e):
            return cols[:, eps_cols[e]:eps_cols[e] + 1]

        C_NG, C_FG, C_MOD, C_GS, C_EG, C_CT = 4, 12, 20, 44, 52, 60
        aux_n = [0]

        def load(act, dst, src):
            act.dma_start(dst, src).then_inc(aux, 16)
            aux_n[0] += 16

        norm1 = Norm("norm1", ACC, NT, ones_d, cols[:, C_GS:C_GS + 8], shift=cols[:, C_MOD:C_MOD + 8], hi=H_hi, lo=H_lo)

        w_ada = [sb("w_ada0", 0, [P, 16, D]), sb("w_ada1", V + 32, [P, 8, D])]
        c_sig = sb("c_sig", V + 82.25, [P, NT])
        c_sil = sb("c_sil", V + 82.5, [P, NT])
        b_ada = sb("b_ada", V + 82.75, [P, 24])
        ada_loaded = [sem(f"ada_loaded{i}") for i in range(6)]
        sem_c = sem("sem_c")
        sem_mod = sem("sem_mod")
        eps_set = sem("eps_set")

        def act_mod(act):
            load(act, cols[:, C_NG:C_NG + 8], io["norm_g"])
            load(act, cols[:, C_FG:C_FG + 8], io["final_g"])
            load(act, cols[:, C_EG:C_EG + 8], io["even_g_pre_2"])
            load(act, cols[:, C_CT:C_CT + 8], io["c"])
            load(act, b_ada[:], io["b_ada"])
            load(act, cols2[:], io["gains"])
            load(act, ident[:], io["consts"][CI["ident"]])
            load(act, ones_d[:], io["consts"][CI["ones_d"]])
            for k in range(NT):
                load(act, ACC[:, k], io["x"][k])
            for j in range(24):
                act.dma_start(w_ada[j // 16][:, j % 16], io["w_ada"][j]).then_inc(ada_loaded[j // 4], 16)
            act.wait_ge(aux, aux_n[0])
            act.wait_ge(eps_set, 2)
            act.activation(c_sig[:], cols[:, C_CT:C_CT + 8], ACT.Sigmoid).then_inc(sem_c, 1)

        def dve_mod(v):
            v.memset(cols[:, 0:1], RMS_EPS).then_inc(eps_set, 1)
            v.memset(cols[:, 1:2], LN_EPS).then_inc(eps_set, 1)
            v.wait_ge(sem_c, 1)
            v.tensor_tensor(c_sil[:], c_sig[:], cols[:, C_CT:C_CT + 8], ALU.mult).then_inc(sem_c, 1)
            norm1.dve_stats(v)
            v.wait_ge(sem_mod, 1)
            link(v, "dve", v.tensor_tensor(cols[:, C_MOD:C_MOD + 24],
                                           ps[3][:, 0:24], b_ada[:], ALU.add))
            link(v, "dve", v.scalar_tensor_tensor(out=cols[:, C_GS:C_GS + 8], in0=cols[:, C_MOD + 8:C_MOD + 16],
                                                  scalar=1.0, in1=cols[:, C_NG:C_NG + 8], op0=ALU.add, op1=ALU.mult))

        def pe_mod(pe):
            pe.wait_ge(sem_c, 2)
            for j in range(24):
                if j % 4 == 0:
                    pe.wait_ge(ada_loaded[j // 4], 64)
                for k in range(NT):
                    pe.matmul(ps[3][:, j:j + 1], w_ada[j // 16][:, j % 16, k * P:(k + 1) * P], c_sil[:, k:k + 1],
                              start=k == 0, stop=k == NT - 1)
            pe.drain().then_inc(sem_mod, 1)

        class Soft:

            def __init__(self, name, units, T, PT, st, finish=None, groups=0):
                self.units, self.T, self.PT, self.st, self.finish = units, T, PT, st, finish
                self.s_ready, self.max_done, self.exp_done, self.p_done, self.t_ready, self.pt_done, self.o_ready, \
                    self.o_out = (sem(f"{name}_{x}") for x in ("scores", "max", "exp", "p", "turned", "pt", "o", "oout"))
                self.groups = sum(u["last"] for u in units)

            def pe(self, pe, b=0, gb=0):
                U = self.units

                def scores(j):
                    u = U[j]
                    if j >= 2:
                        pe.wait_ge(self.exp_done if u["rel"] is None else self.max_done, b + j - 1)
                    t = ps[j % 2]
                    for h0 in range(0, u["L"], HALF):
                        h1 = min(u["L"], h0 + HALF)
                        n = len(u["qk"])
                        for x, (q, k) in enumerate(u["qk"]):
                            mm = pe.matmul(t[:, h0:h1], q, k[:, h0:h1], start=x == 0, stop=x == n - 1)
                    mm.then_inc(self.s_ready, 1)

                scores(0)
                if len(U) > 1:
                    scores(1)
                g = [0]

                def values(j):
                    u = U[j]
                    pe.wait_ge(self.pt_done, b + j + 1)
                    if u["first"] and g[0] >= 2:
                        pe.wait_ge(self.o_out, gb + g[0] - 1)
                    nb = len(u["v"])
                    for x, vv in enumerate(u["v"]):
                        kk = vv.shape[0]
                        mm = pe.matmul(u["o"](g[0]), vv, self.PT[0:kk, j % 2, x * P:(x + 1) * P],
                                       start=u["start"] and x == 0, stop=u["stop"] and x == nb - 1)
                    if u["last"]:
                        mm.then_inc(self.o_ready, 1)
                        g[0] += 1

                for j, u in enumerate(U):
                    if j + 2 < len(U):
                        scores(j + 2)
                    pe.wait_ge(self.p_done, b + j + 1)
                    if j >= 1:
                        pe.wait_ge(self.pt_done, b + j)
                    for x in range(len(u["v"])):
                        mm = pe.transpose(ps[2][:, x * P:(x + 1) * P], self.T[:, j % 3, x * P:(x + 1) * P], ident[:])
                    mm.then_inc(self.t_ready, 1)
                    if j >= 1:
                        values(j - 1)
                values(len(U) - 1)

            def act(self, act, b=0):
                U = self.units

                def exp(j):
                    u = U[j]
                    act.wait_ge(self.max_done, b + j + 1)
                    src = ps[j % 2] if u["rel"] is None else self.T[:, j % 3]
                    st = self.st[:, j % 3]
                    if u.get("sink") is not None:
                        act.activation(st[:, 3:4], u["sink"], ACT.Exp, bias=st[:, 0:1])
                    act.activation(self.T[:, j % 3, 0:u["L"]], src[:, 0:u["L"]], ACT.Exp, bias=st[:, 0:1],
                                   scale=u["scale"], accum_out=st[:, 1:2]).then_inc(self.exp_done, 1)
                exp(0)
                if len(U) > 1:
                    exp(1)
                for j, u in enumerate(U):
                    act.wait_ge(self.t_ready, b + j + 1)
                    w = len(u["v"]) * P
                    act.activation(self.PT[:, j % 2, 0:w], ps[2][:, 0:w], ACT.Copy).then_inc(self.pt_done, 1)
                    if j + 2 < len(U):
                        exp(j + 2)

            def dve(self, v, b=0, gb=0):
                U = self.units

                def top(j):
                    u = U[j]
                    L, st, T = u["L"], self.st[:, j % 3], self.T[:, j % 3]
                    v.wait_ge(self.s_ready, b + j + 1)
                    src = ps[j % 2]
                    if u["rel"] is not None:
                        link(v, "dve", v.scalar_tensor_tensor(
                            out=T[:, 0:L], in0=u["rel"], scalar=-u["slope"] / u["scale"], in1=src[:, 0:L],
                            op0=ALU.mult, op1=ALU.add))
                        src = T
                    link(v, "dve", v.reduce_max(st[:, 2:3], src[:, 0:L], AX.X))
                    if u.get("sink") is not None:
                        link(v, "dve", v.tensor_scalar(st[:, 2:3], st[:, 2:3], u["scale"], u["sink"], ALU.mult, ALU.max))
                        v.tensor_scalar(st[:, 0:1], st[:, 2:3], -1.0, None, ALU.mult).then_inc(self.max_done, 1)
                    elif u.get("clamp"):
                        v.tensor_scalar(st[:, 0:1], st[:, 2:3], -1e20, -u["scale"], ALU.max, ALU.mult).then_inc(
                            self.max_done, 1)
                    else:
                        v.tensor_scalar(st[:, 0:1], st[:, 2:3], -u["scale"], None, ALU.mult).then_inc(self.max_done, 1)

                def fin(g, u):
                    v.wait_ge(self.o_ready, gb + g + 1)
                    self.finish(v, g, u).then_inc(self.o_out, 1)

                top(0)
                if len(U) > 1:
                    top(1)
                g, late = 0, []
                for j, u in enumerate(U):
                    st, T = self.st[:, j % 3], self.T[:, j % 3]
                    v.wait_ge(self.exp_done, b + j + 1)
                    if u.get("sink") is not None:
                        link(v, "dve", v.tensor_tensor(st[:, 1:2], st[:, 1:2], st[:, 3:4], ALU.add))
                    if u.get("clamp"):
                        link(v, "dve", v.tensor_scalar(st[:, 1:2], st[:, 1:2], TINY, None, ALU.max))
                    link(v, "dve", v.reciprocal(st[:, 4:5], st[:, 1:2]))
                    if u.get("gate") is not None:
                        v.tensor_scalar(T[:, 0:u["L"]], T[:, 0:u["L"]], st[:, 4:5], u["gate"], ALU.mult,
                                        ALU.mult).then_inc(self.p_done, 1)
                    else:
                        v.tensor_scalar(T[:, 0:u["L"]], T[:, 0:u["L"]], st[:, 4:5], None, ALU.mult).then_inc(
                            self.p_done, 1)
                    if j + 2 < len(U):
                        top(j + 2)
                    if late and late[0][0] <= j - 2:
                        fin(*late.pop(0)[1:])
                    if u["last"]:
                        late.append((j, g, u))
                        g += 1
                for _, x, u in late:
                    fin(x, u)

        T3 = sb("T3", X, [P, 3, S])
        PT2 = sb("PT2", X + 12, [P, 2, S])
        st3 = sb("st3", X + 20, [P, 3, 8])
        rel_sel = sb("rel_sel", X + 20.125, [P, S])
        rel_win = sb("rel_win", X + 24.125, [P, 640])
        rel_cmp = sb("rel_cmp", X + 26.625, [P, NT, 32])
        v_sel = sb("v_sel", X + 27.625, [P, NT, HD])
        v_win = sb("v_win", X + 29.625, [P, NT, HD])
        gates = sb("gates", X + 31.625, [P, NT, 12])
        pos2 = sb("pos2", X + 32.125, [P, 32])
        kc2 = sb("kc2", X + 32.25, [P, 32])
        vc = sb("vc", X + 32.375, [P, P])
        w2bd = sb("w2bd", X + 32.875, [P, P])
        chid = sb("chid", X + 33.375, [P, 32])
        chid2 = sb("chid2", X + 33.5, [P, 32])
        w1bd = sb("w1bd", V + 32, [P, 32, P])
        prepA = sem("prepA")
        gT = proj[:, 7]

        def act_loadA(act):
            load(act, rel_sel[:], io["rel_sel"])
            load(act, rel_win[:], io["rel_win"])
            load(act, rel_cmp[:], io["rel_cmp"])
            load(act, pos2[:], io["cmp_pos"])
            load(act, w2bd[:], io["cmp_w2"])
            load(act, w1bd[:], io["cmp_w1"])

        def act_prepA(act):
            act.wait_ge(aux, aux_n[0])
            act.activation(gT, gT, ACT.Sigmoid).then_inc(prepA, 1)
            act.wait_ge(prepA, 3)
            act.activation(v_sel[:], ps[0][:].rearrange("p (t c) -> p t c", c=P)[:, :, HD:P], ACT.Copy)
            act.activation(proj[HD:P, 3], proj[0:HD, 3], ACT.Copy).then_inc(prepA, 1)
            act.wait_ge(prepA, 5)
            act.activation(v_win[:], ps[1][:].rearrange("p (t c) -> p t c", c=P)[:, :, HD:P], ACT.Copy)
            act.activation(proj[HD:P, 4], proj[0:HD, 4], ACT.Copy).then_inc(prepA, 1)
            act.wait_ge(prepA, 7)
            act.activation(chid[:], ps[2][:, 0:32], ACT.Sigmoid).then_inc(prepA, 1)
            act.wait_ge(prepA, 10)
            act.activation(vc[0:32, :], ps[2][0:32, 0:P], ACT.Copy)
            act.activation(kc2[0:HD, :], ps[3][0:HD, 0:32], ACT.Copy)
            act.activation(kc2[HD:P, :], ps[3][0:HD, 0:32], ACT.Copy).then_inc(prepA, 1)
            for z in (5, 6):
                act.activation(T3[:, z - 5], proj[:, z], ACT.Sigmoid)
            act.wait_ge(prepA, 12)

        def dve_prepA(v):
            v.wait_ge(prepA, 1)
            kv = proj[:, 2].rearrange("p (b l) -> p b l", l=32)
            v.tensor_tensor(kv, kv, pos2[:].unsqueeze(1).to_broadcast([P, 32, 32]), ALU.add).then_inc(prepA, 1)
            v.wait_ge(prepA, 8)
            v.tensor_tensor(chid2[:], chid[:], ps[2][:, 0:32], ALU.mult).then_inc(prepA, 1)
            v.wait_ge(prepA, 11)
            v.tensor_copy(gates[:], ps[0][:].rearrange("p (t c) -> p t c", c=P)[:, :, 0:12]).then_inc(prepA, 1)
            v.memset(T3[:, 2, 0:P], 0.0)

        def pe_prepA(pe):
            pe.wait_ge(prepA, 2)
            for t in range(NT):
                mm = pe.transpose(ps[0][:, t * P:(t + 1) * P], proj[:, 3, t * P:(t + 1) * P], ident[:])
            mm.then_inc(prepA, 1)
            pe.wait_ge(prepA, 4)
            for t in range(NT):
                mm = pe.transpose(ps[1][:, t * P:(t + 1) * P], proj[:, 4, t * P:(t + 1) * P], ident[:])
            mm.then_inc(prepA, 1)
            pe.wait_ge(prepA, 6)
            for l in range(32):
                mm = pe.matmul(ps[2][:, 0:32], w1bd[:, l], proj[:, 2].rearrange("p (b l) -> p l b", l=32)[:, l],
                               start=l == 0, stop=l == 31)
            mm.then_inc(prepA, 1)
            pe.wait_ge(prepA, 9)
            for t in range(NT):
                pe.transpose(ps[0][:, t * P:(t + 1) * P], gT[:, t * P:(t + 1) * P], ident[:])
            pe.matmul(ps[2][0:32, 0:P], chid2[:], w2bd[:], start=True, stop=True)
            pe.matmul(ps[3][:, 0:32], w2bd[:], chid2[:], start=True, stop=True).then_inc(prepA, 1)

        def rows(h):
            return slice(HD * (h % 2), HD * (h % 2) + HD)

        def unitsA():
            U = []
            for p in range(2):
                for it in range(NT):
                    for hh in range(2):
                        h, r = 2 * p + hh, rows(hh)
                        q = proj[r, p, it * P:(it + 1) * P]
                        w0 = max(0, it - 4)
                        for br in ("win", "sel", "cmp"):
                            u = dict(scale=HD ** -0.5, slope=SLOPES[h], first=hh == 0 and br == "win",
                                     last=hh == 1 and br == "cmp", start=br == "win", stop=br == "cmp",
                                     o=lambda g, r=r: ps[3][r, g % 2 * HALF:g % 2 * HALF + P], pair=p, it=it)
                            if br == "sel":
                                u.update(L=(it + 1) * P, qk=[(q, proj[r, 3])], rel=rel_sel[:, (NT - 1 - it) * P:S],
                                         v=[v_sel[:, t] for t in range(it + 1)], gate=gates[:, it, 3 * h + 1:3 * h + 2])
                            elif br == "win":
                                u.update(L=(it + 1 - w0) * P, qk=[(q, proj[r, 4, w0 * P:(it + 1) * P])],
                                         rel=rel_win[:, 640 - (it + 1 - w0) * P:640],
                                         v=[v_win[:, t] for t in range(w0, it + 1)],
                                         gate=gates[:, it, 3 * h + 2:3 * h + 3])
                            else:
                                u.update(L=32, qk=[(q, kc2[r, :])], rel=rel_cmp[:, it], v=[vc[0:32, HD:P]], clamp=True,
                                         gate=gates[:, it, 3 * h:3 * h + 1])
                            U.append(u)
            return U

        def gated(z0):
            def f(v, g, u):
                z = proj[:, z0 + u["pair"], u["it"] * P:(u["it"] + 1) * P]
                return v.tensor_tensor(z, ps[3][:, g % 2 * HALF:g % 2 * HALF + P], z, ALU.mult)
            return f

        softA = Soft("nsa", unitsA(), T3, PT2, st3, gated(5))

        rel_swa = sb("rel_swa", X + 20.125, [P, 2 * P])
        v_swa = sb("v_swa", X + 21.125, [P, NT, P])
        sink_bc = sb("sink_bc", X + 25.125, [P, 4])
        prepB = sem("prepB")

        def act_loadB(act):
            load(act, rel_swa[:], io["rel_swa"])
            load(act, sink_bc[:], io["sink"].to_broadcast([P, 4]))

        def act_prepB(act):
            act.wait_ge(aux, aux_n[0])
            act.wait_ge(prepB, 1)
            act.activation(v_swa[:], ps[0][:].rearrange("p (t c) -> p t c", c=P), ACT.Copy)
            act.activation(proj[0:HD, 3], proj[HD:P, 2], ACT.Copy)
            link(act, "act", act.activation(proj[HD:P, 3], proj[HD:P, 2], ACT.Copy))
            act.activation(proj[HD:P, 2], proj[0:HD, 2], ACT.Copy)
            for z in (4, 5):
                act.activation(T3[:, z - 4], proj[:, z], ACT.Sigmoid)

        def pe_prepB(pe):
            for t in range(NT):
                mm = pe.transpose(ps[0][:, t * P:(t + 1) * P], proj[:, 3, t * P:(t + 1) * P], ident[:])
            mm.then_inc(prepB, 1)

        def unitsB():
            U = []
            for p in range(2):
                for it in range(NT):
                    for hh in range(2):
                        h, r = 2 * p + hh, rows(hh)
                        w0 = max(0, it - 1)
                        U.append(dict(
                            scale=HD ** -0.5, slope=SLOPES[h], first=hh == 0, last=hh == 1, start=True, stop=True,
                            o=lambda g, r=r: ps[3][r, g % 2 * HALF:g % 2 * HALF + P], pair=p, it=it, L=(it + 1 - w0) * P,
                            qk=[(proj[r, p, it * P:(it + 1) * P], proj[r, 2 + p, w0 * P:(it + 1) * P])],
                            rel=rel_swa[:, 2 * P - (it + 1 - w0) * P:2 * P], sink=sink_bc[:, h:h + 1],
                            v=[v_swa[:, t, p * HD:(p + 1) * HD] for t in range(w0, it + 1)]))
            return U

        softB = Soft("swa", unitsB(), T3, PT2, st3, gated(4))

        def dve_silu(v, z0):
            for z in range(2):
                v.tensor_tensor(proj[:, z0 + z], proj[:, z0 + z], T3[:, z], ALU.mult)

        Lb = sb("Lb", X, [P, 2, S])
        Ls = sb("Ls", X + 8, [P, S])
        v_nat = sb("v_nat", X + 21, [P, NT, 2 * P])
        sum_neg = sb("sum_neg", X + 29, [P, P])
        negs = sb("negs", X + 29.5, [P, P])
        mask_lt = sb("mask_lt", X + 30, [P, P])
        neg_ge = sb("neg_ge", X + 30.5, [P, P])
        E2 = sb("E2", X + 31, [P, S])
        prepC, stk_z, stk_c, stk_e, stk_L, stk_s, stk_a, stk_o, stk_out = (
            sem(x) for x in ("prepC", "stk_z", "stk_c", "stk_e", "stk_L", "stk_s", "stk_a", "stk_o", "stk_out"))
        units4 = [(p, it, hh) for p in range(2) for it in range(NT) for hh in range(2)]

        def act_prep_v(act, sm, zdst):
            for x in range(2):
                act.wait_ge(sm, x + 1)
                act.activation(v_nat[:, :, x * P:(x + 1) * P], ps[x][:].rearrange("p (t c) -> p t c", c=P), ACT.Copy)
            for x in range(2):
                act.activation(zdst[:, x], proj[:, 6 + x], ACT.Sigmoid)
            for x in range(2):
                act.mul(proj[:, x], proj[:, x], HD ** -0.5)

        def pe_prep_v(pe, sm):
            for x in range(2):
                for t in range(NT):
                    mm = pe.transpose(ps[x][:, t * P:(t + 1) * P], proj[:, 4 + x, t * P:(t + 1) * P], ident[:])
                mm.then_inc(sm, 1)

        def act_loadC(act):
            for dst, name in ((sum_neg, "sum_neg"), (negs, "neg"), (mask_lt, "mask_lt"), (neg_ge, "neg_ge")):
                load(act, dst[:], io["consts"][CI[name]])

        def act_prepC(act):
            act.wait_ge(aux, aux_n[0])
            act_prep_v(act, prepC, PT2)

        def dve_silu_cd(v, zsrc):
            for x in range(2):
                v.tensor_tensor(proj[:, 6 + x], proj[:, 6 + x], zsrc[:, x], ALU.mult)

        def pe_stick(pe):
            def z(j):
                p, it, hh = units4[j]
                r = rows(hh)
                if j >= 2:
                    pe.wait_ge(stk_a, j - 1)
                for d in range(it + 1):
                    mm = pe.matmul(ps[j % 2][:, d * P:(d + 1) * P], proj[r, 2 + p, (it - d) * P:(it - d + 1) * P],
                                   proj[r, p, it * P:(it + 1) * P], start=d % 4 == 0, stop=False, skip_group_check=True)
                mm.then_inc(stk_z, 1)

            def sums(j):
                p, it, hh = units4[j]
                pe.wait_ge(stk_s, j + 1)
                t = ps[j % 2]
                w = (it + 1) * P
                pe.matmul(t[:, 0:P], ident[:], neg_ge[:], start=False, stop=False, skip_group_check=True)
                for c0 in range(0, w, HALF):
                    c1, after_first = min(w, c0 + HALF), max(c0, P)
                    if after_first < c1:
                        pe.matmul(t[:, after_first:c1], negs[:], Ls[:, after_first:c1], start=False, stop=False,
                                  skip_group_check=True)
                    mm = pe.matmul(t[:, c0:c1], sum_neg[:], Lb[:, j % 2, c0:c1], start=False, stop=True,
                                   skip_group_check=True)
                mm.then_inc(stk_L, 1)

            def pv(j):
                p, it, hh = units4[j]
                g = j // 2
                pe.wait_ge(stk_a, j + 1)
                if hh == 0 and g >= 2:
                    pe.wait_ge(stk_out, g - 1)
                for d in range(it + 1):
                    mm = pe.matmul(ps[3][rows(hh), g % 2 * HALF:g % 2 * HALF + P],
                                   v_nat[:, it - d, (2 * p + hh) * HD:(2 * p + hh + 1) * HD],
                                   PT2[:, j % 2, d * P:(d + 1) * P], start=d == 0, stop=d == it)
                if hh == 1:
                    mm.then_inc(stk_o, 1)
            N = len(units4)
            z(0)
            for j in range(N):
                if j + 1 < N:
                    z(j + 1)
                sums(j)
                if j >= 1:
                    pv(j - 1)
            pv(N - 1)

        def act_stick(act):
            act.preload_act_table_set("natural_log_exp_and_others")

            def soft(j):
                w = (units4[j][1] + 1) * P
                act.wait_ge(stk_c, j + 1)
                link(act, "act", act.activation(E2[:, 0:w], E2[:, 0:w], ACT.Exp))
                act.activation(E2[:, 0:w], E2[:, 0:w], ACT.Ln, bias=1.0).then_inc(stk_e, 1)

            def prob(j):
                w = (units4[j][1] + 1) * P
                act.wait_ge(stk_L, j + 1)
                act.activation(PT2[:, j % 2, 0:w], ps[j % 2][:, 0:w], ACT.Exp).then_inc(stk_a, 1)
            N = len(units4)
            soft(0)
            for j in range(N):
                if j + 1 < N:
                    soft(j + 1)
                prob(j)

        def dve_stick(v):
            def clip(j):
                w = (units4[j][1] + 1) * P
                v.wait_ge(stk_z, j + 1)
                if j >= 1:
                    v.wait_ge(stk_e, j)
                v.tensor_scalar(E2[:, 0:w], ps[j % 2][:, 0:w], 40.0, None, ALU.min).then_inc(stk_c, 1)

            def plus(j):
                it = units4[j][1]
                w = (it + 1) * P
                v.wait_ge(stk_e, j + 1)
                L, R = Lb[:, j % 2], Ls
                if j >= 1:
                    v.wait_ge(stk_L, j)
                link(v, "dve", v.tensor_tensor(L[:, 0:w], E2[:, 0:w], ps[j % 2][:, 0:w], ALU.max))
                ins = v.tensor_tensor(L[:, 0:P], L[:, 0:P], mask_lt[:], ALU.mult)
                for d in range(1, it + 1):
                    link(v, "dve", ins)
                    if d == 1:
                        ins = v.tensor_copy(R[:, P:2 * P], L[:, 0:P])
                    else:
                        ins = v.tensor_tensor(R[:, d * P:(d + 1) * P], R[:, (d - 1) * P:d * P], L[:, (d - 1) * P:d * P],
                                              ALU.add)
                ins.then_inc(stk_s, 1)

            def fin(g):
                p, it, _ = units4[2 * g]
                v.wait_ge(stk_o, g + 1)
                z = proj[:, 6 + p, it * P:(it + 1) * P]
                v.tensor_tensor(z, ps[3][:, g % 2 * HALF:g % 2 * HALF + P], z, ALU.mult).then_inc(stk_out, 1)
            N = len(units4)
            clip(0)
            for j in range(N):
                plus(j)
                if j + 1 < N:
                    clip(j + 1)
                if j >= 3 and j % 2 == 1:
                    fin(j // 2 - 1)
            fin(N // 2 - 1)

        decay = sb("decay", X + 4, [P, 4, S])
        rPT = sb("rPT", X, [P, S])
        rP = [rPT, sb("rP1", X + 31, [P, S])]
        o_ret = proj[:, 4:6]
        zsig = sb("zsig", V + 32, [P, 2, S])
        onesh = sb("onesh", X + 29, [P, P])
        prepD, ret_s, ret_p, ret_o, ret_out, ln = (sem(x) for x in ("prepD", "ret_s", "ret_p", "ret_o", "ret_out", "ln"))

        def act_loadD(act):
            load(act, decay[:], io["decay"])
            load(act, onesh[:], io["consts"][CI["ones_h"]])

        def act_prepD(act):
            act.wait_ge(aux, aux_n[0])
            act_prep_v(act, prepD, zsig)

        def pe_ret(pe):
            def sc(j):
                p, it, hh = units4[j]
                r = rows(hh)
                if j >= 2:
                    pe.wait_ge(ret_p, j - 1)
                for d in range(it + 1):
                    mm = pe.matmul(ps[j % 2][:, d * P:(d + 1) * P], proj[r, 2 + p, (it - d) * P:(it - d + 1) * P],
                                   proj[r, p, it * P:(it + 1) * P], start=True, stop=True)
                mm.then_inc(ret_s, 1)

            def pv(j):
                p, it, hh = units4[j]
                g = j // 2
                pe.wait_ge(ret_p, j + 1)
                if hh == 0 and g >= 2:
                    pe.wait_ge(ret_out, g - 1)
                for d in range(it + 1):
                    mm = pe.matmul(ps[3][rows(hh), g % 2 * HALF:g % 2 * HALF + P],
                                   v_nat[:, it - d, (2 * p + hh) * HD:(2 * p + hh + 1) * HD],
                                   rP[j % 2][:, d * P:(d + 1) * P], start=d == 0, stop=d == it)
                mm.then_inc(ret_o, 1)
            sc(0)
            for j in range(len(units4)):
                if j + 1 < len(units4):
                    sc(j + 1)
                pv(j)
            for x in range(2):
                pe.wait_ge(ln, 5 * x + 1)
                for h in range(2):
                    mm = pe.matmul(ps[x][:, h * HALF:(h + 1) * HALF], onesh[:], o_ret[:, x, h * HALF:(h + 1) * HALF],
                                   start=True, stop=True)
                mm.then_inc(ln, 1)
                pe.wait_ge(ln, 5 * x + 4)
                for h in range(2):
                    mm = pe.matmul(ps[x][:, h * HALF:(h + 1) * HALF], onesh[:], rPT[:, h * HALF:(h + 1) * HALF],
                                   start=True, stop=True)
                mm.then_inc(ln, 1)

        def dve_ret(v):
            for j, (p, it, hh) in enumerate(units4):
                w = (it + 1) * P
                v.wait_ge(ret_s, j + 1)
                if j >= 2:
                    v.wait_ge(ret_o, j - 1)
                v.tensor_tensor(rP[j % 2][:, 0:w], ps[j % 2][:, 0:w], decay[:, 2 * p + hh, 0:w], ALU.mult).then_inc(ret_p, 1)
            for x in range(2):
                if x == 0:
                    v.wait_ge(ret_out, 2 * NT)
                    v.tensor_copy(rP[1][:, 0:2], onesh[:, 0:2]).then_inc(ln, 1)
                else:
                    v.tensor_copy(rP[1][:, 0:2], onesh[:, 0:2]).then_inc(ln, 1)
                v.wait_ge(ln, 5 * x + 2)
                v.tensor_tensor(o_ret[:, x], o_ret[:, x], ps[x][:], ALU.subtract).then_inc(ln, 1)
                v.wait_ge(ln, 5 * x + 5)
                v.wait_ge(ret_rt, x + 1)
                link(v, "dve", v.reciprocal(rP[1][:], rP[1][:]))
                link(v, "dve", v.tensor_tensor(o_ret[:, x], o_ret[:, x], rP[1][:], ALU.mult))
                link(v, "dve", v.tensor_tensor(proj[:, 6 + x], proj[:, 6 + x], o_ret[:, x], ALU.mult))

        ret_rt = sem("ret_rt")

        def act_ret(act):
            for g in range(2 * NT):
                p, it, _ = units4[2 * g]
                act.wait_ge(ret_o, 2 * g + 2)
                act.activation(o_ret[:, p, it * P:(it + 1) * P], ps[3][:, g % 2 * HALF:g % 2 * HALF + P],
                               ACT.Copy).then_inc(ret_out, 1)
            for x in range(2):
                act.wait_ge(ln, 5 * x + 3)
                act.activation(rPT[:], o_ret[:, x], ACT.Square).then_inc(ln, 1)
                act.wait_ge(ln, 5 * x + 5)
                act.activation(rP[1][:], ps[x][:], ACT.Sqrt, bias=eps_col(LN_EPS)).then_inc(ret_rt, 1)

        R = proj
        m_sig = sb("m_sig", X, [P, 2, S])
        m_t = sb("m_t", X + 8, [P, 2, S])
        ysplit = {b: Split(f"ysplit{b}", proj[:, z:z + 2], 2, Ya_hi, Ya_lo)
                  for b, z in (("A", 5), ("B", 4), ("C", 6), ("D", 6))}
        sig_done = sem("sig_done")
        sig_n = {"act": 0, "dve": 0}

        def act_merge(act):
            s0 = sig_n["act"]
            def one(j, t):
                par = 0 if t is ps[0] else 1
                act.wait_ge(evac_dve, tiles["act"] + 1 + j)
                act.activation(m_sig[:, par], t[:], ACT.Sigmoid).then_inc(evac_act, 1)
            each_tile(act, "act", 8, one)

        def dve_merge(v, first):
            g0 = tiles["dve"]
            c = own["dve"]

            def one(j, par):
                v.wait_ge(evac_act, g0 + 3 + j)
                t = m_sig[:, (g0 + par) % 2]
                if first:
                    v.tensor_tensor(ACC[:, j], t, R[:, j], ALU.mult).then_inc(evac_dve, 1)
                else:
                    link(v, "dve", v.tensor_tensor(m_t[:, par], t, R[:, j], ALU.mult))
                    v.tensor_tensor(ACC[:, j], ACC[:, j], m_t[:, par], ALU.add).then_inc(evac_dve, 1)
            if first:
                pairs(v, 8, one)
            else:
                with v.Fori(0, 4) as i:
                    c.enter(i, 2)
                    for s in range(2):
                        one(2 * i + s, s)
                c.leave(4)
            tiles["dve"] += 8

        merged = Split("merged", ACC, NT, Y_hi, Y_lo)
        x_back = sem("x_back")

        def act_out1(act):
            def one(j, t):
                act.activation(t[:, 0:2], t[:, 0:2], ACT.Copy)
            for k in range(NT):
                act.wait_ge(merged.lo_done, merged.at["lo_done"] + k + 1)
                load(act, ACC[:, k], io["x"][k])
            act.wait_ge(aux, aux_n[0])
            act.drain().then_inc(x_back, 1)
            act_squares(act, norm_f)

        def act_gemm_none(act, n):
            def one(j, t):
                act.sem_inc(evac_act, 1)
            each_tile(act, "act", n, one)

        def dve_out1(v):
            norm_f.start(v)
            v.wait_ge(x_back, 1)

            def one(j, t):
                v.scalar_tensor_tensor(out=ACC[:, j], in0=t[:], scalar=cols[:, bass.ds(C_MOD + 16 + j, 1)], in1=ACC[:, j],
                                       op0=ALU.mult, op1=ALU.add).then_inc(evac_dve, 1)
                norm_f.add(v, j, 0 if t is ps[0] else 1)
            each_tile(v, "dve", 8, one)

        norm_f = Norm("norm_f", ACC, NT, ones_d, cols[:, C_FG:C_FG + 8], into=ACC)
        norm_e = Norm("norm_e", ACC, NT, ones_d, cols[:, C_EG:C_EG + 8], hi=H_hi, lo=H_lo)
        chain_e = Chain(norm_f, norm_e, keep1)

        G_EPOST, G_OPRE, G_OPOST, G_GNG, G_GNB, G_CB, G_HN, G_Q, G_KV, G_BG, G_INV, G_ALT = (
            0, 8, 16, 24, 32, 40, 48, 56, 59, 61, 62, 63)
        Dw = sb("Dw", V, [P, NT, S])
        Db = sb("Db", V + 32, [P, NT, P])
        QKV = sb("QKV", V + 36, [P, 4, S])
        hn = QKV[:, 2:4].rearrange("p a (t c) -> p (a t) c", c=256)
        Vn = sb("Vn", V + 52, [P, NT, 264])
        PTl = sb("PTl", V + 60.25, [P, 2, 9, P])
        Mrow = sb("Mrow", V + 69.25, [4, 2, S])
        lst = sb("lst", V + 77.25, [P, 160])
        a_col = lst[:, 0:64].rearrange("p (d t c) -> p d t c", d=2, t=NT)
        emm = lst[:, 64:128].rearrange("p (d t c) -> p d t c", d=2, t=NT)
        ss8 = lst[:, 128:136]
        rr8 = lst[:, 136:144]
        den = lst[:, 144:160]
        neg_f = sb("neg_f", V + 78, [P, P])
        neg_b = sb("neg_b", V + 78.5, [P, P])
        sel4 = sb("sel4", V + 79, [4, 4, P])
        OZ = sb("OZ", V, [P, 4, S])
        ozs = sb("ozs", V + 16, [P, 4, S])
        gT2 = sb("gT2", V, [P, 1, S])
        arow = sb("arow", V + 4, [4, 2, S])
        cum = [sb("cum_f", V + 12, [P, P]), sb("cum_b", V + 12.5, [P, P])]
        ones1 = sb("ones1", V + 13, [P, P])
        gw = sb("gw", V + 13.5, [P, 6, 128])
        gn = gw[:, 0]
        gn5 = gn.rearrange("p (t d x c) -> p d t x c", t=NT, d=2, x=2)
        fpre, ipre = gn5[:, :, :, 1], gn5[:, :, :, 0]

        def dtc(x):
            return gw[:, x, 0:64].rearrange("p (d t c) -> p d t c", d=2, t=NT)
        fab, flg, lf, lfs, Fc = dtc(1), dtc(2), dtc(3), dtc(4), dtc(5)
        gp = sem("gp")

        def act_load_gates(act):
            act.wait_ge(norm_e.lo_done, norm_e.at["lo_done"] + NT)
            for t, n in ((cum[0], "cum_f"), (cum[1], "cum_b"), (ones1, "ones"), (neg_f, "neg_f"), (neg_b, "neg_b")):
                load(act, t[:], io["consts"][CI[n]])
            load(act, sel4[:], io["sel4"])

        def act_gates(act):
            act.wait_ge(kept, kept_n[0])
            act.wait_ge(aux, aux_n[0])
            act.activation(gT2[:, 0], gT2[:, 0], ACT.Identity, bias=cols2[:, G_BG:G_BG + 1]).then_inc(gp, 1)
            act.wait_ge(gp, 3)
            link(act, "act", act.activation(flg, fab, ACT.Exp, scale=-1.0))
            act.activation(flg, flg, ACT.Ln, bias=1.0).then_inc(gp, 1)
            act.wait_ge(gp, 11)
            act.activation(emm, fab, ACT.Exp, scale=-1.0).then_inc(gp, 1)

        def pe_gates(pe):
            pe.wait_ge(gp, 1)
            for t in range(NT):
                mm = pe.transpose(ps[0][:, t * P:(t + 1) * P], gT2[:, 0, t * P:(t + 1) * P], ident[:])
            mm.then_inc(gp, 1)
            pe.wait_ge(gp, 5)
            for d in range(2):
                o = ps[1][:, d * 32:(d + 1) * 32]
                pe.matmul(o, cum[d][:], lf[:, d], start=True, stop=False)
                mm = pe.matmul(o, ones1[:], lfs[:, d], start=False, stop=True)
            mm.then_inc(gp, 1)
            pe.wait_ge(gp, 7)
            for d in range(2):
                for t in range(NT):
                    mm = pe.transpose(ps[2 + d][0:4, t * P:(t + 1) * P], a_col[:, d, t], ident[:])
            mm.then_inc(gp, 1)
            pe.wait_ge(gp, 9)
            for d in range(2):
                for t in range(NT):
                    x = (d * NT + t) * 4
                    mm = pe.transpose(ps[0][:, x:x + 4], Mrow[0:4, d, t * P:(t + 1) * P], ident[0:4, 0:4])
            mm.then_inc(gp, 1)

        def dve_gates(v):
            v.wait_ge(gp, 2)
            link(v, "dve", v.tensor_copy(gn.rearrange("p (t c) -> p t c", t=NT),
                                         ps[0][:].rearrange("p (t c) -> p t c", c=P)[:, :, 0:16]))
            for d in range(2):
                ins = v.scalar_tensor_tensor(out=fab[:, d], in0=fpre[:, d], scalar=-1.0, in1=fpre[:, d], op0=ALU.mult,
                                             op1=ALU.max)
            ins.then_inc(gp, 1)
            v.wait_ge(gp, 4)
            for d in range(2):
                ins = v.scalar_tensor_tensor(out=lf[:, d], in0=fpre[:, d], scalar=0.0, in1=flg[:, d], op0=ALU.min,
                                             op1=ALU.subtract)
            link(v, "dve", ins)
            for d in range(2):
                order = list(range(NT)) if d == 0 else list(range(NT - 1, -1, -1))
                link(v, "dve", v.memset(lfs[:, d, order[0]], 0.0))
                for a, b in zip(order, order[1:]):
                    link(v, "dve", v.tensor_tensor(lfs[:, d, b], lfs[:, d, a], lf[:, d, a], ALU.add))
            v.drain().then_inc(gp, 1)
            v.wait_ge(gp, 6)
            link(v, "dve", v.tensor_copy(gw[:, 5, 0:64], ps[1][:, 0:64]))
            for d in range(2):
                ins = v.tensor_tensor(a_col[:, d], ipre[:, d], Fc[:, d], ALU.subtract)
            ins.then_inc(gp, 1)
            v.wait_ge(gp, 8)
            for d in range(2):
                link(v, "dve", v.tensor_copy(arow[:, d], ps[2 + d][0:4, :]))
                a, m = arow[:, d], Mrow[:, d]
                if d:
                    a, m = a[:, ::-1], m[:, ::-1]
                ins = v.tensor_tensor_scan(m, a, a, 0.0, ALU.max, ALU.max)
                link(v, "dve", ins)
            v.drain().then_inc(gp, 1)
            v.wait_ge(gp, 10)
            v.tensor_tensor(gw[:, 1, 0:64], gw[:, 5, 0:64], ps[0][:, 0:64], ALU.add).then_inc(gp, 1)
            v.wait_ge(gp, 12)
            v.memset(Vn[:, :, 256:257], 1.0)

        DK = 128.0 ** -0.5

        class Lstm:
            def __init__(self, h):
                self.h = h
                self.bcast, self.turned, self.vn, self.diag, self.s, self.p, self.o, self.o_out, self.t, self.hn, self.f = (
                    shared(f"lstm_{x}") for x in ("bcast", "turned", "vn", "diag", "scores", "p", "o", "oout", "t", "hn",
                                                  "f"))
                self.at = since("lstm", bcast=1, turned=2, vn=2, diag=1, s=NT, p=NT, o=NT, o_out=NT, t=1, hn=1, f=2)

            def pe_w(self, pe):
                for d in range(2):
                    for k in range(2):
                        mm = pe.matmul(ps[2 + d][:, k * HALF:(k + 1) * HALF], sel4[:, self.h],
                                       Mrow[:, d, k * HALF:(k + 1) * HALF], start=True, stop=True)
                mm.then_inc(self.bcast, 1)

            def act_w(self, act):
                h = self.h
                act.wait_ge(self.diag, self.at['diag'] + 1)
                for st in range(NT):
                    if st < NT - 1:
                        act.activation(Dw[:, st, (st + 1) * P:S], ps[2][:, (st + 1) * P:S], ACT.Exp,
                                       bias=a_col[:, 0, st, h:h + 1])
                    if st > 0:
                        act.activation(Dw[:, st, 0:st * P], ps[3][:, 0:st * P], ACT.Exp, bias=a_col[:, 1, st, h:h + 1])
                for st in range(NT):
                    d = Dw[:, st, st * P:(st + 1) * P]
                    act.activation(d, d, ACT.Exp)
                act.activation(Db[:], Db[:], ACT.Exp)

            def dve_w(self, v):
                h = self.h
                v.wait_ge(self.bcast, self.at['bcast'] + 1)
                for st in range(NT):
                    c = slice(st * P, (st + 1) * P)
                    v.scalar_tensor_tensor(out=Dw[:, st, c], in0=ps[2][:, c], scalar=a_col[:, 0, st, h:h + 1],
                                           in1=neg_f[:], op0=ALU.add, op1=ALU.add)
                    ins = v.scalar_tensor_tensor(out=Db[:, st], in0=ps[3][:, c], scalar=a_col[:, 1, st, h:h + 1],
                                                 in1=neg_b[:], op0=ALU.add, op1=ALU.add)
                ins.then_inc(self.diag, 1)

            def pe(self, pe):
                def sc(it):
                    if it >= 2:
                        pe.wait_ge(self.p, self.at['p'] + it - 1)
                    for st in range(NT):
                        mm = pe.matmul(ps[it % 2][:, st * P:(st + 1) * P], QKV[:, 1, st * P:(st + 1) * P],
                                       QKV[:, 0, it * P:(it + 1) * P], start=True, stop=True)
                    mm.then_inc(self.s, 1)
                for x in range(2):
                    for t in range(NT):
                        mm = pe.transpose(ps[2 + x][:, t * P:(t + 1) * P], QKV[:, 2 + x, t * P:(t + 1) * P], ident[:])
                    mm.then_inc(self.turned, 1)
                sc(0)
                for it in range(NT):
                    if it + 1 < NT:
                        sc(it + 1)
                    pe.wait_ge(self.p, self.at['p'] + it + 1)
                    if it == 0:
                        pe.wait_ge(self.vn, self.at['vn'] + 2)
                    if it >= 2:
                        pe.wait_ge(self.o_out, self.at['o_out'] + it - 1)
                    c = it % 2 * HALF
                    for st in range(it + 1):
                        pe.matmul(ps[2][:, c:c + 257], PTl[:, it % 2, st], Vn[:, st, 0:257], start=st == 0, stop=st == it)
                    for st in range(it, NT):
                        mm = pe.matmul(ps[3][:, c:c + 257], PTl[:, it % 2, st + 1], Vn[:, st, 0:257], start=st == it,
                                       stop=st == NT - 1)
                    mm.then_inc(self.o, 1)

            def dve(self, v):
                h = self.h

                def probs(it):
                    v.wait_ge(self.s, self.at['s'] + it + 1)
                    if it >= 2:
                        v.wait_ge(self.o, self.at['o'] + it - 1)
                    q3 = ps[it % 2][:].rearrange("p (s c) -> p s c", c=P)
                    c = slice(it * P, (it + 1) * P)
                    o = PTl[:, it % 2]
                    v.scalar_tensor_tensor(out=o[:, 0:it + 1], in0=q3[:, 0:it + 1], scalar=DK, in1=Dw[:, 0:it + 1, c],
                                           op0=ALU.mult, op1=ALU.mult)
                    if it < NT - 1:
                        v.scalar_tensor_tensor(out=o[:, it + 2:9], in0=q3[:, it + 1:NT], scalar=DK,
                                               in1=Dw[:, it + 1:NT, c], op0=ALU.mult, op1=ALU.mult)
                    v.scalar_tensor_tensor(out=o[:, it + 1], in0=q3[:, it], scalar=DK, in1=Db[:, it],
                                           op0=ALU.mult, op1=ALU.mult).then_inc(self.p, 1)

                def outs(it):
                    v.wait_ge(self.o, self.at['o'] + it + 1)
                    c = it % 2 * HALF
                    for d in range(2):
                        ins = v.tensor_scalar(den[:, d:d + 1], ps[2 + d][:, c + 256:c + 257], -1.0,
                                              emm[:, d, it, h:h + 1], ALU.mult, ALU.max)
                    link(v, "dve", ins)
                    for d in range(2):
                        ins = v.tensor_tensor(den[:, 2 + d:3 + d], den[:, d:d + 1], ps[2 + d][:, c + 256:c + 257],
                                              ALU.max)
                    link(v, "dve", ins)
                    link(v, "dve", v.reciprocal(den[:, 4:6], den[:, 2:4]))
                    link(v, "dve", v.tensor_scalar(hn[:, it], ps[2][:, c:c + 256], den[:, 4:5], None, ALU.mult))
                    v.scalar_tensor_tensor(out=hn[:, it], in0=ps[3][:, c:c + 256], scalar=den[:, 5:6], in1=hn[:, it],
                                           op0=ALU.mult, op1=ALU.add).then_inc(self.o_out, 1)
                for it in range(NT):
                    probs(it)
                    if it >= 1:
                        outs(it - 1)
                outs(NT - 1)
                v.wait_ge(self.t, self.at['t'] + 1)
                link(v, "dve", v.reciprocal(rr8, ss8))
                v.tensor_tensor(hn, hn, rr8.unsqueeze(2).to_broadcast([P, NT, 256]), ALU.mult).then_inc(self.hn, 1)

            def act(self, act):
                for x in range(2):
                    act.wait_ge(self.turned, self.at['turned'] + x + 1)
                    act.activation(Vn[:, :, x * P:(x + 1) * P], ps[2 + x][:].rearrange("p (t c) -> p t c", c=P),
                                   ACT.Copy).then_inc(self.vn, 1)
                for it in range(NT):
                    act.wait_ge(self.o_out, self.at['o_out'] + it + 1)
                    link(act, "act", act.activation(lsq, hn[:, it], ACT.Square, accum_out=ss8[:, it:it + 1]))
                act.activation(ss8, ss8, ACT.Sqrt, bias=eps_col(RMS_EPS), scale=1.0 / 256).then_inc(self.t, 1)

            def pe_f(self, pe):
                n0 = CHUNK0[f"lstm{self.h}"] + 4
                pe_gemm(pe, n0, 2, 8, H_hi, H_lo)
                pe.wait_ge(self.hn, self.at['hn'] + 1)
                for x in range(2):
                    for t in range(NT):
                        mm = pe.transpose(ps[2 + x][:, t * P:(t + 1) * P], hn[:, t, x * P:(x + 1) * P], ident[:])
                    mm.then_inc(self.f, 1)
                pe_gemm(pe, n0 + 2, 2, 8, H_hi, H_lo)

            def act_f(self, act):
                def one(j, t):
                    act.activation(ozs[:, j], t[:], ACT.Sigmoid).then_inc(evac_act, 1)
                each_tile(act, "act", 4, one)

            def dve_f(self, v):
                h, g0 = self.h, tiles["dve"]
                v.sem_inc(evac_dve, 2)
                for x in range(2):
                    v.wait_ge(evac_act, g0 + 3 + x)
                    v.wait_ge(self.f, self.at['f'] + x + 1)
                    v.scalar_tensor_tensor(out=ACC[:, 2 * h + x], in0=ps[2 + x][:],
                                           scalar=cols2[:, G_HN + 2 * h + x:G_HN + 2 * h + x + 1],
                                           in1=ozs[:, x], op0=ALU.mult, op1=ALU.mult)
                for x in range(2):
                    y = ACC[:, 2 * h + x]
                    v.wait_ge(evac_act, g0 + 5 + x)
                    v.tensor_tensor(OZ[:, x], ps[(g0 + x) % 2][:], ozs[:, 2 + x], ALU.mult).then_inc(evac_dve, 1)
                    v.wait_ge(evac_dve, g0 + 5 + x)
                    v.tensor_tensor(y, y, OZ[:, x], ALU.mult)
                tiles["dve"] += 4

        lsq = sb("lsq", V + 81, [P, 256])[:]
        lstm = [Lstm(h) for h in range(H_B)]
        split_b = Split("split_b", ACC, NT, Y_hi, Y_lo)

        Z_hi = sb("Z_hi", 0, [P, NT, S], F32R)
        Z_lo = sb("Z_lo", 32, [P, NT, S], F32R)
        ya = sb("ya", V, [P, NT, S])
        W = V + 32
        Uc = sb("Uc", W, [P, S + 32])
        cacc = [sb("cacc0", W + 4.25, [P, S]), sb("cacc1", W + 42, [P, S])]
        c_sg = sb("c_sg", W + 8.25, [P, S])
        c_sz = sb("c_sz", W + 12.25, [P, S])
        c_zs = [sb("c_zs0", W + 16.25, [P, S]), sb("c_zs1", W + 46, [P, S])]
        c_sq = sb("c_sq", W + 20.25, [P, S])
        c_rt = sb("c_rt", W + 24.25, [P, S])
        c_v = sb("c_v", W + 28.25, [P, S])
        c_s = sb("c_s", W + 32.25, [P, S])
        c_rs = sb("c_rs", W + 36.25, [P, S])
        conv_w = sb("conv_w", W + 40.25, [P, NT, CONV_K + 1])
        ones_c = sb("ones_c", W + 41.5, [P, P])
        PE_TAPS = 6
        diag = sb("diag", W + 50, [P, PE_TAPS, P])
        conv_diag, conv_tap = sem("conv_diag"), sem("conv_tap")
        conv_in, gn_s = sem("conv_in"), sem("gn_s")

        split_a = Split("split_a", ya, NT, Z_hi, Z_lo)
        conv_left = sem("conv_left")

        def hi_a(act, c):
            act.wait_ge(conv_left, c + 1)
            act.activation(Z_hi[:, c], ya[:, c], ACT.Copy).then_inc(split_a.hi_done, 1)

        def act_conv(act):
            g0 = tiles["act"]

            def gate(c):
                g = g0 + 3 * c
                act.wait_ge(out_ready, g + 1)
                if c:
                    act.wait_ge(conv_in, c)
                act.activation(c_sg[:], ps[g % 2][:], ACT.Sigmoid).then_inc(evac_act, 1)
                act.drain().then_inc(evac_act, 1)

            def zgate(c):
                g = g0 + 3 * c
                act.wait_ge(out_ready, g + 3)
                act.activation(c_sz[:], ps[(g + 2) % 2][:], ACT.Sigmoid).then_inc(evac_act, 1)
            gate(0)
            zgate(0)
            for c in range(NT + 1):
                b = 7 * (c - 1)
                if c < NT:
                    if c:
                        act.wait_ge(conv_tap, c)
                    for j in range(PE_TAPS):
                        k = CONV_K - PE_TAPS + j
                        ins = act.activation(diag[:, j], ident[:], ACT.Copy, scale=conv_w[:, c, k:k + 1])
                    ins.then_inc(conv_diag, 1)
                if c:
                    act.wait_ge(gn_s, b + 3)
                    act.activation(c_sq[:], cacc[(c - 1) % 2][:], ACT.Square).then_inc(gn_s, 1)
                if c + 1 < NT:
                    gate(c + 1)
                if c:
                    act.wait_ge(gn_s, b + 5)
                    act.activation(c_rt[:], ps[3][:], ACT.Sqrt, bias=eps_col(LN_EPS)).then_inc(gn_s, 1)
                    act.wait_ge(gn_s, b + 7)
                    x = c - 1
                    link(act, "act", act.activation(c_v[:], cacc[x % 2][:], ACT.Identity,
                                                    scale=cols2[:, G_GNG + x:G_GNG + x + 1],
                                                    bias=cols2[:, G_GNB + x:G_GNB + x + 1]))
                    act.activation(c_s[:], c_v[:], ACT.Sigmoid).then_inc(gn_v, 1)
                if c + 1 < NT:
                    zgate(c + 1)
                if c == NT - 1:
                    for x in range(NT - 1):
                        hi_a(act, x)
            hi_a(act, NT - 1)
            tiles["act"] += 24

        gn_v = sem("gn_v")

        def pe_conv(pe):
            n0, g0 = CHUNK0["conv"], tiles["pe"]

            def product(c, o):
                n, g = n0 + 3 * c + o, g0 + 3 * c + o
                s, t = n % 2, ps[g % 2]
                pe.wait_ge(w_split, n + 1)
                pe.wait_ge(evac_act, g + 1)
                pe.wait_ge(evac_dve, g + 1)
                for k in range(NT):
                    for h in range(2):
                        mm = mm3(pe, t[:, h * HALF:(h + 1) * HALF], w_hi[s][:, k * P:(k + 1) * P],
                                 w_lo[s][:, k * P:(k + 1) * P], H_hi[:, k, h * HALF:(h + 1) * HALF],
                                 H_lo[:, k, h * HALF:(h + 1) * HALF], k == 0, k == NT - 1, opens=k == 0 and h == 0)
                mm.then_inc(out_ready, 1)

            def mean(c, src, x, at):
                pe.wait_ge(gn_s, 7 * c + at)
                for h in range(2):
                    mm = pe.matmul(ps[2 + x][:, h * HALF:(h + 1) * HALF], ones_c[:], src[:, h * HALF:(h + 1) * HALF],
                                   start=True, stop=True)
                mm.then_inc(gn_s, 1)

            def taps(c):
                pe.wait_ge(conv_in, c + 1)
                pe.wait_ge(conv_diag, c + 1)
                for h in range(2):
                    for j in range(PE_TAPS):
                        k = CONV_K - PE_TAPS + j + h * HALF
                        mm = pe.matmul(ps[2][:, h * HALF:(h + 1) * HALF], diag[:, j], Uc[:, k:k + HALF],
                                       start=j == 0, stop=j == PE_TAPS - 1)
                mm.then_inc(conv_tap, 1)
            for o in range(3):
                product(0, o)
            for c in range(NT + 1):
                if c:
                    mean(c - 1, cacc[(c - 1) % 2], 0, 1)
                if c + 1 < NT:
                    product(c + 1, 0)
                if c:
                    mean(c - 1, c_sq, 1, 4)
                if c < NT:
                    taps(c)
                if c + 1 < NT:
                    product(c + 1, 1)
                    product(c + 1, 2)
            tiles["pe"] += 24

        def dve_conv(v):
            g0 = tiles["dve"]
            link(v, "dve", v.memset(Uc[:], 0.0))
            v.sem_inc(evac_dve, 1)

            def centre(c):
                v.wait_ge(gn_s, 7 * c + 2)
                v.tensor_tensor(cacc[c % 2][:], cacc[c % 2][:], ps[2][:], ALU.subtract).then_inc(gn_s, 1)

            def scale(c):
                v.wait_ge(gn_s, 7 * c + 6)
                link(v, "dve", v.reciprocal(c_rs[:], c_rt[:]))
                v.tensor_tensor(cacc[c % 2][:], cacc[c % 2][:], c_rs[:], ALU.mult).then_inc(gn_s, 1)

            def leave(c):
                v.wait_ge(gn_v, c + 1)
                link(v, "dve", v.tensor_tensor(ya[:, c], c_v[:], c_s[:], ALU.mult))
                v.tensor_tensor(ya[:, c], ya[:, c], c_zs[c % 2][:], ALU.mult).then_inc(conv_left, 1)

            def low(c):
                v.wait_ge(split_a.hi_done, split_a.at["hi_done"] + c + 1)
                v.tensor_tensor(Z_lo[:, c], ya[:, c], Z_hi[:, c].bitcast(F32), ALU.subtract).then_inc(
                    split_a.lo_done, 1)
            between = {4: centre, 16: scale, 22: leave}
            for c in range(NT):
                g = g0 + 3 * c
                v.wait_ge(evac_act, g + 3)
                v.wait_ge(out_ready, g + 2)
                if c:
                    v.wait_ge(gn_s, 7 * c - 6)
                v.tensor_tensor(Uc[:, 15:15 + S], ps[(g + 1) % 2][:], c_sg[:], ALU.mult).then_inc(evac_dve, 1)
                v.wait_ge(evac_act, g + 5)
                v.tensor_tensor(c_zs[c % 2][:], ps[(g + 2) % 2][:], c_sz[:], ALU.mult).then_inc(evac_dve, 1)
                v.wait_ge(evac_dve, g + 5)
                v.sem_inc(conv_in, 1)
                if c < NT - 1:
                    v.sem_inc(evac_dve, 1)
                acc = cacc[c % 2]
                ins = v.tensor_scalar(acc[:], Uc[:, 0:S], conv_w[:, c, 0:1], cols2[:, G_CB + c:G_CB + c + 1],
                                      ALU.mult, ALU.add)
                for k in range(1, CONV_K - PE_TAPS):
                    link(v, "dve", ins)
                    if c and k in between:
                        between[k](c - 1)
                    ins = v.scalar_tensor_tensor(out=acc[:], in0=Uc[:, k:k + S], scalar=conv_w[:, c, k:k + 1],
                                                 in1=acc[:], op0=ALU.mult, op1=ALU.add)
                link(v, "dve", ins)
                v.wait_ge(conv_tap, c + 1)
                v.tensor_tensor(acc[:], acc[:], ps[2][:], ALU.add).then_inc(gn_s, 1)
            for step, parts in ((centre, range(0, 4)), (scale, range(4, NT - 1)), (leave, (NT - 1,))):
                step(NT - 1)
                for c in parts:
                    low(c)
            tiles["dve"] += 24

        norm_ep = Norm("norm_ep", ACC, NT, ones_d, cols2[:, G_EPOST:G_EPOST + 8], into=ACC)
        norm_o = Norm("norm_o", ACC, NT, ones_d, cols2[:, G_OPRE:G_OPRE + 8], hi=H_hi, lo=H_lo)
        chain_o = Chain(norm_ep, norm_o, keep2, "x1")

        def dve_add(v, norm):
            def one(j, t):
                v.tensor_tensor(ACC[:, j], ACC[:, j], t[:], ALU.add).then_inc(evac_dve, 1)
                norm.add(v, j, 0 if t is ps[0] else 1)
            norm.start(v)
            each_tile(v, "dve", 8, one)

        def act_back(act, src, name):
            for k in range(NT):
                load(act, xk[:, k], src[k])
            back_at[name] = aux_n[0]

        class Silu:

            def __init__(self, name, x, n, t):
                self.x, self.n, self.t = x, n, t
                self.sig, self.used = sem(f"{name}_sig"), sem(f"{name}_used")

            def act(self, act):
                for k in range(self.n):
                    if k >= 2:
                        act.wait_ge(self.used, k - 1)
                    act.activation(self.t[:, k % 2], self.x[:, k], ACT.Sigmoid).then_inc(self.sig, 1)

            def dve(self, v):
                for k in range(self.n):
                    v.wait_ge(self.sig, k + 1)
                    v.tensor_tensor(self.x[:, k], self.x[:, k], self.t[:, k % 2], ALU.mult).then_inc(self.used, 1)

        L6 = sb("L6", V, [P, 6, S])
        FZ = sb("FZ", V + 53, [P, 8, S])
        o_sq = sb("o_sq", V + 24, [P, 2, S])
        o_t = sb("o_t", V + 32, [P, 2, S])
        o_rs = sb("o_rs", V + 40, [P, S])
        o_rt = sb("o_rt", V + 44, [P, S])
        ones_q = sb("ones_q", V + 48, [P, P])
        ones_kv = sb("ones_kv", V + 48.5, [P, P])
        CQ_hi = sb("CQ_hi", 0, [P, 3, S], F32R)
        CQ_lo = sb("CQ_lo", 12, [P, 3, S], F32R)
        CK_hi = sb("CK_hi", 24, [P, 2, S], F32R)
        CK_lo = sb("CK_lo", 32, [P, 2, S], F32R)
        cos2 = sb("cos2", 40, [P, S])
        sin2 = sb("sin2", 44, [P, S])
        KR_hh = sb("KR_hh", 48, [P, S], F32R)
        KR_lo = sb("KR_lo", V + 37, [P, S], F32R)
        QR_hl = sb("QR_hl", 56, [P, S], F32R)
        QN_hi = sb("QN_hi", 52, [P, S], F32R)
        QN_lo = sb("QN_lo", V + 41, [P, S], F32R)
        KN_hi = sb("KN_hi", 60, [P, S], F32R)
        KN_lo = sb("KN_lo", V + 45, [P, S], F32R)
        rp_i = sb("rp_i", V + 24, [P, S], I32)
        rp_a = sb("rp_a", V + 28, [P, S])
        rp_k = sb("rp_k", V + 32, [P, S])
        rp_r = sb("rp_r", V + 36, [P, S])
        rot = sb("rot", V + 52, [P, P])
        VT = sb("VT", V, [P, S])
        VN = sb("VN", V + 4, [P, NT, P])
        mT3 = sb("mT3", V + 8, [P, 3, S])
        QR = mT3[:, 2]
        mPT = sb("mPT", V + 20, [P, 2, S])
        rt1 = sb("rt1", V + 28, [P, S])
        rt2 = sb("rt2", V + 32, [P, S])
        mst = sb("mst", V + 36, [P, 3, 8])

        silu_c = Silu("silu_c", ACC, 8, o_sq)
        norm_q = Norm("norm_q", L6, 3, ones_q, cols2[:, G_Q:G_Q + 3], hi=CQ_hi, lo=CQ_lo, sq=o_sq, t=o_t, rs=o_rs, rt=o_rt)
        norm_kv = Norm("norm_kv", L6[:, 3:5], 2, ones_kv, cols2[:, G_KV:G_KV + 2], hi=CK_hi, lo=CK_lo, sq=o_sq, t=o_t,
                       rs=o_rs, rt=o_rt)
        norm_op = Norm("norm_op", ACC, NT, ones_d, cols2[:, G_OPOST:G_OPOST + 8], into=ACC)
        chain_out = Chain(norm_op, None, out, "x2")
        rope = sem("rope")
        TWO_PI_1, TWO_PI_2 = 6.28125, 1014.0 / 2 ** 19
        TWO_PI_3 = 2 * np.pi - TWO_PI_1 - TWO_PI_2
        ROUND = 1.5 * 2 ** 23
        PI = 3.1415925

        def act_rope(act):
            load(act, rp_i[:], io["positions_2"].to_broadcast([P, S]))
            load(act, rot[:], io["consts"][CI["rot"]])
            act.wait_ge(aux, aux_n[0])
            act.drain().then_inc(rope, 1)
            for x, dst in enumerate((o_rs, o_rt)):
                act.wait_ge(rope, 2 * x + 2)
                act.activation(dst[:], rp_r[:], ACT.Sin).then_inc(rope, 1)

        def act_tables(act):
            act.activation(sin2[:], o_rs[:], ACT.Copy)
            act.activation(cos2[:], o_rt[:], ACT.Copy).then_inc(rope, 1)

        def dve_rope(v):
            v.wait_ge(rope, 1)
            link(v, "dve", v.tensor_copy(rp_k[:], rp_i[:]))
            link(v, "dve", v.tensor_scalar(rp_a[:], rp_k[:], cols2[:, G_INV:G_INV + 1], None, ALU.mult))
            for x in range(2):
                if x:
                    v.wait_ge(rope, 3)
                link(v, "dve", v.tensor_scalar(rp_k[:], rp_a[:], 1 / (2 * np.pi), 0.25 * x, ALU.mult, ALU.add))
                link(v, "dve", v.tensor_scalar(rp_k[:], rp_k[:], ROUND, None, ALU.add))
                link(v, "dve", v.tensor_scalar(rp_k[:], rp_k[:], ROUND, None, ALU.subtract))
                link(v, "dve", v.scalar_tensor_tensor(out=rp_r[:], in0=rp_k[:], scalar=-TWO_PI_1, in1=rp_a[:],
                                                      op0=ALU.mult, op1=ALU.add))
                for c in (TWO_PI_2, TWO_PI_3):
                    link(v, "dve", v.scalar_tensor_tensor(out=rp_r[:], in0=rp_k[:], scalar=-c, in1=rp_r[:],
                                                          op0=ALU.mult, op1=ALU.add))
                if x:
                    link(v, "dve", v.tensor_scalar(rp_r[:], rp_r[:], np.pi / 2, None, ALU.add))
                v.tensor_scalar(rp_r[:], rp_r[:], PI, -PI, ALU.min, ALU.max).then_inc(rope, 1)

        def dve_key(v):
            v.wait_ge(rope, 7)
            v.wait_ge(norm_kv.lo_done, norm_kv.at["lo_done"] + 2)
            r = slice(0, ROPE)
            v.tensor_tensor(rp_a[r], L6[r, 5], cos2[r], ALU.mult)
            link(v, "dve", v.tensor_tensor(rp_k[r], ps[3][r], sin2[r], ALU.mult))
            link(v, "dve", v.tensor_tensor(rp_a[r], rp_a[r], rp_k[r], ALU.add))
            v.tensor_copy(KR_hh[ROPE:P], rp_a[r])
            link(v, "dve", v.tensor_copy(KR_hh[r], rp_a[r]))
            v.tensor_tensor(KR_lo[r], rp_a[r], KR_hh[r].bitcast(F32), ALU.subtract)

        def pe_rope(pe):
            for h in range(2):
                mm = pe.matmul(ps[3][0:ROPE, h * HALF:(h + 1) * HALF], rot[0:ROPE, 0:ROPE],
                               L6[0:ROPE, 5, h * HALF:(h + 1) * HALF], start=True, stop=True)
            pe.wait_ge(rope, 6)
            mm = pe.transpose(ps[1][:, 0:P], rot[:], ident[:])
            mm.then_inc(rope, 1)

        def unitsM(dst):
            return [dict(scale=192.0 ** -0.5, first=True, last=True, start=True, stop=True, L=S, rel=None,
                         qk=[(q[:, it * P:(it + 1) * P], k) for q, k in (
                             (QN_hi, KN_hi), (QN_hi, KN_lo), (QN_lo, KN_hi),
                             (QR_hl, KR_hh), (QR_hl[0:ROPE], KR_lo[0:ROPE]))],
                         v=[VN[:, t] for t in range(NT)], it=it,
                         o=lambda g: ps[3][:, g % 2 * HALF:g % 2 * HALF + P]) for it in range(NT)]

        mla_head = [None]

        def mla_fin(v, g, u):
            z = ACC[:, mla_head[0], u["it"] * P:(u["it"] + 1) * P]
            return v.tensor_tensor(z, ps[3][:, g % 2 * HALF:g % 2 * HALF + P], z, ALU.mult)

        softM = Soft("mla", unitsM(None), mT3, mPT, mst, mla_fin)
        m_pre, m_vn, m_qr, m_rot, m_rope, m_qh = (
            sem(x) for x in ("m_pre", "m_vn", "m_qr", "m_rot", "m_rope", "m_qh"))

        def pe_mla(pe):
            n0, g0 = CHUNK0["mla"], tiles["pe"]
            with pe.Fori(0, H_C) as i:
                for o, (ch, b0, kt, hi, lo) in enumerate(((0, 0, 3, CQ_hi, CQ_lo), (0, 3, 3, CQ_hi, CQ_lo),
                                                          (0, 6, 2, CK_hi, CK_lo), (1, 0, 2, CK_hi, CK_lo))):
                    s = (n0 + ch) % 2
                    if b0 == 0:
                        pe.wait_ge(w_split, 2 * i + (n0 + ch + 1))
                    pe.wait_ge(evac_act, 4 * i + (g0 + o + 1))
                    pe.wait_ge(evac_dve, 4 * i + (g0 + o + 1))
                    if o == 2:
                        for h in range(2):
                            mm = pe.matmul(ps[2][:, h * HALF:(h + 1) * HALF], rot[:],
                                           QR[:, h * HALF:(h + 1) * HALF], start=True, stop=True)
                        mm.then_inc(m_rot, 1)
                    for k in range(kt):
                        b = (b0 + k) * P
                        for h in range(2):
                            mm = mm3(pe, ps[(g0 + o) % 2][:, h * HALF:(h + 1) * HALF], w_hi[s][:, b:b + P],
                                     w_lo[s][:, b:b + P], hi[:, k, h * HALF:(h + 1) * HALF],
                                     lo[:, k, h * HALF:(h + 1) * HALF], k == 0, k == kt - 1,
                                     opens=b0 == 0 and k == 0 and h == 0)
                    mm.then_inc(out_ready, 1)
                pe.wait_ge(evac_act, 4 * i + (g0 + 6))
                pe.wait_ge(evac_dve, 4 * i + (g0 + 6))
                for t in range(NT):
                    mm = pe.transpose(ps[3][:, t * P:(t + 1) * P], VT[:, t * P:(t + 1) * P], ident[:])
                mm.then_inc(m_pre, 1)
                pe.wait_ge(m_vn, i + 1)
                pe.wait_ge(m_qr, i + 1)
                softM.pe(pe, 8 * i, 8 * i)
                pe.wait_ge(softM.o_out, 8 * i + 8)
            tiles["pe"] += 4 * H_C

        def act_mla(act):
            g0 = tiles["act"]
            r = slice(0, ROPE)
            with act.Fori(0, H_C) as i:
                for o, (dst, w) in enumerate(((QR, HALF), (QN_hi, S), (KN_hi, S), (VT, HALF))):
                    if o == 3:
                        act.wait_ge(m_rope, i + 1)
                        act.activation(QR_hl[r], rt1[r], ACT.Copy).then_inc(m_qh, 1)
                    act.wait_ge(out_ready, 4 * i + (g0 + o + 1))
                    act.activation(dst[:, 0:w], ps[(g0 + o) % 2][:, 0:w], ACT.Copy).then_inc(evac_act, 1)
                act.wait_ge(m_pre, i + 1)
                act.activation(VN[:], ps[3][:].rearrange("p (t c) -> p t c", c=P), ACT.Copy).then_inc(m_vn, 1)
                softM.act(act, 8 * i)
            tiles["act"] += 4 * H_C

        def dve_mla(v):
            g0 = tiles["dve"]
            c = own["dve"]
            r = slice(0, ROPE)

            def half(i, o, dst):
                v.wait_ge(out_ready, 4 * i + (g0 + o + 1))
                v.tensor_copy(dst[:, HALF:S], ps[(g0 + o) % 2][:, HALF:S]).then_inc(evac_dve, 1)

            def low(i, o, hi, lo):
                v.wait_ge(evac_act, 4 * i + (g0 + o + 3))
                v.tensor_tensor(lo[:], ps[(g0 + o) % 2][:], hi[:].bitcast(F32), ALU.subtract).then_inc(evac_dve, 1)
            with v.Fori(0, H_C) as i:
                c.enter(i, 17)
                mla_head[0] = i
                half(i, 0, QR)
                low(i, 1, QN_hi, QN_lo)
                v.wait_ge(m_rot, i + 1)
                v.tensor_tensor(rt1[r], QR[r], cos2[r], ALU.mult)
                link(v, "dve", v.tensor_tensor(rt2[r], ps[2][r], sin2[r], ALU.mult))
                v.tensor_tensor(rt1[r], rt1[r], rt2[r], ALU.add).then_inc(m_rope, 1)
                low(i, 2, KN_hi, KN_lo)
                v.wait_ge(m_qh, i + 1)
                v.tensor_tensor(QR_hl[ROPE:P], rt1[r], QR_hl[r].bitcast(F32), ALU.subtract).then_inc(m_qr, 1)
                half(i, 3, VT)
                softM.dve(v, 8 * i, 8 * i)
            c.leave(H_C)
            tiles["dve"] += 4 * H_C

        split_c = Split("split_c", ACC, NT, Z_hi, Z_lo)

        silu_d = Silu("silu_d", FZ[:, 4:8], 4, o_sq)
        UV_hi = sb("UV_hi", 0, [P, 16, HALF], F32R)
        UV_lo = sb("UV_lo", 32, [P, 16, HALF], F32R)
        dft_c = sb("dft_c", V + 48.5, [P, 2 * P])
        FT = sb("FT", V, [P, 4, S])
        FU = sb("FU", V + 20, [P, HALF])
        FB = sb("FB", V + 16, [P, 2, HALF])
        FT_hi = sb("FT_hi", V + 16, [P, 4, S], F32R)
        FT_lo = sb("FT_lo", V + 32, [P, 4, S], F32R)
        YD_hi = sb("YD_hi", 0, [P, 4, S], F32R)
        YD_lo = sb("YD_lo", 16, [P, 4, S], F32R)
        fu, fu_hi, fu_lo, ft, ft_hi, ft_lo = (sem(x) for x in ("fu", "fu_hi", "fu_lo", "ft", "ft_hi", "ft_lo"))

        def pe_fft1(pe):
            for t in range(NT):
                if t >= 2:
                    pe.wait_ge(fu_lo, t - 1)
                for g in range(4):
                    mm = pe.matmul(ps[t % 2][:, g * 256:(g + 1) * 256], FZ[:, g, t * P:(t + 1) * P], dft_c[:],
                                   start=True, stop=True)
                mm.then_inc(fu, 1)

        def act_fft1(act):
            for t in range(NT):
                act.wait_ge(fu, t + 1)
                act.activation(uv(UV_hi, t), ps[t % 2][:].rearrange("p (g x c) -> p x g c", g=4, x=2),
                               ACT.Copy).then_inc(fu_hi, 1)

        def uv(x, t):
            return x[:].rearrange("p (x t) (g c) -> p t x g c", x=2, g=4)[:, t]

        def dve_fft1(v):
            for t in range(NT):
                v.wait_ge(fu_hi, t + 1)
                src = ps[t % 2][:].rearrange("p (g x c) -> p x g c", g=4, x=2)
                v.tensor_tensor(uv(UV_lo, t), src, uv(UV_hi, t).bitcast(F32), ALU.subtract).then_inc(fu_lo, 1)

        def pe_dft(pe):
            n0 = CHUNK0["dft"]
            for k in range(NT):
                s = (n0 + k) % 2
                pe.wait_ge(w_split, n0 + k + 1)
                for g in range(4):
                    c = slice(g * P, (g + 1) * P)
                    for x in range(2):
                        cols_x = slice(x * HALF, (x + 1) * HALF)
                        mm = mm3(pe, ps[g][:, cols_x], UV_hi[:, x * NT + k, c], UV_lo[:, x * NT + k, c],
                                 w_hi[s][:, cols_x], w_lo[s][:, cols_x], k == 0, k == NT - 1,
                                 opens=g == 0 and x == 0)
                    if k == NT - 1:
                        mm.then_inc(ft, 1)
            pe.wait_ge(ft_lo, 1)
            for g in range(4):
                mm = pe.matmul(ps[0][:, g:g + 1], FU[:, g * P:(g + 1) * P], cols2[:, G_ALT:G_ALT + 1],
                               start=True, stop=True)
            mm.then_inc(ft, 1)

        def dve_dft(v):
            link(v, "dve", v.tensor_tensor(FU[:], UV_hi[:, 0].bitcast(F32), UV_lo[:, 0].bitcast(F32), ALU.add))
            for k in range(1, NT):
                for uvx in (UV_hi, UV_lo):
                    link(v, "dve", v.tensor_tensor(FU[:], FU[:], uvx[:, k].bitcast(F32), ALU.add))
            for g in range(4):
                v.wait_ge(ft, g + 1)
                link(v, "dve", v.tensor_copy(FB[:, g % 2], ps[g][:, HALF:S]))
                v.tensor_tensor(FT[:, g, 0:HALF], ps[g][:, 0:HALF], FB[:, g % 2], ALU.add)
                v.tensor_tensor(FT[:, g, S - 1:HALF:-1], ps[g][:, 1:HALF], FB[:, g % 2, 1:HALF],
                                ALU.subtract).then_inc(ft_lo, 1)
            v.wait_ge(ft, 5)
            v.tensor_copy(FT[:, :, HALF], ps[0][:, 0:4]).then_inc(ft_lo, 1)
            for g in range(4):
                v.wait_ge(ft_hi, g + 1)
                v.tensor_tensor(FT_lo[:, g], FT[:, g], FT_hi[:, g].bitcast(F32), ALU.subtract)

        def act_dft(act):
            act.wait_ge(ft_lo, 5)
            for g in range(4):
                act.activation(FT_hi[:, g], FT[:, g], ACT.Copy).then_inc(ft_hi, 1)

        def dve_fd(v):
            def one(j, t):
                v.tensor_tensor(FZ[:, 4 + j], FZ[:, 4 + j], t[:], ALU.mult).then_inc(evac_dve, 1)
            each_tile(v, "dve", 4, one)

        split_d = Split("split_d", FZ[:, 4:8], 4, YD_hi, YD_lo)


        @block.tensor
        def _(pe):
            pe.sem_inc(slot_free, 1)
            norm1.pe(pe)
            pe_mod(pe)
            for b in "ABCD":
                pe_gemm(pe, "proj" + b, PROJ[b], 8, H_hi, H_lo, after=norm1 if b == "A" else None)
                end_phase(pe, "pe")
                if b == "A":
                    pe_prepA(pe)
                    end_phase(pe, "pe")
                    softA.pe(pe)
                elif b == "B":
                    pe_prepB(pe)
                    end_phase(pe, "pe")
                    softB.pe(pe)
                elif b == "C":
                    pe_prep_v(pe, prepC)
                    end_phase(pe, "pe")
                    pe_stick(pe)
                else:
                    pe_prep_v(pe, prepD)
                    end_phase(pe, "pe")
                    pe_ret(pe)
                end_phase(pe, "pe")
                pe_gemm(pe, "br" + b, 2, 2, Ya_hi, Ya_lo, after=ysplit[b])
                end_phase(pe, "pe")
                pe_gemm(pe, "merge" + b, 8, 8, H_hi, H_lo)
                end_phase(pe, "pe")
            pe_gemm(pe, "out1", 8, 8, Y_hi, Y_lo, after=merged)
            chain_e.pe(pe)
            pe_gemm(pe, "gates", 1, 8, H_hi, H_lo, after=norm_e)
            end_phase(pe, "pe")
            pe_gates(pe)
            end_phase(pe, "pe")
            for l in lstm:
                l.pe_w(pe)
                pe_gemm(pe, CHUNK0[f"lstm{l.h}"], 4, 8, H_hi, H_lo)
                end_phase(pe, "pe")
                l.pe(pe)
                l.pe_f(pe)
                end_phase(pe, "pe")
            pe_gemm(pe, "out_b", 8, 8, Y_hi, Y_lo, after=split_b)
            end_phase(pe, "pe")
            pe_conv(pe)
            pe_gemm(pe, "out_a", 8, 8, Z_hi, Z_lo, after=split_a)
            chain_o.pe(pe)
            pe_gemm(pe, "zc", 8, 8, H_hi, H_lo, after=norm_o)
            end_phase(pe, "pe")
            pe_gemm(pe, "lat", 6, 8, H_hi, H_lo)
            end_phase(pe, "pe")
            pe_gemm(pe, "fin", 8, 8, H_hi, H_lo)
            end_phase(pe, "pe")
            pe_rope(pe)
            norm_q.pe(pe)
            norm_kv.pe(pe)
            pe.wait_ge(norm_kv.lo_done, norm_kv.at["lo_done"] + 2)
            pe_mla(pe)
            end_phase(pe, "pe")
            pe_gemm(pe, "out_c", 8, 8, Z_hi, Z_lo, after=split_c)
            end_phase(pe, "pe")
            pe_fft1(pe)
            end_phase(pe, "pe")
            pe_dft(pe)
            end_phase(pe, "pe")
            pe_gemm(pe, "fd", 2, 4, FT_hi, FT_lo)
            end_phase(pe, "pe")
            pe_gemm(pe, "out_d", 4, 4, YD_hi, YD_lo, after=split_d)
            chain_out.pe(pe)

        @block.scalar
        def _(act):
            act.sem_inc(evac_act, 2)
            act_mod(act)
            norm1.act(act)
            for b, loads in (("A", act_loadA), ("B", act_loadB), ("C", act_loadC), ("D", act_loadD)):
                loads(act)
                copy_half(act, "act", PROJ[b], proj)
                end_phase(act, "act")
                if b == "A":
                    act_prepA(act)
                    end_phase(act, "act")
                    softA.act(act)
                elif b == "B":
                    act_prepB(act)
                    end_phase(act, "act")
                    softB.act(act)
                elif b == "C":
                    act_prepC(act)
                    end_phase(act, "act")
                    act_stick(act)
                else:
                    act_prepD(act)
                    end_phase(act, "act")
                    act_ret(act)
                end_phase(act, "act")
                ysplit[b].act(act)
                copy_half(act, "act", 8, R)
                end_phase(act, "act")
                act_merge(act)
                end_phase(act, "act")
            merged.act(act)
            act_out1(act)
            chain_e.act(act)
            act_load_gates(act)
            copy_half(act, "act", 1, gT2)
            end_phase(act, "act")
            act_gates(act)
            end_phase(act, "act")
            for l in lstm:
                l.act_w(act)
                copy_half(act, "act", 4, QKV)
                end_phase(act, "act")
                l.act(act)
                l.act_f(act)
                end_phase(act, "act")
            split_b.act(act)
            load(act, conv_w[:], io["conv_w"])
            load(act, ones_c[:], io["consts"][CI["ones_c"]])
            copy_half(act, "act", 8, ACC)
            act.wait_ge(aux, aux_n[0])
            end_phase(act, "act")
            act_conv(act)
            act.wait_ge(split_a.lo_done, split_a.at["lo_done"] + NT)
            act_back(act, keep1, "x1")
            act_squares(act, norm_ep)
            chain_o.act(act)
            act.wait_ge(kept, kept_n[0])
            copy_half(act, "act", 8, ACC)
            end_phase(act, "act")
            silu_c.act(act)
            copy_half(act, "act", 6, L6)
            end_phase(act, "act")
            act_rope(act)
            load(act, ones_q[:], io["consts"][CI["ones_q"]])
            load(act, ones_kv[:], io["consts"][CI["ones_kv"]])
            copy_half(act, "act", 8, FZ)
            act.wait_ge(aux, aux_n[0])
            end_phase(act, "act")
            act_tables(act)
            norm_q.act(act)
            norm_kv.act(act)
            act_mla(act)
            end_phase(act, "act")
            split_c.act(act)
            load(act, dft_c[:], io["dft_c"])
            copy_half(act, "act", 8, ACC)
            act.wait_ge(aux, aux_n[0])
            end_phase(act, "act")
            act_fft1(act)
            silu_d.act(act)
            end_phase(act, "act")
            act_dft(act)
            end_phase(act, "act")
            act_gemm_none(act, 4)
            end_phase(act, "act")
            split_d.act(act)
            act.wait_ge(split_d.lo_done, split_d.at["lo_done"] + 4)
            act_back(act, keep2, "x2")
            act_squares(act, norm_op)
            chain_out.act(act)
            act.wait_ge(kept, kept_n[0])

        @block.vector
        def _(v):
            v.sem_inc(evac_dve, 2)
            dve_mod(v)
            norm1.invert(v)
            norm1.split_dve(v)
            for b in "ABCD":
                copy_half(v, "dve", PROJ[b], proj)
                end_phase(v, "dve")
                if b == "A":
                    dve_prepA(v)
                    end_phase(v, "dve")
                    dve_silu(v, 5)
                    v.drain()
                    softA.dve(v)
                elif b == "B":
                    end_phase(v, "dve")
                    dve_silu(v, 4)
                    v.drain()
                    softB.dve(v)
                elif b == "C":
                    end_phase(v, "dve")
                    dve_silu_cd(v, PT2)
                    v.drain()
                    dve_stick(v)
                else:
                    end_phase(v, "dve")
                    dve_silu_cd(v, zsig)
                    v.drain()
                    dve_ret(v)
                end_phase(v, "dve")
                ysplit[b].dve(v)
                copy_half(v, "dve", 8, R)
                end_phase(v, "dve")
                dve_merge(v, b == "A")
                end_phase(v, "dve")
            merged.dve(v)
            dve_out1(v)
            chain_e.dve(v)
            copy_half(v, "dve", 1, gT2)
            end_phase(v, "dve")
            dve_gates(v)
            end_phase(v, "dve")
            for l in lstm:
                l.dve_w(v)
                copy_half(v, "dve", 4, QKV)
                end_phase(v, "dve")
                l.dve(v)
                l.dve_f(v)
                end_phase(v, "dve")
            split_b.dve(v)
            copy_half(v, "dve", 8, ACC)
            end_phase(v, "dve")
            dve_conv(v)
            dve_add(v, norm_ep)
            chain_o.dve(v)
            v.wait_ge(kept, 16 * 2 * NT)
            copy_half(v, "dve", 8, ACC)
            end_phase(v, "dve")
            silu_c.dve(v)
            copy_half(v, "dve", 6, L6)
            end_phase(v, "dve")
            dve_rope(v)
            copy_half(v, "dve", 8, FZ)
            end_phase(v, "dve")
            v.wait_ge(rope, 6)
            norm_q.dve(v)
            norm_kv.dve(v)
            dve_key(v)
            dve_mla(v)
            end_phase(v, "dve")
            split_c.dve(v)
            copy_half(v, "dve", 8, ACC)
            end_phase(v, "dve")
            dve_fft1(v)
            silu_d.dve(v)
            end_phase(v, "dve")
            dve_dft(v)
            end_phase(v, "dve")
            dve_fd(v)
            end_phase(v, "dve")
            split_d.dve(v)
            v.wait_ge(split_d.lo_done, split_d.at["lo_done"] + 4)
            dve_add(v, norm_op)
            chain_out.dve(v)


def _blocks(w):
    k, n = w.shape
    return w.reshape(k // P, P, n // P, P).transpose(2, 0, 1, 3).reshape(-1, P, P)


def _pad_cols(w, n):
    return np.concatenate([w, np.zeros((w.shape[0], n - w.shape[1]), w.dtype)], axis=1)


def _chunks(blocks):
    b = np.concatenate(blocks, axis=0)
    assert b.shape[0] % BLK == 0
    return b.reshape(-1, BLK, P, P).transpose(0, 2, 1, 3).reshape(-1, P, BLK * P)


def _dft():
    n = np.arange(S)
    a = 2 * np.pi * (np.outer(n, n) % S) / S
    m = np.arange(P)
    b = 2 * np.pi * (np.outer(m, m) % P) / P
    scale = 1.0 / np.sqrt(float(S * P))
    return (np.cos(a).astype(np.float32), np.sin(a).astype(np.float32),
            (np.cos(b) * scale).astype(np.float32), (-np.sin(b) * scale).astype(np.float32))


def _stream(i, dft_cos, dft_sin):
    w_in = i["w_in"][0]
    out = {}
    z = lambda a, b: w_in[:, a:b]
    a_kv = 256
    order = {
        "A": [z(0, 256), z(a_kv, a_kv + 128), z(a_kv + 128, a_kv + 256), z(a_kv + 256, a_kv + 384), z(652, 908),
              _pad_cols(z(640, 652), P)],
        "B": [z(908, 1676)], "C": [z(1676, 2700)], "D": [z(2700, 3724)],
    }
    for n, b in enumerate("ABCD"):
        out["proj" + b] = _blocks(np.concatenate(order[b], axis=1))
        out["br" + b] = _blocks(i["w_br"][0, n])
        out["merge" + b] = _blocks(i["w_merge"][0, n])
    out["out1"] = _blocks(i["w_out"][0])
    we = i["even_w_in_2"][0]
    out["gates"] = _blocks(_pad_cols(we[:, 7168:7184], P))
    for h in range(H_B):
        out[f"lstm{h}"] = _blocks(np.concatenate(
            [we[:, 3072 + 128 * h:3200 + 128 * h], we[:, 3584 + 128 * h:3712 + 128 * h],
             we[:, 4096 + 256 * h:4352 + 256 * h], we[:, 5120 + 256 * h:5376 + 256 * h],
             we[:, 6144 + 256 * h:6400 + 256 * h]], axis=1))
    wo = i["even_w_out_2"][0]
    out["out_b"] = _blocks(wo[1024:])
    out["conv"] = _blocks(np.concatenate(
        [we[:, g + 128 * c:g + 128 * c + 128] for c in range(8) for g in (1024, 0, 2048)], axis=1))
    out["out_a"] = _blocks(wo[:1024])
    wd = i["odd_w_in_2"][0]
    out["zc"] = _blocks(wd[:, 1216:2240])
    out["lat"] = _blocks(np.concatenate([wd[:, 0:640], _pad_cols(wd[:, 640:704], P)], axis=1))
    out["fin"] = _blocks(np.concatenate([wd[:, 704:1216], wd[:, 2240:2752]], axis=1))
    uq, ukv = i["odd_w_uq_2"][0], i["odd_w_ukv_2"][0]
    mla = []
    for h in range(H_C):
        q = uq[:, 192 * h:192 * h + 192]
        kv = ukv[:, 256 * h:256 * h + 256]
        mla += [_blocks(_pad_cols(q[:, 128:], P)), _blocks(q[:, :128]), _blocks(kv[:, :128]), _blocks(kv[:, 128:]),
                np.zeros((6, P, P), np.float32)]
    out["mla"] = np.concatenate(mla)
    wc = i["odd_w_out_2"][0]
    out["out_c"] = _blocks(wc[:1024])
    out["dft"] = np.concatenate([dft_cos[:, :HALF], dft_sin[:, :HALF]], axis=1).reshape(NT, P, BLK, P).transpose(
        0, 2, 1, 3).reshape(-1, P, P)
    out["fd"] = _blocks(i["odd_w_fd_2"][0])
    out["out_d"] = _blocks(wc[1024:])
    for name, n in STREAM:
        assert out[name].shape[0] == n * BLK, (name, out[name].shape, n)
    pad = [np.zeros((BLK * (N_CHUNKS_PADDED - N_CHUNKS), P, P), np.float32)]
    return _chunks([out[name] for name, _ in STREAM] + pad)


def _consts():
    r, c = np.arange(P)[:, None], np.arange(P)[None, :]
    z = np.zeros((P, P))
    rot = z.copy()
    for k in range(32):
        rot[k + 32, k] = -1
        rot[k, k + 32] = 1
    m = {
        "ident": np.eye(P), "ones_d": z + 1.0 / D, "ones_c": z + 1.0 / P, "ones_h": (r // HD == c // HD) / HD,
        "ones": z + 1, "sum_neg": -1.0 * (r >= c), "neg": z - 1, "mask_lt": r < c, "neg_ge": NEG * (r >= c),
        "cum_f": r <= c, "cum_b": r >= c, "neg_f": NEG * (r > c), "neg_b": NEG * (r < c), "rot": rot, "ones_q": z + 1.0 / 384, "ones_kv": z + 1.0 / 256,
    }
    return np.stack([m[n].astype(np.float32) for n in CONST])


def _rel(width, window):
    d = np.arange(P)[:, None] + (width - P) - np.arange(width)[None, :]
    return np.where((d >= 0) & (d < window), d, -NEG).astype(np.float32)


def layout(i):
    i = {k: np.asarray(v) for k, v in i.items()}
    col = lambda v, n: np.ascontiguousarray(v.reshape(n, P).T)
    dc, ds_, cc, cs = _dft()
    t = np.arange(S).reshape(NT, P).T[:, :, None]
    dist = t - (32 * np.arange(32) + 31)[None, None, :]
    log_g = np.log(1.0 - 2.0 ** (-5.0 - np.arange(4)))
    u = np.arange(S)[None, None, :] - np.arange(P)[:, None, None]
    decay = np.where(u >= 0, np.exp(log_g[None, :, None] * np.maximum(u, 0)), 0.0)
    bd = lambda w: np.block([[w[0], np.zeros_like(w[0])], [np.zeros_like(w[1]), w[1]]])
    w1 = i["cmp_w1"][0].reshape(2, 32, HD, HD)
    f = {
        "x": i["x"][0].T.reshape(NT, P, S),
        "wstream": _stream(i, dc, ds_),
        "w_ada": _chunks([_blocks(i["w_ada"][0])]),
        "consts": _consts(),
        "c": col(i["c"][0], 8), "b_ada": col(i["b_ada"][0], 24), "norm_g": col(i["norm_g"][0], 8),
        "final_g": col(i["final_g"], 8), "even_g_pre_2": col(i["even_g_pre_2"][0], 8),
        "rel_sel": _rel(S, S), "rel_win": _rel(640, 512), "rel_swa": _rel(256, 128),
        "rel_cmp": np.where(dist >= 0, dist, -NEG).astype(np.float32),
        "cmp_pos": i["cmp_pos"][0].transpose(0, 2, 1).reshape(P, 32),
        "cmp_w1": np.stack([bd(w1[:, l]) for l in range(32)], axis=1),
        "cmp_w2": bd(i["cmp_w2"][0]),
        "sink": i["sink"][0:1],
        "decay": decay.astype(np.float32),
    }
    f.update(layout2(i, cc, cs, col))
    return {k: np.ascontiguousarray(v) for k, v in f.items()}


def layout2(i, cc, cs, col):
    inv = np.float32(10000.0) ** (-np.arange(0, ROPE, 2, dtype=np.float32) / np.float32(ROPE))
    one = np.zeros((P, 1), np.float32)
    bg = one.copy()
    bg[:16, 0] = i["even_b_gate_2"][0]
    parts = [col(i["even_g_post_2"][0], 8), col(i["odd_g_pre_2"][0], 8), col(i["odd_g_post_2"][0], 8),
             col(i["even_gn_g_2"][0], 8), col(i["even_gn_b_2"][0], 8), col(i["even_conv_b_2"][0], 8),
             col(i["even_hn_g_2"][0], 8), col(i["odd_g_q_2"][0], 3), col(i["odd_g_kv_2"][0], 2), bg,
             np.tile(inv, 4)[:, None], 1 - 2 * (np.arange(P, dtype=np.float32) % 2)[:, None]]
    g = np.concatenate(parts, axis=1)
    sel4 = np.zeros((4, 4, P), np.float32)
    for h in range(4):
        sel4[h, h] = -1
    w = i["even_conv_w_2"][0].T.reshape(NT, P, CONV_K).transpose(1, 0, 2)
    return {"gains": np.concatenate([g, np.zeros((P, 96 - g.shape[1]), np.float32)], axis=1).astype(np.float32),
            "sel4": sel4, "dft_c": np.concatenate([cc, cs], axis=1), "positions_2": i["positions_2"],
            "conv_w": np.concatenate([w, np.zeros((P, NT, 1), w.dtype)], axis=2)}


def kernel(**inputs):
    import concourse.bacc as _bacc
    from concourse.bass_utils import run_bass_kernel_spmd as _run

    nc = _bacc.Bacc("TRN2", target_bir_lowering=False, num_devices=1)
    arrays = {f"in_{n}": a for n, a in layout(inputs).items()}
    io = {n[3:]: nc.dram_tensor(n, a.shape, mybir.dt.from_np(a.dtype), kind="ExternalInput").ap()
          for n, a in arrays.items()}
    out = nc.dram_tensor("out", (NT, P, S), F32, kind="ExternalOutput").ap()
    build(nc, io, out)
    r = _run(nc, [arrays], core_ids=[0])
    return r.results[0]["out"].reshape(D, S).T.reshape(1, S, D)
```
